# Optimizing a Trainium2 kernel written in Bass

```python
import math
import jax, jax.numpy as jnp
from jax import lax
import numpy as np

D_MODEL = 2048
BATCH = 1
SEQ = 256
DEPTH = 1

HEAD_DIM = 64
Q_BLOCK = 128
RMS_EPS = 1e-6
MASK_VALUE = -1e30
ALIBI_MAX_EXP = 8.0
FOX_HEADS = 7
NSA_HEADS = 8
NSA_KV_GROUPS = 2
NSA_CMP_LEN = 32
NSA_CMP_STRIDE = 16
NSA_SEL_BLOCK = 64
NSA_TOP_N = 16
NSA_WINDOW = 512
NSA_FORCE_SCORE = 1e4
DIL_CONFIGS = ((128, 1), (512, 4), (2048, 16))
DIL_HEADS_PER_GROUP = 3
DIL_HEADS = DIL_HEADS_PER_GROUP * len(DIL_CONFIGS)
DIFF_HEADS = 4
DIFF_QK_DIM = 64
DIFF_V_DIM = 2 * DIFF_QK_DIM
MIX_WIDTH = (FOX_HEADS + NSA_HEADS + DIL_HEADS) * HEAD_DIM + DIFF_HEADS * DIFF_V_DIM
D_FF = ((8 * D_MODEL + 3 * 256 - 1) // (3 * 256)) * 256
NSA_KV = NSA_KV_GROUPS * HEAD_DIM
IN_SPLITS = (
    ('fox_q', FOX_HEADS * HEAD_DIM), ('fox_k', FOX_HEADS * HEAD_DIM), ('fox_v', FOX_HEADS * HEAD_DIM), ('fox_f', FOX_HEADS),
    ('nsa_q', NSA_HEADS * HEAD_DIM),
    ('nsa_cmp_k', NSA_KV), ('nsa_cmp_v', NSA_KV), ('nsa_slc_k', NSA_KV), ('nsa_slc_v', NSA_KV), ('nsa_win_k', NSA_KV), ('nsa_win_v', NSA_KV),
    ('nsa_gate', NSA_HEADS * 3),
    ('dil_q', DIL_HEADS * HEAD_DIM), ('dil_k', DIL_HEADS * HEAD_DIM), ('dil_v', DIL_HEADS * HEAD_DIM),
    ('diff_q', DIFF_HEADS * 2 * DIFF_QK_DIM), ('diff_k', DIFF_HEADS * 2 * DIFF_QK_DIM), ('diff_v', DIFF_HEADS * DIFF_V_DIM),
)
N_IN = sum(w for _, w in IN_SPLITS)


def rms_norm(x, gain):
    xf = x.astype(jnp.float32)
    y = xf * lax.rsqrt(jnp.mean(xf * xf, axis=-1, keepdims=True) + RMS_EPS)
    return (y * gain.astype(jnp.float32)).astype(x.dtype)

def masked_softmax(s, mask):
    p = jax.nn.softmax(jnp.where(mask, s, MASK_VALUE), axis=-1)
    return jnp.where(mask, p, 0.0)

def alibi_slopes(n_heads):
    return jnp.asarray(2.0 ** (-ALIBI_MAX_EXP * np.arange(1, n_heads + 1) / n_heads), jnp.float32)

def blocks_to_seq(o):
    o = jnp.moveaxis(o, 0, 1)
    return o.reshape(o.shape[0], o.shape[1] * o.shape[2], *o.shape[3:])

def fox_attention(q, k, v, f_logit, f_bias):
    B, S, H, dh = q.shape
    scale = dh ** -0.5
    log_f = jax.nn.log_sigmoid(f_logit.astype(jnp.float32) + f_bias.astype(jnp.float32))
    cum = jnp.cumsum(log_f, axis=1).transpose(0, 2, 1)
    pos = jnp.arange(S)

    def block(i):
        qs = i * Q_BLOCK
        tq = qs + jnp.arange(Q_BLOCK)
        qb = lax.dynamic_slice_in_dim(q, qs, Q_BLOCK, 1)
        cq = lax.dynamic_slice_in_dim(cum, qs, Q_BLOCK, 2)
        s = jnp.einsum('bqhd,bkhd->bhqk', qb, k).astype(jnp.float32) * scale
        s = s + cq[..., None] - cum[:, :, None, :]
        p = jax.nn.softmax(jnp.where(pos[None, :] <= tq[:, None], s, MASK_VALUE), axis=-1)
        return jnp.einsum('bhqk,bkhd->bqhd', p.astype(v.dtype), v)

    o = blocks_to_seq(lax.map(block, jnp.arange(S // Q_BLOCK)))
    return o.reshape(B, S, H * dh)

def cmp_to_sel_matrix(n_cmp, n_sel):
    a = NSA_SEL_BLOCK // NSA_CMP_STRIDE
    b = NSA_CMP_LEN // NSA_CMP_STRIDE
    j = np.arange(n_sel)[:, None, None]
    idx = a * j + np.arange(a)[None, :, None] - np.arange(b)[None, None, :]
    jj = np.broadcast_to(j, idx.shape)
    ok = (idx >= 0) & (idx < n_cmp)
    m = np.zeros((n_cmp, n_sel), np.float32)
    np.add.at(m, (idx[ok], jj[ok]), 1.0)
    return m

def nsa_attention(q, k_cmp, v_cmp, k_slc, v_slc, k_win, v_win, gate_logit, cmp_w1, cmp_w2, cmp_pos):
    B, S, H, dh = q.shape
    G = k_cmp.shape[2]
    hpg = H // G
    scale = dh ** -0.5
    slopes = alibi_slopes(H).reshape(G, hpg)[None, :, :, None, None]
    ratio = NSA_CMP_LEN // NSA_CMP_STRIDE
    n_chunk = S // NSA_CMP_STRIDE
    n_cmp = n_chunk - ratio + 1
    n_sel = S // NSA_SEL_BLOCK
    n_top = min(NSA_TOP_N, n_sel)

    def compress(t, w1, w2, pos_emb):
        ch = t.reshape(B, n_chunk, NSA_CMP_STRIDE, G, dh)
        blk = jnp.concatenate([ch[:, r:r + n_cmp] for r in range(ratio)], axis=2)
        blk = (blk + pos_emb[:, None, :]).transpose(0, 1, 3, 2, 4).reshape(B, n_cmp, G, NSA_CMP_LEN * dh)
        return jax.nn.gelu(blk @ w1) @ w2

    kc = compress(k_cmp, cmp_w1[0], cmp_w2[0], cmp_pos[0])
    vc = compress(v_cmp, cmp_w1[1], cmp_w2[1], cmp_pos[1])
    cmp_end = jnp.arange(n_cmp) * NSA_CMP_STRIDE + (NSA_CMP_LEN - 1)
    cmp_to_sel = jnp.asarray(cmp_to_sel_matrix(n_cmp, n_sel), jnp.float32)
    k_blocks = k_slc.transpose(0, 2, 1, 3).reshape(B, G, n_sel, NSA_SEL_BLOCK, dh)
    v_blocks = v_slc.transpose(0, 2, 1, 3).reshape(B, G, n_sel, NSA_SEL_BLOCK, dh)
    pad = ((0, 0), (NSA_WINDOW, 0), (0, 0), (0, 0))
    k_win_p = jnp.pad(k_win, pad)
    v_win_p = jnp.pad(v_win, pad)
    gates = jax.nn.sigmoid(gate_logit).reshape(B, S, G, hpg, 3)
    sel_ids = jnp.arange(n_sel)
    win_offsets = jnp.arange(Q_BLOCK + NSA_WINDOW) - NSA_WINDOW
    sel_offsets = jnp.arange(NSA_SEL_BLOCK)

    def block(i):
        qs = i * Q_BLOCK
        tq = qs + jnp.arange(Q_BLOCK)
        qb = lax.dynamic_slice_in_dim(q, qs, Q_BLOCK, 1).reshape(B, Q_BLOCK, G, hpg, dh)
        dist_c = (tq[:, None] - cmp_end[None, :]).astype(jnp.float32)
        s_c = jnp.einsum('bqgjd,bcgd->bgjqc', qb, kc).astype(jnp.float32) * scale - slopes * dist_c
        p_c = masked_softmax(s_c, dist_c >= 0)
        o_c = jnp.einsum('bgjqc,bcgd->bqgjd', p_c.astype(vc.dtype), vc)
        imp = jnp.einsum('bgjqc,cn->bgqn', p_c, cmp_to_sel)
        cur = (tq // NSA_SEL_BLOCK)[:, None]
        forced = (sel_ids == 0) | (sel_ids == cur) | (sel_ids == cur - 1)
        causal = sel_ids * NSA_SEL_BLOCK <= tq[:, None]
        score = jnp.where(causal, jnp.where(forced, NSA_FORCE_SCORE, imp), MASK_VALUE)
        _, top_idx = lax.top_k(score, n_top)
        flat = top_idx.reshape(B, G, Q_BLOCK * n_top)[..., None, None]
        ks = jnp.take_along_axis(k_blocks, flat, axis=2).reshape(B, G, Q_BLOCK, n_top * NSA_SEL_BLOCK, dh)
        vs = jnp.take_along_axis(v_blocks, flat, axis=2).reshape(B, G, Q_BLOCK, n_top * NSA_SEL_BLOCK, dh)
        kpos = (top_idx[..., None] * NSA_SEL_BLOCK + sel_offsets).reshape(B, G, Q_BLOCK, n_top * NSA_SEL_BLOCK)
        dist_s = (tq[:, None] - kpos).astype(jnp.float32)[:, :, None]
        s_s = jnp.einsum('bqgjd,bgqkd->bgjqk', qb, ks).astype(jnp.float32) * scale - slopes * dist_s
        p_s = masked_softmax(s_s, dist_s >= 0)
        o_s = jnp.einsum('bgjqk,bgqkd->bqgjd', p_s.astype(vs.dtype), vs)
        kw = lax.dynamic_slice_in_dim(k_win_p, qs, Q_BLOCK + NSA_WINDOW, 1)
        vw = lax.dynamic_slice_in_dim(v_win_p, qs, Q_BLOCK + NSA_WINDOW, 1)
        kpos_w = qs + win_offsets
        dist_w = tq[:, None] - kpos_w[None, :]
        mask_w = (dist_w >= 0) & (dist_w < NSA_WINDOW) & (kpos_w[None, :] >= 0)
        s_w = jnp.einsum('bqgjd,bkgd->bgjqk', qb, kw).astype(jnp.float32) * scale - slopes * dist_w.astype(jnp.float32)
        p_w = masked_softmax(s_w, mask_w)
        o_w = jnp.einsum('bgjqk,bkgd->bqgjd', p_w.astype(vw.dtype), vw)
        g = lax.dynamic_slice_in_dim(gates, qs, Q_BLOCK, 1)
        return g[..., 0:1] * o_c + g[..., 1:2] * o_s + g[..., 2:3] * o_w

    o = blocks_to_seq(lax.map(block, jnp.arange(S // Q_BLOCK)))
    return o.reshape(B, S, H * dh)

def dilated_attention(q, k, v):
    B, S, H, dh = q.shape
    scale = dh ** -0.5
    slopes = alibi_slopes(H)
    hpg = DIL_HEADS_PER_GROUP
    k_groups = [k[:, :, g * hpg:(g + 1) * hpg] for g in range(len(DIL_CONFIGS))]
    v_groups = [v[:, :, g * hpg:(g + 1) * hpg] for g in range(len(DIL_CONFIGS))]

    def block(i):
        qs = i * Q_BLOCK
        tq = qs + jnp.arange(Q_BLOCK)
        qb = lax.dynamic_slice_in_dim(q, qs, Q_BLOCK, 1)
        outs, lses = [], []
        for g, (window, dilation) in enumerate(DIL_CONFIGS):
            steps = jnp.arange(window // dilation + 1) * dilation
            kidx = tq[:, None] - steps[None, :]
            valid = kidx >= 0
            kidx = jnp.maximum(kidx, 0)
            kg = k_groups[g][:, kidx]
            vg = v_groups[g][:, kidx]
            s = jnp.einsum('bqhd,bqkhd->bhqk', qb[:, :, g * hpg:(g + 1) * hpg], kg).astype(jnp.float32) * scale
            s = s - slopes[g * hpg:(g + 1) * hpg][:, None, None] * steps.astype(jnp.float32)
            s = jnp.where(valid, s, MASK_VALUE)
            lse = jax.nn.logsumexp(s, axis=-1)
            p = jnp.exp(s - lse[..., None])
            outs.append(jnp.einsum('bhqk,bqkhd->bqhd', p.astype(vg.dtype), vg))
            lses.append(lse)
        w = jax.nn.softmax(jnp.stack(lses, axis=0), axis=0).transpose(0, 1, 3, 2)[..., None]
        return jnp.concatenate([o * w[g].astype(o.dtype) for g, o in enumerate(outs)], axis=2)

    o = blocks_to_seq(lax.map(block, jnp.arange(S // Q_BLOCK)))
    return o.reshape(B, S, H * dh)

def diff_attention(q, k, v, lam_vecs, subln_g, lam_init):
    B, S, H, _, dq = q.shape
    dv = v.shape[-1]
    scale = dq ** -0.5
    lv = lam_vecs.astype(jnp.float32)
    lam = jnp.exp(jnp.sum(lv[0] * lv[1])) - jnp.exp(jnp.sum(lv[2] * lv[3])) + lam_init
    slopes = alibi_slopes(H)[None, :, None, None, None]
    pos = jnp.arange(S)

    def block(i):
        qs = i * Q_BLOCK
        tq = qs + jnp.arange(Q_BLOCK)
        qb = lax.dynamic_slice_in_dim(q, qs, Q_BLOCK, 1)
        dist = tq[:, None] - pos[None, :]
        s = jnp.einsum('bqhmd,bkhmd->bhmqk', qb, k).astype(jnp.float32) * scale - slopes * dist.astype(jnp.float32)
        p = jax.nn.softmax(jnp.where(dist >= 0, s, MASK_VALUE), axis=-1)
        a = p[:, :, 0] - lam * p[:, :, 1]
        return jnp.einsum('bhqk,bkhd->bqhd', a.astype(v.dtype), v)

    o = blocks_to_seq(lax.map(block, jnp.arange(S // Q_BLOCK)))
    o = rms_norm(o, subln_g) * (1.0 - lam_init)
    return o.reshape(B, S, H * dv)

def hybrid_mixer(u, w_in, fox_f_bias, cmp_w1, cmp_w2, cmp_pos, diff_lambda, diff_subln_g, diff_lam_init, w_out):
    B, S, _ = u.shape
    proj = u @ w_in
    offsets = [int(o) for o in np.cumsum([w for _, w in IN_SPLITS])[:-1]]
    p = dict(zip([n for n, _ in IN_SPLITS], jnp.split(proj, offsets, axis=-1)))

    def hd(name, *shape):
        return p[name].reshape(B, S, *shape)

    o_fox = fox_attention(hd('fox_q', FOX_HEADS, HEAD_DIM), hd('fox_k', FOX_HEADS, HEAD_DIM),
                          hd('fox_v', FOX_HEADS, HEAD_DIM), p['fox_f'], fox_f_bias)
    o_nsa = nsa_attention(hd('nsa_q', NSA_HEADS, HEAD_DIM),
                          hd('nsa_cmp_k', NSA_KV_GROUPS, HEAD_DIM), hd('nsa_cmp_v', NSA_KV_GROUPS, HEAD_DIM),
                          hd('nsa_slc_k', NSA_KV_GROUPS, HEAD_DIM), hd('nsa_slc_v', NSA_KV_GROUPS, HEAD_DIM),
                          hd('nsa_win_k', NSA_KV_GROUPS, HEAD_DIM), hd('nsa_win_v', NSA_KV_GROUPS, HEAD_DIM),
                          hd('nsa_gate', NSA_HEADS, 3), cmp_w1, cmp_w2, cmp_pos)
    o_dil = dilated_attention(hd('dil_q', DIL_HEADS, HEAD_DIM), hd('dil_k', DIL_HEADS, HEAD_DIM),
                              hd('dil_v', DIL_HEADS, HEAD_DIM))
    o_diff = diff_attention(hd('diff_q', DIFF_HEADS, 2, DIFF_QK_DIM), hd('diff_k', DIFF_HEADS, 2, DIFF_QK_DIM),
                            hd('diff_v', DIFF_HEADS, DIFF_V_DIM), diff_lambda, diff_subln_g, diff_lam_init)
    o = jnp.concatenate([o_fox, o_nsa, o_dil, o_diff], axis=-1)
    return o @ w_out

def swiglu(u, w_gate, w_up, w_down):
    return (jax.nn.silu(u @ w_gate) * (u @ w_up)) @ w_down

def first_inputs(seed: int = 0) -> dict:
    key = jax.random.key(seed)
    ks = jax.random.split(key, 18)
    D = D_MODEL

    def nrm(k, shape, scale):
        return jax.random.normal(k, shape, jnp.float32) * scale

    return {
        'x': nrm(ks[0], (BATCH, SEQ, D), 1.0),
        'c': nrm(ks[1], (BATCH, D), 1.0),
        'ada_w': nrm(ks[2], (DEPTH, D, 6 * D), 0.5 * D ** -0.5),
        'ada_b': nrm(ks[3], (DEPTH, 6 * D), 0.02),
        'norm_mix_g': 1.0 + nrm(ks[4], (DEPTH, D), 0.02),
        'norm_ffn_g': 1.0 + nrm(ks[5], (DEPTH, D), 0.02),
        'w_in': nrm(ks[6], (DEPTH, D, N_IN), D ** -0.5),
        'fox_f_bias': 3.0 + nrm(ks[7], (DEPTH, FOX_HEADS), 0.5),
        'nsa_cmp_w1': nrm(ks[8], (DEPTH, 2, NSA_CMP_LEN * HEAD_DIM, HEAD_DIM), (NSA_CMP_LEN * HEAD_DIM) ** -0.5),
        'nsa_cmp_w2': nrm(ks[9], (DEPTH, 2, HEAD_DIM, HEAD_DIM), 1.5 * HEAD_DIM ** -0.5),
        'nsa_cmp_pos': nrm(ks[10], (DEPTH, 2, NSA_CMP_LEN, HEAD_DIM), 0.1),
        'diff_lambda': nrm(ks[11], (DEPTH, 4, DIFF_QK_DIM), 0.1),
        'diff_subln_g': 1.0 + nrm(ks[12], (DEPTH, DIFF_V_DIM), 0.02),
        'w_out': nrm(ks[13], (DEPTH, MIX_WIDTH, D), MIX_WIDTH ** -0.5),
        'ffn_w_gate': nrm(ks[14], (DEPTH, D, D_FF), D ** -0.5),
        'ffn_w_up': nrm(ks[15], (DEPTH, D, D_FF), D ** -0.5),
        'ffn_w_down': nrm(ks[16], (DEPTH, D_FF, D), D_FF ** -0.5),
        'final_norm_g': 1.0 + nrm(ks[17], (D,), 0.02),
    }

def first_block(x, c, ada_w, ada_b, norm_mix_g, norm_ffn_g, w_in, fox_f_bias, nsa_cmp_w1, nsa_cmp_w2,
              nsa_cmp_pos, diff_lambda, diff_subln_g, w_out, ffn_w_gate, ffn_w_up, ffn_w_down, final_norm_g):
    c_act = jax.nn.silu(c)
    h = x
    for layer in range(DEPTH):
        mod = c_act @ ada_w[layer] + ada_b[layer]
        sh1, sc1, g1, sh2, sc2, g2 = [m[:, None, :] for m in jnp.split(mod, 6, axis=-1)]
        lam_init = 0.8 - 0.6 * math.exp(-0.3 * layer)
        u = rms_norm(h, norm_mix_g[layer]) * (1.0 + sc1) + sh1
        h = h + g1 * hybrid_mixer(u, w_in[layer], fox_f_bias[layer], nsa_cmp_w1[layer], nsa_cmp_w2[layer],
                                  nsa_cmp_pos[layer], diff_lambda[layer], diff_subln_g[layer], lam_init, w_out[layer])
        u = rms_norm(h, norm_ffn_g[layer]) * (1.0 + sc2) + sh2
        h = h + g2 * swiglu(u, ffn_w_gate[layer], ffn_w_up[layer], ffn_w_down[layer])
    return rms_norm(h, final_norm_g)


DEPTH_2 = 2

N_MEM = 256
N_A_LAYERS = DEPTH_2 // 2
N_B_LAYERS = DEPTH_2 - N_A_LAYERS
HEAD_DIM_2 = 128
MIX_WIDTH_2 = D_MODEL
MEM_HEADS = 4
MEM_WIDTH = MEM_HEADS * HEAD_DIM_2
BRANCH_WIDTH = MIX_WIDTH_2 - MEM_WIDTH
POOL_WINDOWS = (2, 4, 8, 16)
N_POOL_GROUPS = len(POOL_WINDOWS)
POOL_GROUP = BRANCH_WIDTH // N_POOL_GROUPS
MOBA_HEADS = BRANCH_WIDTH // HEAD_DIM_2
MOBA_BLOCK = 256
MOBA_TOPK = 3
Q_CHUNK = 64
IN_WIDTH = 2 * BRANCH_WIDTH + 2 * MEM_WIDTH
DEEPNORM_ALPHA = (2 * DEPTH_2) ** 0.25
DEEPNORM_BETA = (8 * DEPTH_2) ** -0.25
LN_EPS = 1e-5


def layer_norm(x, g, b):
    xf = x.astype(jnp.float32)
    mu = xf.mean(-1, keepdims=True)
    var = jnp.square(xf - mu).mean(-1, keepdims=True)
    return ((xf - mu) * lax.rsqrt(var + LN_EPS) * g + b).astype(x.dtype)

def multiscale_pool(u, pool_w, pool_scale):
    B, S, _ = u.shape
    uf = u.astype(jnp.float32)
    cs = jnp.concatenate([jnp.zeros((B, 1, BRANCH_WIDTH), jnp.float32),
                          jnp.cumsum(uf, axis=1)], axis=1)
    t = jnp.arange(S)
    outs = []
    for g, w in enumerate(POOL_WINDOWS):
        sl = slice(g * POOL_GROUP, (g + 1) * POOL_GROUP)
        csg = cs[:, :, sl]
        lo = jnp.maximum(t + 1 - w, 0)
        cnt = (t + 1 - lo).astype(jnp.float32)
        outs.append((csg[:, 1:] - csg[:, lo]) / cnt[None, :, None] - uf[:, :, sl])
    pooled = jnp.stack(outs, axis=2).astype(u.dtype)
    mixed = jnp.einsum('bsgc,gcd->bsgd', pooled, pool_w).reshape(B, S, BRANCH_WIDTH)
    return mixed * pool_scale

def memory_attention(mq, mem, w_mem_kv):
    B, S, _ = mq.shape
    M = mem.shape[1]
    mk, mv = jnp.split(mem @ w_mem_kv, 2, axis=-1)
    q = mq.reshape(B, S, MEM_HEADS, HEAD_DIM_2)
    k = mk.reshape(B, M, MEM_HEADS, HEAD_DIM_2)
    v = mv.reshape(B, M, MEM_HEADS, HEAD_DIM_2)
    s = jnp.einsum('bshd,bmhd->bhsm', q, k).astype(jnp.float32) * (HEAD_DIM_2 ** -0.5)
    p = jax.nn.softmax(s, axis=-1).astype(v.dtype)
    return jnp.einsum('bhsm,bmhd->bshd', p, v).reshape(B, S, MEM_WIDTH)

def moba_shared_kv(h, w_kv):
    B, S, _ = h.shape
    k, v = jnp.split(h @ w_kv, 2, axis=-1)
    nb = -(-S // MOBA_BLOCK)
    pad = nb * MOBA_BLOCK - S
    k = k.reshape(B, S, MOBA_HEADS, HEAD_DIM_2).transpose(0, 2, 1, 3)
    v = v.reshape(B, S, MOBA_HEADS, HEAD_DIM_2).transpose(0, 2, 1, 3)
    k = jnp.pad(k, ((0, 0), (0, 0), (0, pad), (0, 0)))
    v = jnp.pad(v, ((0, 0), (0, 0), (0, pad), (0, 0)))
    k_blocks = k.reshape(B, MOBA_HEADS, nb, MOBA_BLOCK, HEAD_DIM_2)
    v_blocks = v.reshape(B, MOBA_HEADS, nb, MOBA_BLOCK, HEAD_DIM_2)
    k_mean = k_blocks.astype(jnp.float32).mean(axis=3).astype(k.dtype)
    return k_blocks, v_blocks, k_mean

def moba_attention(q_in, k_blocks, v_blocks, k_mean):
    B, S, _ = q_in.shape
    H = MOBA_HEADS
    nb = k_blocks.shape[2]
    n_sel = min(MOBA_TOPK, nb)
    scale = HEAD_DIM_2 ** -0.5
    q = q_in.reshape(B, S, H, HEAD_DIM_2).transpose(0, 2, 1, 3)
    b_idx = jnp.arange(B)[:, None, None, None]
    h_idx = jnp.arange(H)[None, :, None, None]
    blk_ids = jnp.arange(nb)
    blk_offs = jnp.arange(MOBA_BLOCK)

    def chunk(c):
        start = c * Q_CHUNK
        qc = lax.dynamic_slice_in_dim(q, start, Q_CHUNK, axis=2)
        own = start // MOBA_BLOCK
        q_pos = start + jnp.arange(Q_CHUNK)
        gate = jnp.einsum('bhqd,bhnd->bhqn', qc, k_mean).astype(jnp.float32)
        gate = jnp.where(blk_ids < own, gate, -jnp.inf)
        _, sel = lax.top_k(gate, n_sel)
        valid = sel < own
        kg = k_blocks[b_idx, h_idx, sel]
        vg = v_blocks[b_idx, h_idx, sel]
        s_sel = jnp.einsum('bhqd,bhqjkd->bhqjk', qc, kg).astype(jnp.float32) * scale
        s_sel = jnp.where(valid[..., None], s_sel, -jnp.inf)
        s_sel = s_sel.reshape(B, H, Q_CHUNK, n_sel * MOBA_BLOCK)
        k_own = lax.dynamic_index_in_dim(k_blocks, own, axis=2, keepdims=False)
        v_own = lax.dynamic_index_in_dim(v_blocks, own, axis=2, keepdims=False)
        s_own = jnp.einsum('bhqd,bhkd->bhqk', qc, k_own).astype(jnp.float32) * scale
        k_pos = own * MOBA_BLOCK + blk_offs
        s_own = jnp.where(k_pos[None, :] <= q_pos[:, None], s_own, -jnp.inf)
        p = jax.nn.softmax(jnp.concatenate([s_sel, s_own], axis=-1), axis=-1).astype(v_blocks.dtype)
        p_sel = p[..., :n_sel * MOBA_BLOCK].reshape(B, H, Q_CHUNK, n_sel, MOBA_BLOCK)
        p_own = p[..., n_sel * MOBA_BLOCK:]
        return (jnp.einsum('bhqjk,bhqjkd->bhqd', p_sel, vg)
                + jnp.einsum('bhqk,bhkd->bhqd', p_own, v_own))

    out = lax.map(chunk, jnp.arange(S // Q_CHUNK))
    return out.transpose(1, 0, 3, 2, 4).reshape(B, S, H * HEAD_DIM_2)

def second_inputs(seed: int = 0) -> dict:
    key = jax.random.key(seed)
    ks = jax.random.split(key, 10)
    f32 = jnp.float32
    nrm = jax.random.normal
    x = nrm(ks[0], (BATCH, SEQ, D_MODEL), f32)
    mem = nrm(ks[1], (BATCH, N_MEM, D_MODEL), f32)
    w_in = nrm(ks[2], (DEPTH_2, D_MODEL, IN_WIDTH), f32) * D_MODEL ** -0.5
    w_out = nrm(ks[3], (DEPTH_2, MIX_WIDTH_2, D_MODEL), f32) * (MIX_WIDTH_2 ** -0.5 * DEEPNORM_BETA)
    w_mem_kv = nrm(ks[4], (DEPTH_2, D_MODEL, 2 * MEM_WIDTH), f32) * D_MODEL ** -0.5
    ln_g = 1.0 + 0.02 * nrm(ks[5], (DEPTH_2, D_MODEL), f32)
    ln_b = 0.02 * nrm(ks[6], (DEPTH_2, D_MODEL), f32)
    pool_w = nrm(ks[7], (N_A_LAYERS, N_POOL_GROUPS, POOL_GROUP, POOL_GROUP), f32) * POOL_GROUP ** -0.5
    pool_scale = 1.0 + 0.02 * nrm(ks[8], (N_A_LAYERS, BRANCH_WIDTH), f32)
    w_kv_shared = nrm(ks[9], (D_MODEL, 2 * BRANCH_WIDTH), f32) * D_MODEL ** -0.5
    return {"x": x, "mem": mem, "w_in": w_in, "w_out": w_out, "w_mem_kv": w_mem_kv,
            "ln_g": ln_g, "ln_b": ln_b, "pool_w": pool_w, "pool_scale": pool_scale,
            "w_kv_shared": w_kv_shared}

def second_block(x, mem, w_in, w_out, w_mem_kv, ln_g, ln_b, pool_w, pool_scale, w_kv_shared):
    h = x
    split_at = [BRANCH_WIDTH, 2 * BRANCH_WIDTH, 2 * BRANCH_WIDTH + MEM_WIDTH]
    for i in range(DEPTH_2):
        if i == N_A_LAYERS:
            k_blocks, v_blocks, k_mean = moba_shared_kv(h, w_kv_shared)
        u = h @ w_in[i]
        branch_in, gate_b, mem_q, gate_m = jnp.split(u, split_at, axis=-1)
        if i < N_A_LAYERS:
            branch = multiscale_pool(branch_in, pool_w[i], pool_scale[i])
        else:
            branch = moba_attention(branch_in, k_blocks, v_blocks, k_mean)
        mem_o = memory_attention(mem_q, mem, w_mem_kv[i])
        mixed = jnp.concatenate([branch * jax.nn.silu(gate_b), mem_o * jax.nn.silu(gate_m)], axis=-1)
        y = mixed @ w_out[i]
        h = layer_norm(DEEPNORM_ALPHA * h + y, ln_g[i], ln_b[i])
    return h


def setup_inputs(seed=0):
    out = dict(first_inputs(seed))
    for name, value in second_inputs(seed + 1).items():
        if name != "x":
            out[name + "_2"] = value
    return out


def reference(
    x, c, ada_w, ada_b, norm_mix_g, norm_ffn_g, w_in, fox_f_bias, nsa_cmp_w1, nsa_cmp_w2,
    nsa_cmp_pos, diff_lambda, diff_subln_g, w_out, ffn_w_gate, ffn_w_up, ffn_w_down,
    final_norm_g, mem_2, w_in_2, w_out_2, w_mem_kv_2, ln_g_2, ln_b_2, pool_w_2, pool_scale_2,
    w_kv_shared_2,
):
    x = first_block(
        x, c, ada_w, ada_b, norm_mix_g, norm_ffn_g, w_in, fox_f_bias, nsa_cmp_w1, nsa_cmp_w2,
        nsa_cmp_pos, diff_lambda, diff_subln_g, w_out, ffn_w_gate, ffn_w_up, ffn_w_down,
        final_norm_g,
    )
    return second_block(
        x, mem_2, w_in_2, w_out_2, w_mem_kv_2, ln_g_2, ln_b_2, pool_w_2, pool_scale_2,
        w_kv_shared_2,
    )


_drawn_inputs = setup_inputs


def setup_inputs(seed=0):
    import zlib

    import numpy as np

    out = dict(_drawn_inputs(seed))
    spreads = {}
    factors = {'norm_mix_g': 8.0,
     'norm_ffn_g': 8.0,
     'fox_f_bias': 3.738,
     'nsa_cmp_pos': 8.0,
     'diff_lambda': 4.59,
     'diff_subln_g': 8.0,
     'final_norm_g': 2.793,
     'mem_2': 3.763,
     'w_mem_kv_2': 3.594,
     'pool_scale_2': 8.0}
    for name, (base, spread) in spreads.items():
        noise = np.random.default_rng([zlib.crc32(name.encode()), seed]).standard_normal(out[name].shape)
        drawn = base * np.exp(spread * noise) if base else spread * noise
        out[name] = __import__('jax').numpy.asarray(drawn.astype(out[name].dtype))
    for name, factor in factors.items():
        out[name] = (out[name] * factor).astype(out[name].dtype)
    return out
```

```python
import numpy as np
import concourse.bass as bass
from concourse import mybir
from contextlib import ExitStack

P = 128
T = 2
SEQ = P * T
D = 2048
KD = D // P
NC = 512
HD = 64
FF = 5632
FOX, NSA, GROUPS, DIL, DIFF = 7, 8, 2, 9, 4
SPLITS = [("fox_q", FOX * HD), ("fox_k", FOX * HD), ("fox_v", FOX * HD), ("fox_f", FOX), ("nsa_q", NSA * HD),
          ("cmp_k", 128), ("cmp_v", 128), ("slc_k", 128), ("slc_v", 128), ("win_k", 128), ("win_v", 128),
          ("gate", NSA * 3), ("dil_q", DIL * HD), ("dil_k", DIL * HD), ("dil_v", DIL * HD),
          ("diff_q", 512), ("diff_k", 512), ("diff_v", 512)]
COL, _at = {}, 0
for _n, _w in SPLITS:
    COL[_n] = _at
    _at += _w
N_IN = _at
LAST_W = 288
MASKED = 1.0e30
CMP_LEN, CMP_STRIDE = 32, 16
N_CMP = SEQ // CMP_STRIDE - CMP_LEN // CMP_STRIDE + 1
LAM_INIT = 0.2
RMS_EPS, LN_EPS = 1e-6, 1e-5
ALPHA = 4 ** 0.25
BR, MEMW, HD2 = 1536, 512, 128
POOL_WINDOWS = (2, 4, 8, 16)
RING, HILO = 8, 4


def slope(h, n):
    return float(np.float32(2.0 ** (-8.0 * (h + 1) / n)))


class Stage:

    def __init__(self, name, bodies, panels):
        self.name, self.bodies, self.panels = name, bodies, panels


STAGES = [
    Stage("memkv", 2, [("w", 16)] * 2), Stage("ada1", 4, [("a", 16)] * 2),
    Stage("win", 4, [("wa", 16)] * 2), Stage("win_end", 1, [("w", 16)] * 4),
    Stage("wout", 2, [("wa", 16)] * 2),
    Stage("gu0", 4, [("w", 16), ("wa", 16)]), Stage("down0", 2, [("w", 16)] * 2),
    Stage("gu1", 4, [("w", 16)] * 2), Stage("down1", 2, [("w", 16)] * 2),
    Stage("gu2", 3, [("w", 16)] * 2), Stage("down2", 1, [("w", 12)] * 4),
    Stage("in0", 4, [("w", 16)] * 2), Stage("out0", 2, [("w", 16)] * 2),
    Stage("kv", 3, [("w", 16)] * 2), Stage("in1", 4, [("w", 16)] * 2), Stage("out1", 2, [("w", 16)] * 2),
]


class Place:

    def __init__(self, kb, gb, pn, an):
        self.kb, self.gb, self.pn, self.an = kb, gb, pn, an


_kb = _gb = _pn = _an = 0
for _s in STAGES:
    _s.start = (_kb, _gb, _pn, _an)
    _s.local = []
    k = g = n = a = 0
    for _kind, _nk in _s.panels:
        _s.local.append((k, g, n, a))
        k += _nk * len(_kind)
        g += _nk * ("w" in _kind)
        n += "w" in _kind
        a += "a" in _kind
    _s.per = (k, g, n, a)
    _kb, _gb, _pn, _an = (x + y * _s.bodies for x, y in zip(_s.start, _s.per))
    _s.end = (_kb, _gb, _pn, _an)
ST = {s.name: s for s in STAGES}


def place(stage, p, j):
    return Place(*(s + l + p * q for s, l, q in zip(stage.start, stage.local[j], stage.per)))


def run_bodies(eng, stage, body):
    body(0, True)
    if stage.bodies > 1:
        with eng.Fori(1, stage.bodies) as p:
            body(p, False)


def program(nc, x, c, ada_w, ada_b, norm_mix_g, norm_ffn_g, w_in, fox_f_bias, cmp_w1, cmp_w2, cmp_pos,
            diff_lambda, diff_subln_g, w_out, w_gate, w_up, w_down, final_g, mem, w_in2, w_out2,
            w_mem_kv, ln_g, ln_b, pool_w, pool_scale, w_kv, out):
    f32, f32r, i32 = mybir.dt.float32, mybir.dt.float32r, mybir.dt.int32
    ACT, ALU, AX = mybir.ActivationFunctionType, mybir.AluOpType, mybir.AxisListType
    ds = bass.ds
    ctx = ExitStack()
    with ctx:
        arena_bytes = 212800
        arena = ctx.enter_context(nc.sbuf_tensor("arena", [P, arena_bytes // 4], f32))
        base = nc.sbuf_base
        base = (base - arena_bytes) // 32 * 32 + 32 if nc.sbuf_base > arena_bytes else (base + 31) // 32 * 32
        top = [0]

        def at(name, shape, dt, off):
            size = 4 * int(np.prod(shape[1:]))
            assert off % 32 == 0 and off + size <= arena_bytes, (name, off, size)
            return nc.alloc_sbuf_tensor_at(name, shape, dt, offset=base + off)

        def new(name, shape, dt=f32):
            off = top[0]
            top[0] += (4 * int(np.prod(shape[1:])) + 31) // 32 * 32
            return at(name, shape, dt, off)

        def region(size):
            off = top[0]
            top[0] += size
            return off

        raw = new("raw", [P, RING, 2, NC])
        r_hilo = region(2 * HILO * NC * 4)
        w_hi = at("w_hi", [P, HILO, NC], f32r, r_hilo)
        w_lo = at("w_lo", [P, HILO, NC], f32r, r_hilo + HILO * NC * 4)
        probs = at("probs", [P, 2, 2, 512], f32, r_hilo)
        probsT = at("probsT", [P, 2, 2, 512], f32, r_hilo + 8192)
        r_act = region(32768)
        actT = at("actT", [P, 2, KD, SEQ], f32r, r_act)
        res_nsa = at("res_nsa", [P, T, 16, HD], f32, r_act)
        res_diff = at("res_diff", [P, T, DIFF, 2, 128], f32, r_act + 8192)
        diff_tmp = at("diff_tmp", [P, T, 512], f32, r_act + 16384)
        pooledT = at("pooledT", [P, 12, SEQ], f32, r_act)
        poolw_s = at("poolw_s", [P, 4, 3, 384], f32, r_act + 12288)
        X = new("X", [P, T, D])
        memkv = new("memkv", [P, 2, T, 1024])
        r_one = region(66048)
        proj = at("proj", [P, T, N_IN], f32, r_one)
        o1 = (N_IN * T * 4 + 31) // 32 * 32
        cumk = at("cumk", [P, FOX, SEQ], f32, r_one + o1)
        dist = at("dist", [P, 5, 384], f32, r_one + o1 + 7168)
        cmask1 = at("cmask1", [P, 384], f32, r_one + o1 + 7168 + 7680)
        upper = at("upper", [P, T, SEQ], f32, r_one + o1 + 7168 + 9216)
        assert o1 + 7168 + 9216 + 2048 <= 66048
        hidT = at("hidT", [P, 2, KD, SEQ], f32r, r_one)
        xn2 = at("xn2", [P, T, D], f32, r_one + 32768)
        hid = at("hid", [P, 2, T, 256], f32, r_one + 49152)
        sil = at("sil", [P, 2, T, 256], f32, r_one + 53248)
        U = at("U", [P, T, 4096], f32, r_one)
        KV = at("KV", [P, T, 3072], f32, r_one + 32768)
        band = at("band", [P, 4, T, SEQ], f32, r_one + 57344)
        r_stg = region(20480)
        gb0 = at("gb0", [P, D], f32, r_stg)
        gb1 = at("gb1", [P, D], f32, r_stg + 8192)
        ada_acc = at("ada_acc", [P, 2, NC], f32, r_stg + 16384)
        w1_s = at("w1_s", [P, 2, CMP_LEN, HD], f32, r_stg)
        qk_s = at("qk_s", [P, 2, 2, T, 128], f32, r_stg)
        v_s = at("v_s", [P, 2, T, 128], f32, r_stg + 4096)
        tab_s = at("tab_s", [P, 2, 2, 384], f32, r_stg + 6144)
        qkT_s = at("qkT_s", [P, 2, 2, SEQ], f32, r_stg + 12288)
        qk2_s = at("qk2_s", [P, 2, 2, T, 256], f32, r_stg)
        v2_s = at("v2_s", [P, 2, T, 256], f32, r_stg + 8192)
        qkT2_s = at("qkT2_s", [P, 2, 2, 2, SEQ], f32, r_stg + 12288)
        ident = new("ident", [P, P])
        ones = new("ones", [P, P])
        rows = new("rows", [P, 2, P])
        pos_r = new("pos_r", [CMP_LEN, 2, 2, HD])
        cols = new("cols", [P, P])
        c_col = new("c_col", [P, KD])
        c_raw = new("c_raw", [P, KD])
        posT = new("posT", [P, 2, CMP_LEN])
        modT = new("modT", [P, 4 * KD])
        gain = new("gain", [P, 2, KD])
        cmask = new("cmask", [P, 384])
        stats = new("stats", [P, T, 4, 6])
        mv = new("mv", [P, T, 2])
        ms = new("ms", [P, T])
        rinv_x = new("rinv_x", [P, T])
        mhalf = new("mhalf", [P, 8])
        sm = new("sm", [P, 2, 8])
        mx = new("mx", [P, 2, 4])
        mx_zero = new("mx_zero", [P, 2, 2])
        rs = new("rs", [P, 2, 4])
        stat = new("stat", [P, 12, 8])
        fox_b = new("fox_b", [P, FOX])
        fz = new("fz", [P, 8, T, FOX])
        logf = new("logf", [P, T, FOX])
        cumq = new("cumq", [P, T, FOX])
        gates = new("gates", [P, T, NSA, 3])
        lamv = new("lamv", [P, 4, HD])
        lam = new("lam", [P, 8])
        subg = new("subg", [P, 128])
        dl = new("dl", [P, 6, T * 9])
        dnm = new("dnm", [P, 2, T, 24])
        dss = new("dss", [P, 3, 8])
        cmp_in = at("cmp_in", [P, 2, 2, SEQ], f32, r_act)
        cmp_h = new("cmp_h", [HD, 2, 2, 16])
        w2_s = new("w2_s", [HD, 2, HD])
        cmp_kv = at("cmp_kv", [P, 2, T, 2, HD], f32, r_act + 24576)
        evac = at("evac", [P, 2, 512], f32, r_one + 49152)
        valid = new("valid", [P, 1])
        rec = new("rec", [P, 16])
        gy = at("gy", [P, T, NC], f32, r_stg + 8192)
        ps = ctx.enter_context(nc.psum_tensor("ps", [P, 8, 512], f32))

        def o3(ap, a):
            return ap.rearrange("p (a b) -> p a b", a=a)

        sems = {}

        def S(name):
            if name not in sems:
                sems[name] = ctx.enter_context(nc.semaphore(name))
            return sems[name]

        w_loaded = [S(f"w_loaded{i}") for i in range(RING)]
        blocks_read = S("blocks_read")
        hi_ready = S("hi_ready")
        parts_used = S("parts_used")
        acc_read = S("acc_read")
        ada_summed = S("ada_summed")
        ada_taken = S("ada_taken")

        def chunks(stage, j):
            kind, nk = stage.panels[j]
            off = 0
            for ch in range(nk // 2):
                for k in kind:
                    yield k, ch, off
                    off += 2

        def stage_loads(sp, name, w_src, a_src=None, width=NC):
            st = ST[name]

            def body(p, first):
                for j in range(len(st.panels)):
                    pl = place(st, p, j)
                    for kind, ch, off in chunks(st, j):
                        slot = ((st.start[0] + st.local[j][0] + off) // 2) % RING
                        sp.wait_ge(blocks_read, pl.kb + off + 2)
                        if kind == "w":
                            for dst, src in w_src(p, j, ch):
                                sp.dma_start(raw[:, slot, :, dst[0]:dst[1]], src).then_inc(w_loaded[slot], 16)
                        else:
                            sp.dma_start(raw[:, slot, :, :], a_src(p, j, ch)).then_inc(w_loaded[slot], 16)
            run_bodies(sp, st, body)

        loads_before = []
        n = [0] * RING
        for st in STAGES:
            st.slot_start = list(n)
            st.slot_local = []
            cnt = [0] * RING
            for j in range(len(st.panels)):
                row = []
                for kind, ch, off in chunks(st, j):
                    s = ((st.start[0] + st.local[j][0] + off) // 2) % RING
                    cnt[s] += 32 if st.name.startswith("gu") and kind == "w" else 16
                    row.append((s, cnt[s]))
                st.slot_local.append(row)
            st.slot_per = cnt
            n = [a + b * st.bodies for a, b in zip(n, cnt)]

        def wait_chunk(eng, st, p, j, idx):
            s, local = st.slot_local[j][idx]
            eng.wait_ge(w_loaded[s], st.slot_start[s] + local + p * st.slot_per[s])

        def stage_split_hi(act, name, hooks=None, width=None):
            st = ST[name]

            def body(p, first):
                for j in range(len(st.panels)):
                    if "w" not in st.panels[j][0]:
                        continue
                    pl = place(st, p, j)
                    w = width[j] if width else NC
                    for idx, (kind, ch, off) in enumerate(chunks(st, j)):
                        if kind != "w":
                            continue
                        for b in range(2):
                            k = 2 * ch + b
                            if hooks and k in hooks and not (first and j == 0):
                                hooks[k](*((p, j - 1) if j else (p - 1, len(st.panels) - 1)))
                            if b == 0:
                                wait_chunk(act, st, p, j, idx)
                            slot = ((st.start[0] + st.local[j][0] + off) // 2) % RING
                            act.wait_ge(parts_used, pl.gb + k + 1)
                            g = (st.local[j][1] + k) % HILO
                            act.activation(w_hi[:, g, 0:w], raw[:, slot, b, 0:w], ACT.Copy).then_inc(hi_ready, 1)
            run_bodies(act, st, body)

        def stage_split_lo(dve, name, hooks=None, width=None, take=None, one_acc=False):
            st = ST[name]
            kinds = [k for k, _ in st.panels]

            def before(p, j):
                return (p, j - 1) if j else (p - 1, len(st.panels) - 1)

            def body(p, first):
                na = 0
                for j in range(len(st.panels)):
                    pl = place(st, p, j)
                    w = width[j] if width else NC
                    alone = first and j == 0
                    for idx, (kind, ch, off) in enumerate(chunks(st, j)):
                        slot = ((st.start[0] + st.local[j][0] + off) // 2) % RING
                        for b in range(2):
                            k = 2 * ch + b
                            if not alone and kind == kinds[j][0]:
                                if k == 12 and take and "a" in kinds[before(0, j)[1]]:
                                    take(*before(p, j))
                                if hooks and k in hooks:
                                    hooks[k](*before(p, j))
                            if kind == "w":
                                dve.wait_ge(hi_ready, pl.gb + k + 1)
                                g = (st.local[j][1] + k) % HILO
                                nc.vector.tensor_tensor(w_lo[:, g, 0:w], raw[:, slot, b, 0:w],
                                                        w_hi[:, g, 0:w].bitcast(f32),
                                                        ALU.subtract).then_inc(blocks_read, 1)
                            else:
                                acc = ada_acc[:, 0 if one_acc else na % 2, :]
                                if k == 0:
                                    wait_chunk(dve, st, p, j, idx)
                                    nc.vector.tensor_scalar(acc, raw[:, slot, b, :], c_col[:, 0:1], None,
                                                            ALU.mult).then_inc(blocks_read, 1)
                                else:
                                    if b == 0:
                                        wait_chunk(dve, st, p, j, idx)
                                    dve.wait_ge(blocks_read, 2 * RING + pl.kb + off + b - (1 if b else
                                                1 + 2 * (len(kinds[j]) - 1)) + 1)
                                    nc.vector.scalar_tensor_tensor(acc, raw[:, slot, b, :], c_col[:, k:k + 1], acc,
                                                                   ALU.mult, ALU.add).then_inc(blocks_read, 1)
                    na += "a" in kinds[j]
            run_bodies(dve, st, body)
            if take and "a" in kinds[-1]:
                take(st.bodies - 1, len(st.panels) - 1)

        def ada_sum(pe, st, p, j, na, as_columns, one_acc=False):
            pl = place(st, p, j)
            acc = ada_acc[:, 0 if one_acc else na % 2, :]
            kind, nk = st.panels[j]
            pe.wait_ge(blocks_read, 2 * RING + pl.kb + nk * len(kind))
            pe.wait_ge(ada_taken, pl.an + 1)
            if as_columns:
                for i in range(4):
                    last = nc.tensor.matmul(ps[:, 6, i:i + 1], acc[:, i * P:(i + 1) * P], ones[:, 0:1],
                                            start=True, stop=True)
            else:
                last = nc.tensor.matmul(ps[:, 6, :], ones[:, :], acc, start=True, stop=True)
            last.then_inc(ada_summed, 1)

        def stage_matmuls(pe, name, lhs, hooks=None, width=None, as_columns=False, one_acc=False):
            st = ST[name]
            kinds = [k for k, _ in st.panels]

            def body(p, first):
                na = 0
                for j, (kind, nk) in enumerate(st.panels):
                    pl = place(st, p, j)
                    w = width[j] if width else NC
                    pj = (p, j - 1) if j else (p - 1, len(st.panels) - 1)
                    pa = [sum("a" in q for q in kinds[:pj[1]])][0]
                    if kind == "a":
                        ada_sum(pe, st, p, j, na, as_columns)
                        na += 1
                        continue
                    pe.wait_ge(acc_read, pl.pn + 1)
                    bank = 2 * ((st.start[2] + st.local[j][2]) % 2)
                    for idx, (kd, ch, off) in enumerate(chunks(st, j)):
                        if kd != "w":
                            continue
                        for b in range(2):
                            k = 2 * ch + b
                            if not (first and j == 0):
                                if k == 8 and "a" in kinds[pj[1]]:
                                    ada_sum(pe, st, pj[0], pj[1], pa, as_columns, one_acc)
                                if hooks and k in hooks:
                                    hooks[k](*pj)
                            pe.wait_ge(blocks_read, 2 * RING + pl.kb + off + b + 1)
                            g = (st.local[j][1] + k) % HILO
                            for t in range(T):
                                hi, lo = (lhs[:, part, k, t * P:(t + 1) * P] for part in range(2))
                                o = ps[:, bank + t, 0:w]
                                nc.tensor.matmul(o, hi, w_hi[:, g, 0:w], start=(k == 0), stop=False)
                                nc.tensor.matmul(o, hi, w_lo[:, g, 0:w], start=False, stop=False)
                                last = nc.tensor.matmul(o, lo, w_hi[:, g, 0:w], start=False, stop=(k == nk - 1))
                            last.then_inc(parts_used, 1)
            run_bodies(pe, st, body)
            if kinds[-1] == "wa":
                ada_sum(pe, st, st.bodies - 1, len(kinds) - 1, sum("a" in q for q in kinds[:-1]), as_columns, one_acc)

        def panel_done(eng, st, p, j):
            pl = place(st, p, j)
            eng.wait_ge(parts_used, HILO + pl.gb + st.panels[j][1])

        def bank_of(st, j):
            return 2 * ((st.start[2] + st.local[j][2]) % 2)

        def panel_no(st, p, j):
            return p * len(st.panels) + j

        TURNS = {tag: 8 * i for i, tag in enumerate(("mem", "u1", "o1", "u2", "h0", "m0", "h1", "m1"))}
        MODS = {"u1": 0, "u2": 8}
        turned = S("turned")
        turn_mod = S("turn_mod")
        turn_hi = S("turn_hi")
        turn_taken = S("turn_taken")

        def transposes(pe, tag, src, ready):
            ready(pe)
            for g in range(8):
                if g >= 4:
                    pe.wait_ge(turn_taken, TURNS[tag] + g - 3)
                for i in range(4):
                    k, t = 2 * g + i // 2, i % 2
                    last = nc.tensor.transpose(ps[:, 4 + g % 4, i * P:(i + 1) * P], src(k, t), ident[:, :])
                last.then_inc(turned, 1)

        def split_plain_hi(act, tag, dst):
            for g in range(8):
                act.wait_ge(turned, TURNS[tag] + g + 1)
                act.activation(dst[:, 0, 2 * g:2 * g + 2, :], o3(ps[:, 4 + g % 4, :], 2),
                               ACT.Copy).then_inc(turn_hi, 1)

        def split_plain_lo(dve, tag, dst):
            for g in range(8):
                dve.wait_ge(turn_hi, TURNS[tag] + g + 1)
                nc.vector.tensor_tensor(dst[:, 1, 2 * g:2 * g + 2, :], o3(ps[:, 4 + g % 4, :], 2),
                                        dst[:, 0, 2 * g:2 * g + 2, :].bitcast(f32),
                                        ALU.subtract).then_inc(turn_taken, 1)

        def split_mod_hi(act, tag, dst):
            for g in range(8):
                act.wait_ge(turn_mod, MODS[tag] + g + 1)
                act.activation(dst[:, 0, 2 * g:2 * g + 2, :], o3(evac[:, g % 2, :], 2),
                               ACT.Copy).then_inc(turn_hi, 1)

        def split_mod_lo(dve, tag, dst, half):
            def low(g):
                dve.wait_ge(turn_hi, TURNS[tag] + g + 1)
                nc.vector.tensor_tensor(dst[:, 1, 2 * g:2 * g + 2, :], o3(evac[:, g % 2, :], 2),
                                        dst[:, 0, 2 * g:2 * g + 2, :].bitcast(f32),
                                        ALU.subtract).then_inc(turn_taken, 1)
            for g in range(8):
                if g >= 2:
                    low(g - 2)
                    dve.wait_ge(turn_taken, TURNS[tag] + g - 1)
                dve.wait_ge(turned, TURNS[tag] + g + 1)
                for i in range(2):
                    k = 2 * g + i
                    last = nc.vector.tensor_scalar(evac[:, g % 2, i * SEQ:(i + 1) * SEQ],
                                                   ps[:, 4 + g % 4, i * SEQ:(i + 1) * SEQ],
                                                   gain[:, half, k:k + 1], modT[:, 32 * half + k:32 * half + k + 1],
                                                   ALU.mult, ALU.add)
                last.then_inc(turn_mod, 1)
            low(6)
            low(7)

        class Attn:

            def __init__(self, tag, pairs, dh, dv, full, table, scale, dest, keep=False):
                self.tag, self.pairs, self.dh, self.dv, self.full = tag, pairs, dh, dv, full
                self.table, self.scale, self.dest, self.keep = table, scale, dest, keep
                self.start = Attn.started
                Attn.started += pairs
                self.kw = 512 if full else 384

            PER = {"exp": 2, "scores": 2, "p_tr": 2}
            started = 0

            def s(self, name):
                return S("at_" + name)

            def wait(self, eng, name, value):
                eng.wait_ge(self.s(name), self.start * self.PER.get(name, 1) + value)

            def staged(self, eng, what, i_par, half):
                n = 64 if what == "qk" else 32
                eng.wait_ge(S(f"at_{what}{i_par}"), n * (self.start // 2) + n * half + n)

            def spans(self):
                return [(0, 0, 256 if self.full else 128), (1, self.kw - 256, 256)]

            def steps(self, eng, step, first):
                first()
                n = self.pairs
                if n > 4:
                    with eng.Fori(0, n // 2 - 2) as p:
                        step(2 * p, 0, p, 3)
                        step(2 * p + 1, 1, p, 3)
                for i in range(max(n - 4, 0), n):
                    step(i, i % 2, i // 2, n - 1 - i)

            def q_src(self, par, kind, head, t):
                if self.dh == HD:
                    return qk_s[:, par, kind, t, :]
                return qk2_s[:, par, kind, t, head * 128:(head + 1) * 128]

            def qT(self, par, head, kind):
                if self.dh == HD:
                    return qkT_s[head * HD:(head + 1) * HD, par, kind, :]
                return qkT2_s[:, par, head, kind, :]

            def v(self, par, head, kt):
                if self.dh == HD:
                    return v_s[:, par, kt, :] if self.dv == 128 else v_s[:, par, kt, head * HD:(head + 1) * HD]
                return v2_s[:, par, kt, head * 128:(head + 1) * 128]

            def pe(self, pe):
                nq = 1 if self.dh == HD else 2

                def turn(i, par, p):
                    self.staged(pe, "qk", par, p)
                    for b in range(nq):
                        for kind in range(2):
                            for t in range(T):
                                last = nc.tensor.transpose(ps[:, b, (kind * T + t) * P:(kind * T + t + 1) * P],
                                                           self.q_src(par, kind, b, t), ident[:, :])
                    last.then_inc(self.s("qk_tr"), 1)

                def scores(i, par, wait_read):
                    self.wait(pe, "qkT", i + 1)
                    if wait_read:
                        if self.table:
                            self.wait(pe, "max", i)
                        else:
                            self.wait(pe, "exp", 2 * i)
                    for h in range(2):
                        q, k = self.qT(par, h, 0), self.qT(par, h, 1)
                        for t, c0, nk in self.spans():
                            last = nc.tensor.matmul(ps[:, 2 + h, c0:c0 + nk], q[:, t * P:(t + 1) * P], k[:, 0:nk],
                                                    start=True, stop=True)
                        last.then_inc(self.s("scores"), 1)

                def step(i, par, p, more):
                    if more:
                        scores(i + 1, 1 - par, True)
                    if more > 1:
                        turn(i + 2, par, p + 1)
                    for h in range(2):
                        self.wait(pe, "exp", 2 * i + h + 1)
                        if h == 1:
                            self.wait(pe, "pT1", i + 1)
                        for t, c0, nk in self.spans():
                            for kt in range(nk // P):
                                d = self.pT_col(kt, t)
                                last = nc.tensor.transpose(ps[:, 4 + h, d:d + P],
                                                           probs[:, par, h, c0 + kt * P:c0 + (kt + 1) * P], ident[:, :])
                        last.then_inc(self.s("p_tr"), 1)
                    self.staged(pe, "v", par, p)
                    for h in range(2):
                        self.wait(pe, "pT0", i + 1) if h == 0 else self.wait(pe, "pT1", i + 2)
                        for t, c0, nk in self.spans():
                            o = ps[:, 6 + par, (t * 2 + h) * self.dv:(t * 2 + h + 1) * self.dv]
                            for kt in range(nk // P):
                                d = self.pT_col(kt, t)
                                last = nc.tensor.matmul(o, probsT[:, par, h, d:d + P], self.v(par, h, kt),
                                                        start=(kt == 0), stop=(kt == nk // P - 1))
                    last.then_inc(self.s("pv"), 1)

                def first():
                    turn(0, 0, 0)
                    scores(0, 0, False)
                    turn(1, 1, 0)
                self.steps(pe, step, first)

            def pT_col(self, kt, t):
                return (kt * T + t) * P if self.full or kt == 0 else 256

            def act(self, act):
                def early(i, par):
                    self.wait(act, "qk_tr", i + 1)
                    if self.dh == HD:
                        act.activation(qkT_s[:, par, :, :], o3(ps[:, 0, :], 2), ACT.Copy).then_inc(self.s("qkT"), 1)
                    else:
                        act.activation(qkT2_s[:, par, :, :, :].rearrange("p a b c -> p (a b c)"),
                                       ps[:, 0:2, :].rearrange("p a b -> p (a b)"), ACT.Copy).then_inc(self.s("qkT"), 1)

                def late(i, par):
                    self.wait(act, "max", i + 1)
                    for h in range(2):
                        for t, c0, nk in self.spans():
                            src = (probs[:, par, h, c0:c0 + nk] if self.table else ps[:, 2 + h, c0:c0 + nk])
                            q = t * 2 + h
                            last = act.activation(probs[:, par, h, c0:c0 + nk], src, ACT.Exp, bias=sm[:, par, q:q + 1],
                                                  scale=self.scale, accum_out=sm[:, par, 4 + q:5 + q])
                        last.then_inc(self.s("exp"), 1)

                def step(i, par, p, more):
                    if more > 1:
                        early(i + 2, par)
                    self.wait(act, "p_tr", 2 * i + 1)
                    act.activation(probsT[:, par, 0, 0:self.kw], ps[:, 4, 0:self.kw],
                                   ACT.Copy).then_inc(self.s("pT0"), 1)
                    if more:
                        late(i + 1, 1 - par)

                def first():
                    early(0, 0)
                    early(1, 1)
                    late(0, 0)
                self.steps(act, step, first)

            def dve(self, dve):
                def late(i, par):
                    if self.table == "staged":
                        self.wait(dve, "tab", i + 1)
                    for h in range(2):
                        self.wait(dve, "scores", 2 * i + h + 1)
                        if self.table:
                            nc.vector.memset(mx_zero[:, par, h:h + 1], 0.0)
                            for t, c0, nk in self.spans():
                                q = t * 2 + h
                                tab = tab_s[:, par, h, c0:c0 + nk] if self.table == "staged" else cmask[:, c0:c0 + nk]
                                last = nc.vector.tensor_tensor_reduce(
                                    out=probs[:, par, h, c0:c0 + nk], in0=ps[:, 2 + h, c0:c0 + nk], in1=tab,
                                    scale=1.0, scalar=-3.0e38, op0=ALU.add, op1=ALU.max,
                                    accum_out=mx[:, par, q:q + 1])
                        else:
                            last = nc.vector.tensor_reduce(mx[:, par, h:h + 3:2], o3(ps[:, 2 + h, :], 2), AX.X, ALU.max)
                    last.then_inc(self.s("raw_max"), 1)
                    self.wait(dve, "raw_max", i + 1)
                    nc.vector.tensor_scalar(sm[:, par, 0:4], mx[:, par, :], -self.scale, None,
                                            ALU.mult).then_inc(self.s("max"), 1)

                def step(i, par, p, more):
                    if more:
                        late(i + 1, 1 - par)
                    self.wait(dve, "p_tr", 2 * i + 2)
                    nc.vector.tensor_copy(probsT[:, par, 1, 0:self.kw], ps[:, 5, 0:self.kw]).then_inc(self.s("pT1"), 1)
                    if self.keep:
                        nc.vector.tensor_copy(stat[:, ds(i, 1), :], sm[:, par:par + 1, :])
                    nc.vector.reciprocal(rs[:, par, :], sm[:, par, 4:8]).then_inc(self.s("rs"), 1)
                    self.wait(dve, "rs", i + 1)
                    self.wait(dve, "pv", i + 1)
                    o = ps[:, 6 + par, 0:4 * self.dv].rearrange("p (t h d) -> p t h d", t=T, h=2)
                    r = rs[:, par, :].rearrange("p (t h) -> p t h", t=T).unsqueeze(3).broadcast_to([P, T, 2, self.dv])
                    nc.vector.tensor_tensor(self.dest(i), o, r, ALU.mult).then_inc(self.s("normed"), 1)

                self.steps(dve, step, lambda: late(0, 0))

            def gather(self, sp, source):
                wide = self.dh == HD2

                def move(i, kinds, sem):
                    for kind in kinds:
                        src = source(i, kind)
                        for t in range(T):
                            qkv = (qk2_s, v2_s) if wide else (qk_s, v_s)
                            dst = qkv[1][:, i % 2, t, :] if kind == 2 else qkv[0][:, i % 2, kind, t, :]
                            if len(src.shape) == 4:
                                dst = dst.rearrange("p (h d) -> p h d", h=2)
                            sp.dma_start(dst, src[:, t]).then_inc(sem, 16)

                for i in range(self.pairs + 2):
                    if i >= 2:
                        if i >= 4:
                            self.wait(sp, "pv", i - 3)
                        move(i - 2, (2,), S(f"at_v{i % 2}"))
                    if i < self.pairs:
                        if i >= 2:
                            self.wait(sp, "qk_tr", i - 1)
                        move(i, (0, 1), S(f"at_qk{i % 2}"))

            def tables(self, pool, build):
                for i in range(self.pairs):
                    if i >= 2:
                        self.wait(pool, "max", i - 1)
                    build(i, i % 2).then_inc(self.s("tab"), 1)

            def finished(self, eng):
                self.wait(eng, "normed", self.pairs)

        SC = HD ** -0.5
        heads = []
        for h in range(FOX):
            heads.append((COL["fox_q"] + h * HD, COL["fox_k"] + h * HD, COL["fox_v"] + h * HD, ("fox", h)))
        for h in range(NSA):
            g = h // (NSA // GROUPS) * HD
            heads.append((COL["nsa_q"] + h * HD, COL["slc_k"] + g, COL["slc_v"] + g, (0, slope(h, NSA))))
        for h in range(DIL):
            heads.append((COL["dil_q"] + h * HD, COL["dil_k"] + h * HD, COL["dil_v"] + h * HD,
                          (1 + h // 3, slope(h, DIL))))
        for h in range(NSA):
            g = h // (NSA // GROUPS) * HD
            heads.append((COL["nsa_q"] + h * HD, COL["win_k"] + g, COL["win_v"] + g, (0, slope(h, NSA))))
        for h in range(NSA):
            heads.append((COL["nsa_q"] + h * HD, ("cmp", h // 4), ("cmp", h // 4), (4, slope(h, NSA))))

        at_main = Attn("main", 12, HD, HD, False, "staged", SC,
                       lambda i: X[:, :, ds(i * 128, 128)].rearrange("p t (h d) -> p t h d", h=2), keep=True)
        at_nsa = Attn("nsa", 8, HD, HD, False, "staged", SC, lambda i: res_nsa[:, :, ds(i * 2, 2), :])
        at_diff = Attn("diff", 4, HD, 128, False, "staged", SC,
                       lambda i: res_diff[:, :, ds(i, 1), :, :].rearrange("p t a m d -> p t (a m) d"))
        SC2 = HD2 ** -0.5

        def mem_attn(tag):
            return Attn(tag, 2, HD2, HD2, True, None, SC2,
                        lambda i: U[:, :, ds(2 * BR + i * 256, 256)].rearrange("p t (h d) -> p t h d", h=2))
        at_mem = [mem_attn("mem0")]
        at_moba = Attn("moba", 6, HD2, HD2, False, "mask", SC2,
                       lambda i: U[:, :, ds(i * 256, 256)].rearrange("p t (h d) -> p t h d", h=2))
        at_mem.append(mem_attn("mem1"))

        def bcast(row, n):
            return row.rearrange("(a n) -> a n", a=1).broadcast_to([P, n])

        NORM = {"n1": 1, "n2": 2, "n3": 3, "l0": 4, "l1": 5}

        block = ctx.enter_context(nc.Block())

        @block.sync
        def _(sp):
            def blocks2(w, row0, ch, c0, n):
                r = row0 + ch * 256
                return w[ds(r, 256), :].rearrange("(b p) n -> p b n", p=P)[:, :, ds(c0, n)]

            def pair64(first):
                def source(i, what):
                    a, b = (h[what] for h in heads[first + 2 * i:first + 2 * i + 2])
                    if isinstance(a, tuple):
                        return cmp_kv[:, what - 1, :, a[1], :].unsqueeze(2).broadcast_to([P, T, 2, HD])
                    if a == b:
                        return proj[:, :, a:a + HD].unsqueeze(2).broadcast_to([P, T, 2, HD])
                    if b == a + HD:
                        return proj[:, :, a:a + 2 * HD]
                    return proj[:, :, a:2 * b - a].rearrange("p t (h s) -> p t h s", h=2)[:, :, :, 0:HD]
                return source

            def pair_diff(i, what):
                c0 = COL[("diff_q", "diff_k", "diff_v")[what]] + i * 128
                return proj[:, :, c0:c0 + 128]

            def pair_mem(layer):
                def source(i, what):
                    if what == 0:
                        return U[:, :, 2 * BR + i * 256:2 * BR + (i + 1) * 256]
                    c0 = (what - 1) * MEMW + i * 256
                    return memkv[:, layer, :, c0:c0 + 256]
                return source

            def pair_moba(i, what):
                src = U if what == 0 else KV
                c0 = i * 256 + (BR if what == 2 else 0)
                return src[:, :, c0:c0 + 256]

            def panels(w, row0=0):
                return lambda p, j, ch: [((0, NC), blocks2(w, row0, ch, p * 2 * NC + j * NC, NC))]

            ADA = {"ada1": lambda p, j: (p * 2 + j) * NC, "win": lambda p, j: 3 * D + (p * 2 + j) * NC,
                   "wout": lambda p, j: 2 * D + (p * 2 + j) * NC, "gu0": lambda p, j: 5 * D + p * NC}

            def ada(name):
                return lambda p, j, ch: blocks2(ada_w[0], 0, ch, ADA[name](p, j), NC)

            def gate_up(first):
                def src(p, j, ch):
                    c0 = first * P + (p * 2 + j) * 256
                    return [((0, 256), blocks2(w_gate[0], 0, ch, c0, 256)), ((256, 512), blocks2(w_up[0], 0, ch, c0, 256))]
                return src

            sp.dma_start(X[:, :, :], mem[0].rearrange("(t p) n -> p t n", p=P)).then_inc(S("mem_in"), 16)
            stage_loads(sp, "memkv", lambda p, j, ch: [((0, NC), w_mem_kv[ds(p, 1), :, :].rearrange("a k n -> (a k) n")[
                ch * 256:(ch + 1) * 256, j * NC:(j + 1) * NC].rearrange("(b p) n -> p b n", p=P))])
            stage_loads(sp, "ada1", None, ada("ada1"))
            stage_loads(sp, "win", panels(w_in[0]), ada("win"))

            def win_end(p, j, ch):
                c0, n = (8 * NC + j * NC, NC) if j < 3 else (N_IN - LAST_W, LAST_W)
                return [((0, n), blocks2(w_in[0], 0, ch, c0, n))]
            stage_loads(sp, "win_end", win_end)
            sp.wait_ge(S("cmp_done"), 1)
            at_main.gather(sp, pair64(0))
            at_main.wait(sp, "pv", 12)
            at_nsa.gather(sp, pair64(24))
            at_nsa.wait(sp, "pv", 8)
            at_diff.gather(sp, pair_diff)
            stage_loads(sp, "wout", panels(w_out[0]), ada("wout"))
            stage_loads(sp, "gu0", gate_up(0), ada("gu0"))
            stage_loads(sp, "down0", panels(w_down[0], 0))
            stage_loads(sp, "gu1", gate_up(16))
            stage_loads(sp, "down1", panels(w_down[0], 2048))
            stage_loads(sp, "gu2", gate_up(32))
            stage_loads(sp, "down2", panels(w_down[0], 4096))
            stage_loads(sp, "in0", panels(w_in2[0]))
            sp.wait_ge(S("pool_mixed"), 8)
            at_mem[0].gather(sp, pair_mem(0))
            stage_loads(sp, "out0", panels(w_out2[0]))
            stage_loads(sp, "kv", panels(w_kv))
            stage_loads(sp, "in1", panels(w_in2[1]))
            sp.wait_ge(S("u1l_done"), 1)
            at_moba.gather(sp, pair_moba)
            at_moba.wait(sp, "pv", 6)
            at_mem[1].gather(sp, pair_mem(1))
            stage_loads(sp, "out1", panels(w_out2[1]))
            for t in range(T):
                sp.wait_ge(S("y_done"), t + 1)
                sp.dma_start(out[0, t * P:(t + 1) * P, :], X[:, t, :]).then_inc(S("stored"), 16)
            sp.wait_ge(S("stored"), 16 * T)

        @block.gpsimd
        def _(pool):
            g = nc.gpsimd
            cn = [0]

            def chain(ins):
                cn[0] += 1
                ins.then_inc(S("pool_chain"), 1)
                pool.wait_ge(S("pool_chain"), cn[0])

            pool.dma_start(rows[0:96, 0, :], ada_b[0].rearrange("(r n) -> r n", n=P)).then_inc(S("rows_in"), 16)
            pool.dma_start(rows[96:112, 0, :], norm_mix_g[0].rearrange("(r n) -> r n", n=P)).then_inc(S("rows_in"), 16)
            pool.dma_start(rows[112:128, 0, :], norm_ffn_g[0].rearrange("(r n) -> r n", n=P)).then_inc(S("rows_in"), 16)
            pool.dma_start(rows[0:KD, 1, :], c[0].rearrange("(r n) -> r n", n=P)).then_inc(S("rows_in"), 16)
            chain(g.memset(ident[:, :], 0.0))
            g.affine_select(out=ident[:, :], in_=ident[:, :], compare_op=ALU.not_equal, fill=1.0, base=0,
                            pattern=[[-1, P]], channel_multiplier=1).then_inc(S("ident"), 1)
            g.memset(ones[:, :], 1.0).then_inc(S("ones"), 1)
            g.memset(mhalf[:, :], -0.5)
            for half in range(2):
                for kv in range(2):
                    pool.dma_start(pos_r[:, kv, half, :], cmp_pos[0, kv]).then_inc(S("cmp_in"), 16)
                    pool.dma_start(w1_s[half * HD:(half + 1) * HD, kv, :, :],
                                   cmp_w1[0, kv].rearrange("(j d) f -> d j f", d=HD)).then_inc(S("cmp_in"), 16)
            pool.dma_start(w2_s[:, :, :], cmp_w2[0].rearrange("a d f -> d a f")).then_inc(S("cmp_in"), 16)
            pool.dma_start(fox_b[:, :], bcast(fox_f_bias[0], FOX)).then_inc(S("cmp_in"), 16)
            pool.dma_start(lamv[:, :, :], diff_lambda[0].rearrange("(a r) d -> a r d", a=1).broadcast_to([P, 4, HD])
                           ).then_inc(S("cmp_in"), 16)
            pool.dma_start(subg[:, :], bcast(diff_subln_g[0], 128)).then_inc(S("cmp_in"), 16)
            spans = [(0, 128, 0), (128, 256, 128)]
            for c0, n, q0 in spans:
                g.iota(dist[:, 0, c0:c0 + n], [[-1, n]], base=q0, channel_multiplier=1,
                       allow_small_or_imprecise_dtypes=True)
                g.iota(dist[:, 4, c0:c0 + n], [[-CMP_STRIDE, n]], base=q0 - (CMP_LEN - 1), channel_multiplier=1,
                       allow_small_or_imprecise_dtypes=True)
                for kk in (2, 3):
                    last = g.iota(dist[:, kk, c0:c0 + n].bitcast(i32), [[-1, n]], base=q0 + 256, channel_multiplier=1)
            chain(last)
            chain(g.memset(cmask[:, :], 0.0))
            for c0, n, q0 in spans:
                g.affine_select(out=dist[:, 0, c0:c0 + n], in_=dist[:, 0, c0:c0 + n], compare_op=ALU.is_ge, fill=MASKED,
                                base=q0, pattern=[[-1, n]], channel_multiplier=1)
                g.affine_select(out=dist[:, 4, c0:c0 + n], in_=dist[:, 4, c0:c0 + n], compare_op=ALU.is_ge, fill=MASKED,
                                base=q0 - (CMP_LEN - 1), pattern=[[-CMP_STRIDE, n]], channel_multiplier=1)
                last = g.affine_select(out=cmask[:, c0:c0 + n], in_=cmask[:, c0:c0 + n], compare_op=ALU.is_ge,
                                       fill=-MASKED, base=q0, pattern=[[-1, n]], channel_multiplier=1)
            chain(last)
            for c0, n, q0 in spans:
                last = g.affine_select(out=dist[:, 1, c0:c0 + n], in_=dist[:, 0, c0:c0 + n], compare_op=ALU.is_ge,
                                       fill=MASKED, base=128 - q0, pattern=[[1, n]], channel_multiplier=-1)
            last.then_inc(S("dist"), 1)
            chain(g.memset(upper[:, :, :], -1.0 / SC))
            for t in range(T):
                last = g.affine_select(out=upper[:, t, :], in_=upper[:, t, :], compare_op=ALU.is_ge, fill=0.0,
                                       base=-t * P, pattern=[[1, SEQ]], channel_multiplier=-1)
            last.then_inc(S("upper"), 1)
            chain(g.memset(valid[:, :], 1.0))
            g.affine_select(out=valid[:, :], in_=valid[:, :], compare_op=ALU.is_ge, fill=0.0, base=-(CMP_LEN - 1),
                            pattern=[[0, 1]], channel_multiplier=1).then_inc(S("valid"), 1)
            for i in range(16):
                last = g.memset(rec[:, i:i + 1], 1.0 / (i + 1))
            chain(last)

            pool.wait_ge(turned, TURNS["mem"] + 8)
            pool.dma_start(X[:, :, :], x[0].rearrange("(t p) n -> p t n", p=P)).then_inc(S("x_in"), 16)

            def inv_sqrt(tag, n, dst, src):
                pool.wait_ge(S("ms"), NORM[tag])
                g.tensor_tensor(dst, src, mhalf[:, 0:n], ALU.pow).then_inc(S("rinv"), 1)
            inv_sqrt("n1", T, rinv_x[:, :], ms[:, :])

            pool.wait_ge(S("proj_done"), 1)
            g.memset(cmp_kv[:, :, :, :, :].rearrange("p a t g d -> p (a t g d)"), 0.0).then_inc(S("cmp_zero"), 1)

            pool.wait_ge(S("tabs"), 1)
            pool.wait_ge(S("cmp_done"), 1)

            def fox_table(par, h, val):
                for t, c0, n in at_main.spans():
                    last = g.tensor_tensor(tab_s[:, par, h, c0:c0 + n], cmask[:, c0:c0 + n], cumk[:, val, 0:n], ALU.add)
                chain(last)
                for t, c0, n in at_main.spans():
                    last = g.tensor_scalar(tab_s[:, par, h, c0:c0 + n], tab_s[:, par, h, c0:c0 + n],
                                           cumq[:, t, val:val + 1], 1.0, ALU.add, ALU.mult)
                return last

            def tables64(first):
                def build(i, par):
                    for h in range(2):
                        kind, val = heads[first + 2 * i + h][3]
                        last = fox_table(par, h, val) if kind == "fox" else g.tensor_scalar(
                            tab_s[:, par, h, :], dist[:, kind, :], -val / SC, 1.0, ALU.mult, ALU.mult)
                    return last
                return build

            def tables_diff(i, par):
                return g.tensor_scalar(tab_s[:, par, :, :], dist[:, 0, :].unsqueeze(1).broadcast_to([P, 2, 384]),
                                       -slope(i, DIFF) / SC, 1.0, ALU.mult, ALU.mult)
            at_main.tables(pool, tables64(0))
            at_main.wait(pool, "max", 12)
            at_nsa.tables(pool, tables64(24))
            at_nsa.wait(pool, "max", 8)
            at_diff.tables(pool, tables_diff)

            pool.wait_ge(S("dif_ms"), 1)
            g.tensor_tensor(dss[:, 2, :], dss[:, 1, :], mhalf[:, 0:8], ALU.pow).then_inc(S("dif_rinv"), 1)

            pool.wait_ge(turned, TURNS["o1"] + 8)
            pool.dma_start(X[:, :, :], x[0].rearrange("(t p) n -> p t n", p=P)).then_inc(S("x_again"), 16)
            pool.dma_start(gb0[:, :], bcast(ada_b[0, 2 * D:3 * D], D)).then_inc(S("x_again"), 16)
            inv_sqrt("n2", T, rinv_x[:, :], ms[:, :])
            pool.dma_start(gb0[:, :], bcast(ada_b[0, 5 * D:6 * D], D)).then_inc(S("g2b_in"), 16)
            for w, win in enumerate(POOL_WINDOWS):
                for s in range(T):
                    g.tensor_copy(band[:, w, s, 0:win], rec[:, 0:win])
                    last = g.memset(band[:, w, s, win:SEQ], 1.0 / win)
            chain(last)
            for w, win in enumerate(POOL_WINDOWS):
                for s in range(T):
                    last = g.affine_select(out=band[:, w, s, :], in_=band[:, w, s, :], compare_op=ALU.is_ge, fill=0.0,
                                           base=-s * P, pattern=[[1, SEQ]], channel_multiplier=-1)
            chain(last)
            for w, win in enumerate(POOL_WINDOWS):
                for s in range(T):
                    last = g.affine_select(out=band[:, w, s, :], in_=band[:, w, s, :], compare_op=ALU.is_ge, fill=0.0,
                                           base=win - 1 + s * P, pattern=[[-1, SEQ]], channel_multiplier=1)
            chain(last)
            for w in range(4):
                for s in range(T):
                    last = g.tensor_tensor(band[:, w, s, s * P:(s + 1) * P], band[:, w, s, s * P:(s + 1) * P],
                                           ident[:, :], ALU.subtract)
            last.then_inc(S("band"), 1)

            inv_sqrt("n3", T, rinv_x[:, :], ms[:, :])
            pool.dma_start(gb0[:, :], bcast(final_g, D)).then_inc(S("fin_in"), 16)

            pool.wait_ge(S("u0_done"), 1)
            for grp in range(4):
                pool.dma_start(poolw_s[:, grp, :, :], pool_w[0, grp].rearrange("(k p) n -> p k n", p=P)
                               ).then_inc(S("poolw_in"), 16)
            pool.dma_start(gb0[:, 0:BR], bcast(pool_scale[0], BR)).then_inc(S("poolw_in"), 16)
            pool.wait_ge(turned, TURNS["m0"] + 8)
            pool.dma_start(gb0[:, :], bcast(ln_g[0], D)).then_inc(S("ln0_in"), 16)
            pool.dma_start(gb1[:, :], bcast(ln_b[0], D)).then_inc(S("ln0_in"), 16)
            inv_sqrt("l0", T, rinv_x[:, :], ms[:, :])
            pool.wait_ge(turned, TURNS["m1"] + 8)
            pool.dma_start(gb0[:, :], bcast(ln_g[1], D)).then_inc(S("ln1_in"), 16)
            pool.dma_start(gb1[:, :], bcast(ln_b[1], D)).then_inc(S("ln1_in"), 16)
            inv_sqrt("l1", T, rinv_x[:, :], ms[:, :])

        @block.tensor
        def _(pe):
            pe.sem_inc(parts_used, HILO)
            pe.wait_ge(S("ident"), 1)
            pe.wait_ge(S("rows_in"), 64)
            nc.tensor.transpose(ps[:, 0, 0:P], rows[:, 0, :], ident[:, :])
            nc.tensor.transpose(ps[:, 0, P:P + KD], rows[0:KD, 1, :], ident[0:KD, 0:KD]).then_inc(S("cols_tr"), 1)
            transposes(pe, "mem", lambda k, t: X[:, t, k * P:(k + 1) * P], lambda e: e.wait_ge(S("mem_in"), 16))
            pe.wait_ge(S("cols_done"), 1)
            pe.wait_ge(turn_taken, TURNS["mem"] + 8)
            stage_matmuls(pe, "memkv", actT)
            pe.wait_ge(S("ones"), 1)
            stage_matmuls(pe, "ada1", None, as_columns=True)
            pe.wait_ge(S("cmp_in"), 16 * 12)
            pe.wait_ge(ada_taken, 1 + ST["ada1"].end[3])
            transposes(pe, "u1", lambda k, t: X[:, t, k * P:(k + 1) * P], lambda e: e.wait_ge(S("xn"), 1))
            pe.wait_ge(turn_taken, TURNS["u1"] + 8)
            stage_matmuls(pe, "win", actT, as_columns=True)
            stage_matmuls(pe, "win_end", actT, width=[NC, NC, NC, LAST_W])

            pe.wait_ge(S("upper"), 1)
            pe.wait_ge(S("logf"), 1)
            for h in range(FOX):
                for s in range(T):
                    last = nc.tensor.matmul(ps[:, 4 + h // 2, (h % 2) * SEQ:(h % 2 + 1) * SEQ],
                                            logf[:, s, h:h + 1].broadcast_to([P, P]), upper[:, s, :],
                                            start=(s == 0), stop=(s == 1))
            for t in range(T):
                for s in range(T):
                    last = nc.tensor.matmul(ps[:, 3, t * FOX:(t + 1) * FOX], upper[:, s, t * P:(t + 1) * P],
                                            logf[:, s, :], start=(s == 0), stop=(s == 1))
            last.then_inc(S("cum_ps"), 1)
            for kv in range(2):
                for t in range(T):
                    cc = COL["cmp_k"] + kv * 128
                    last = nc.tensor.transpose(ps[:, 0, (kv * T + t) * P:(kv * T + t + 1) * P],
                                               proj[:, t, cc:cc + 128], ident[:, :])
            for kv in range(2):
                last = nc.tensor.transpose(ps[:, 1, kv * CMP_LEN:(kv + 1) * CMP_LEN],
                                           pos_r[:, kv, :, :].rearrange("j a d -> j (a d)"),
                                           ident[0:CMP_LEN, 0:CMP_LEN])
            last.then_inc(S("cmp_tr"), 1)
            pe.wait_ge(S("cmp_pos"), 1)
            for grp in range(GROUPS):
                half = slice(grp * HD, (grp + 1) * HD)
                for kv in range(2):
                    for j in range(CMP_LEN):
                        r, jj = divmod(j, CMP_STRIDE)
                        src = cmp_in[half, kv, r, :].rearrange("p (c j) -> p c j", j=CMP_STRIDE)[:, r:r + N_CMP, jj]
                        last = nc.tensor.matmul(ps[0:HD, 1 + grp, 64 + kv * 16:64 + kv * 16 + N_CMP],
                                                w1_s[half, kv, j, :], src, start=(j == 0), stop=(j == CMP_LEN - 1))
            last.then_inc(S("cmp_h_ps"), 1)
            pe.wait_ge(S("cmp_h"), 1)
            for kv in range(2):
                for grp in range(GROUPS):
                    last = nc.tensor.matmul(ps[0:N_CMP, 0, (kv * 2 + grp) * HD:(kv * 2 + grp + 1) * HD],
                                            cmp_h[:, kv, grp, 0:N_CMP], w2_s[:, kv, :], start=True, stop=True)
            last.then_inc(S("cmp_ps"), 1)
            pe.wait_ge(S("cmp_done"), 1)
            pe.wait_ge(S("tabs"), 1)
            at_main.pe(pe)
            at_nsa.pe(pe)
            at_diff.pe(pe)
            transposes(pe, "o1", lambda k, t: X[:, t, k * P:(k + 1) * P], lambda e: e.wait_ge(S("o1_ready"), 1))
            pe.wait_ge(turn_taken, TURNS["o1"] + 8)
            stage_matmuls(pe, "wout", actT, one_acc=False)
            transposes(pe, "u2", lambda k, t: xn2[:, t, k * P:(k + 1) * P], lambda e: e.wait_ge(S("xn"), 2))
            pe.wait_ge(turn_taken, TURNS["u2"] + 8)
            done = 0
            for i in range(3):
                st = ST[f"gu{i}"]

                def turn(p, j):
                    q = panel_no(st, p, j)
                    pe.wait_ge(acc_read, 2 + place(st, p, j).pn + 1)
                    for kk in range(2):
                        for t in range(T):
                            last = nc.tensor.transpose(ps[:, 4 + j, (kk * T + t) * P:(kk * T + t + 1) * P],
                                                       hid[:, j, t, kk * P:(kk + 1) * P], ident[:, :])
                    last.then_inc(S("hid_tr"), 1)
                stage_matmuls(pe, f"gu{i}", actT, hooks={11: turn}, one_acc=True)
                turn(st.bodies - 1, 1)
                pe.wait_ge(S("hid_taken"), 8 * i + 2 * st.bodies)
                stage_matmuls(pe, f"down{i}", hidT)
            transposes(pe, "h0", lambda k, t: X[:, t, k * P:(k + 1) * P], lambda e: e.wait_ge(S("h0_ready"), T))
            pe.wait_ge(turn_taken, TURNS["h0"] + 8)
            stage_matmuls(pe, "in0", actT)
            pe.wait_ge(S("u0_done"), 1)
            pe.wait_ge(S("band"), 1)
            for cb in range(12):
                bank = cb // 2 % 2
                if cb % 2 == 0 and cb >= 4:
                    pe.wait_ge(S("pooledT"), cb // 2 - 1)
                for s in range(T):
                    last = nc.tensor.matmul(ps[:, bank, (cb % 2) * SEQ:(cb % 2 + 1) * SEQ],
                                            U[:, s, cb * P:(cb + 1) * P], band[:, cb // 3, s, :],
                                            start=(s == 0), stop=(s == 1))
                if cb % 2:
                    last.then_inc(S("pool_ps"), 1)
            pe.wait_ge(S("pooledT"), 6)
            pe.wait_ge(S("poolw_in"), 80)
            for grp in range(4):
                for t in range(T):
                    n = grp * T + t
                    if n >= 2:
                        pe.wait_ge(S("pool_mixed"), n - 1)
                    for kk in range(3):
                        last = nc.tensor.matmul(ps[:, 2 + n % 2, 0:384], pooledT[:, grp * 3 + kk, t * P:(t + 1) * P],
                                                poolw_s[:, grp, kk, :], start=(kk == 0), stop=(kk == 2))
                    last.then_inc(S("pool_out"), 1)
            pe.wait_ge(S("pool_mixed"), 8)
            at_mem[0].pe(pe)
            mixed = lambda k, t: U[:, t, k * P:(k + 1) * P] if k < 12 else U[:, t, 2 * BR + (k - 12) * P:2 * BR + (k - 11) * P]
            transposes(pe, "m0", mixed, lambda e: e.wait_ge(S("m0_ready"), 1))
            pe.wait_ge(turn_taken, TURNS["m0"] + 8)
            stage_matmuls(pe, "out0", actT)
            transposes(pe, "h1", lambda k, t: X[:, t, k * P:(k + 1) * P], lambda e: e.wait_ge(S("h1_ready"), T))
            pe.wait_ge(turn_taken, TURNS["h1"] + 8)
            stage_matmuls(pe, "kv", actT)
            stage_matmuls(pe, "in1", actT)
            pe.wait_ge(S("u1l_done"), 1)
            at_moba.pe(pe)
            at_mem[1].pe(pe)
            transposes(pe, "m1", mixed, lambda e: e.wait_ge(S("m1_ready"), 1))
            pe.wait_ge(turn_taken, TURNS["m1"] + 8)
            stage_matmuls(pe, "out1", actT)

        @block.scalar
        def _(act):
            a = nc.scalar

            def stage_copy(name, dst, flag=None, width=None):
                st = ST[name]

                def take(p, j):
                    panel_done(act, st, p, j)
                    for t in range(T):
                        d = dst(p, j, t)
                        w = width[j] if width else NC
                        last = a.activation(d, ps[:, bank_of(st, j) + t, 0:w], ACT.Copy)
                    last.then_inc(acc_read, 1)
                stage_split_hi(act, name, {6: take}, width)
                take(st.bodies - 1, len(st.panels) - 1)
                if flag:
                    act.wait_ge(acc_read, 2 + st.end[2])
                    act.sem_inc(S(flag), 1)

            act.sem_inc(acc_read, 2)
            act.wait_ge(S("cols_tr"), 1)
            a.activation(c_col[:, :], ps[:, 0, P:P + KD], ACT.Silu).then_inc(S("c_col"), 1)
            split_plain_hi(act, "mem", actT)
            stage_copy("memkv", lambda p, j, t: memkv[:, ds(p, 1), t, j * NC:(j + 1) * NC].rearrange("p a n -> p (a n)"))
            act.wait_ge(S("rinv"), NORM["n1"])
            for t in range(T):
                last = a.activation(X[:, t, :], X[:, t, :], ACT.Copy, scale=rinv_x[:, t:t + 1])
            last.then_inc(S("xn"), 1)
            split_mod_hi(act, "u1", actT)
            stage_copy("win", lambda p, j, t: proj[:, t, ds(p * 2 * NC + j * NC, NC)])
            stage_copy("win_end", lambda p, j, t: proj[:, t, (8 + j) * NC:(9 + j) * NC] if j < 3 else
                       proj[:, t, N_IN - LAST_W:N_IN], "proj_done", width=[NC, NC, NC, LAST_W])
            act.wait_ge(S("fz"), 1)
            a.activation(fz[:, 2, :, :], fz[:, 1, :, :], ACT.Exp).then_inc(S("fe"), 1)
            act.wait_ge(S("lam_s"), 1)
            a.activation(lam[:, 2:4], lam[:, 0:2], ACT.Exp).then_inc(S("lam_e"), 1)
            a.activation(gates[:, :, :, :].rearrange("p t h c -> p t (h c)"), proj[:, :, COL["gate"]:COL["gate"] + 24],
                         ACT.Sigmoid).then_inc(S("gates"), 1)
            act.wait_ge(S("cmp_h_ps"), 1)
            for grp in range(GROUPS):
                last = a.activation(cmp_h[:, :, grp, 0:N_CMP], o3(ps[0:HD, 1 + grp, 64:96], 2)[:, :, 0:N_CMP],
                                    ACT.Gelu_apprx_tanh)
            last.then_inc(S("cmp_h"), 1)
            act.wait_ge(S("cmp_done"), 1)
            act.wait_ge(S("tabs"), 1)
            at_main.act(act)
            at_nsa.act(act)
            at_diff.act(act)
            act.wait_ge(S("dd"), 1)
            a.activation(dl[:, 2, :], dl[:, 1, :], ACT.Exp).then_inc(S("dexp"), 1)
            split_plain_hi(act, "o1", actT)
            stage_split_hi(act, "wout")
            act.wait_ge(S("rinv"), NORM["n2"])
            for t in range(T):
                last = a.activation(xn2[:, t, :], X[:, t, :], ACT.Copy, scale=rinv_x[:, t:t + 1])
            last.then_inc(S("xn"), 1)
            split_mod_hi(act, "u2", actT)
            for i in range(3):
                st = ST[f"gu{i}"]

                def gate_act(p, j):
                    panel_done(act, st, p, j)
                    for t in range(T):
                        last = a.activation(sil[:, j, t, :], ps[:, bank_of(st, j) + t, 0:256], ACT.Silu)
                    last.then_inc(S("sil"), 1)

                def hid_hi(p, j):
                    q = panel_no(st, p, j)
                    act.wait_ge(S("hid_tr"), 8 * i + q + 1)
                    a.activation(hidT[:, 0, ds(2 * q, 2), :], o3(ps[:, 4 + j, :], 2), ACT.Copy).then_inc(S("hid_hi"), 1)
                stage_split_hi(act, f"gu{i}", {6: gate_act, 15: hid_hi})
                gate_act(st.bodies - 1, 1)
                hid_hi(st.bodies - 1, 1)
                stage_split_hi(act, f"down{i}")
            split_plain_hi(act, "h0", actT)

            def u_dst(p, j, t):
                return U[:, t, ds(p * 2 * NC + j * NC, NC)]
            stage_copy("in0", u_dst, "u0_done")

            def silu_gates(tag):
                a.activation(U[:, :, BR:2 * BR], U[:, :, BR:2 * BR], ACT.Silu)
                a.activation(U[:, :, 2 * BR + 512:], U[:, :, 2 * BR + 512:], ACT.Silu).then_inc(S(tag), 1)
            silu_gates("gsilu0")
            for n in range(6):
                act.wait_ge(S("pool_ps"), n + 1)
                a.activation(pooledT[:, 2 * n:2 * n + 2, :], o3(ps[:, n % 2, :], 2), ACT.Copy).then_inc(S("pooledT"), 1)
            act.wait_ge(S("pool_mixed"), 8)
            at_mem[0].act(act)
            split_plain_hi(act, "m0", actT)
            stage_split_hi(act, "out0")
            split_plain_hi(act, "h1", actT)
            stage_copy("kv", lambda p, j, t: KV[:, t, ds(p * 2 * NC + j * NC, NC)])
            stage_copy("in1", u_dst, "u1l_done")
            silu_gates("gsilu1")
            at_moba.act(act)
            at_mem[1].act(act)
            split_plain_hi(act, "m1", actT)
            stage_split_hi(act, "out1")

        @block.vector
        def _(dve):
            v = nc.vector
            cn = [0]

            def chain(ins):
                cn[0] += 1
                ins.then_inc(S("dve_chain"), 1)
                dve.wait_ge(S("dve_chain"), cn[0])

            def take_columns(first_bias, first_mod):
                def take(st):
                    def f(p, j):
                        pl = place(st, p, j)
                        q = p * 2 + j
                        dve.wait_ge(ada_summed, pl.an + 1)
                        v.tensor_tensor(modT[:, ds(first_mod + q * 4, 4)], ps[:, 6, 0:4],
                                        cols[:, ds(first_bias + q * 4, 4)], ALU.add).then_inc(ada_taken, 1)
                    return f
                return take

            def take_rows(st, per):
                def f(p, j):
                    pl = place(st, p, j)
                    q = p * 2 + j if per == 2 else p
                    dve.wait_ge(ada_summed, pl.an + 1)
                    v.tensor_tensor(gb0[:, ds(q * NC, NC)], ps[:, 6, :], gb0[:, ds(q * NC, NC)],
                                    ALU.add).then_inc(ada_taken, 1)
                return f

            def moments(tag, eps, rms):
                for t in range(T):
                    for i in range(4):
                        last = v.bn_stats(stats[:, t, i, :], X[:, t, i * 512:(i + 1) * 512])
                chain(last)
                for t in range(T):
                    last = v.bn_aggr(mv[:, t, :], stats[:, t, :, :].rearrange("p a b -> p (a b)"))
                chain(last)
                if rms:
                    chain(v.tensor_tensor(ms[:, :], mv[:, :, 0], mv[:, :, 0], ALU.mult))
                    chain(v.tensor_tensor(ms[:, :], ms[:, :], mv[:, :, 1], ALU.add))
                    v.tensor_scalar(ms[:, :], ms[:, :], eps, None, ALU.add).then_inc(S("ms"), 1)
                else:
                    v.tensor_scalar(ms[:, :], mv[:, :, 1], eps, None, ALU.add).then_inc(S("ms"), 1)

            def gains(half):
                m = modT[:, 32 * half + KD:32 * half + 2 * KD]
                chain(v.tensor_scalar(m, m, 1.0, None, ALU.add))
                chain(v.tensor_tensor(gain[:, half, :], m, cols[:, 96 + KD * half:96 + KD * (half + 1)], ALU.mult))

            dve.sem_inc(blocks_read, 2 * RING)
            dve.sem_inc(ada_taken, 1)
            dve.sem_inc(S("at_pT1"), 1)
            dve.wait_ge(S("cols_tr"), 1)
            dve.wait_ge(S("c_col"), 1)
            v.tensor_copy(cols[:, :], ps[:, 0, 0:P]).then_inc(S("cols_done"), 1)
            dve.wait_ge(S("cols_done"), 1)
            split_plain_lo(dve, "mem", actT)
            stage_split_lo(dve, "memkv")
            dve.wait_ge(S("x_in"), 16)
            moments("n1", RMS_EPS, True)
            st = ST["ada1"]
            stage_split_lo(dve, "ada1", take=take_columns(0, 0)(st))
            dve.wait_ge(ada_taken, 1 + ST["ada1"].end[3])
            gains(0)
            split_mod_lo(dve, "u1", actT, 0)
            stage_split_lo(dve, "win", take=take_columns(48, 32)(ST["win"]))
            stage_split_lo(dve, "win_end", width=[NC, NC, NC, LAST_W])

            dve.wait_ge(S("dist"), 1)
            for kk, mask in ((2, 3), (3, 15)):
                di = dist[:, kk, :].bitcast(i32)
                chain(v.tensor_scalar(di, di, mask, None, ALU.bitwise_and))
                chain(v.tensor_scalar(dist[:, kk, :], di, 1.0, MASKED, ALU.min, ALU.mult))
                chain(v.tensor_tensor(dist[:, kk, :], dist[:, kk, :], dist[:, 0, :], ALU.add))
            dve.wait_ge(S("proj_done"), 1)
            dve.wait_ge(S("cmp_in"), 16 * 12)
            fb = fox_b[:, :].unsqueeze(1).broadcast_to([P, T, FOX])
            chain(v.tensor_tensor(fz[:, 0, :, :], proj[:, :, COL["fox_f"]:COL["fox_f"] + FOX], fb, ALU.add))
            chain(v.tensor_scalar(fz[:, 1, :, :], fz[:, 0, :, :], -1.0, None, ALU.mult))
            chain(v.tensor_tensor(fz[:, 1, :, :], fz[:, 1, :, :], fz[:, 0, :, :], ALU.min))
            dve.sem_inc(S("fz"), 1)
            for i in range(2):
                chain(v.tensor_tensor_reduce(out=lamv[:, 2 * i, :], in0=lamv[:, 2 * i, :], in1=lamv[:, 2 * i + 1, :],
                                             scale=1.0, scalar=0.0, op0=ALU.mult, op1=ALU.add,
                                             accum_out=lam[:, i:i + 1]))
            dve.sem_inc(S("lam_s"), 1)
            dve.wait_ge(S("fe"), 1)
            e, tt, t2, acc = (fz[:, i, :, :] for i in (2, 3, 4, 5))
            chain(v.tensor_scalar(tt, e, 2.0, None, ALU.add))
            chain(v.reciprocal(tt, tt))
            chain(v.tensor_tensor(tt, tt, e, ALU.mult))
            chain(v.tensor_tensor(t2, tt, tt, ALU.mult))
            chain(v.tensor_scalar(acc, t2, 1.0 / 17.0, None, ALU.mult))
            for m in (15, 13, 11, 9, 7, 5, 3):
                chain(v.scalar_tensor_tensor(acc.rearrange("p t h -> p (t h)"), acc.rearrange("p t h -> p (t h)"), 1.0 / m,
                                             t2.rearrange("p t h -> p (t h)"), ALU.add, ALU.mult))
            chain(v.scalar_tensor_tensor(acc.rearrange("p t h -> p (t h)"), acc.rearrange("p t h -> p (t h)"), 1.0,
                                         tt.rearrange("p t h -> p (t h)"), ALU.add, ALU.mult))
            chain(v.tensor_scalar(fz[:, 6, :, :], fz[:, 0, :, :], 0.0, None, ALU.min))
            v.scalar_tensor_tensor(logf[:, :, :].rearrange("p t h -> p (t h)"), acc.rearrange("p t h -> p (t h)"), -2.0,
                                   fz[:, 6, :, :].rearrange("p t h -> p (t h)"), ALU.mult, ALU.add).then_inc(S("logf"), 1)
            dve.wait_ge(S("cum_ps"), 1)
            for h in range(FOX):
                last = v.tensor_copy(cumk[:, h, :], ps[:, 4 + h // 2, (h % 2) * SEQ:(h % 2 + 1) * SEQ])
            chain(last)
            v.tensor_scalar(cumq[:, :, :].rearrange("p t h -> p (t h)"), ps[:, 3, 0:T * FOX], -1.0, None,
                            ALU.mult).then_inc(S("tabs"), 1)
            dve.wait_ge(S("lam_e"), 1)
            chain(v.tensor_tensor(lam[:, 4:5], lam[:, 3:4], lam[:, 2:3], ALU.subtract))
            chain(v.tensor_scalar(lam[:, 5:6], lam[:, 4:5], -LAM_INIT, None, ALU.add))
            chain(v.tensor_scalar(subg[:, :], subg[:, :], 1.0 - LAM_INIT, None, ALU.mult))
            dve.wait_ge(S("cmp_tr"), 1)
            chain(v.tensor_copy(posT[:, :, :].rearrange("p a j -> p (a j)"), ps[:, 1, 0:2 * CMP_LEN]))
            for kv in range(2):
                for r in range(2):
                    pv = posT[:, kv, r * 16:(r + 1) * 16].unsqueeze(1).broadcast_to([P, 16, 16])
                    last = v.tensor_tensor(o3(cmp_in[:, kv, r, :], 16), o3(ps[:, 0, kv * SEQ:(kv + 1) * SEQ], 16),
                                           pv, ALU.add)
            last.then_inc(S("cmp_pos"), 1)
            dve.wait_ge(S("cmp_ps"), 1)
            dve.wait_ge(S("cmp_zero"), 1)
            for kv in range(2):
                last = v.tensor_copy(cmp_kv[0:N_CMP, kv, 0, :, :].rearrange("p g d -> p (g d)"),
                                     ps[0:N_CMP, 0, kv * 128:(kv + 1) * 128])
            last.then_inc(S("cmp_done"), 1)
            at_main.dve(dve)
            at_nsa.dve(dve)
            at_diff.dve(dve)

            at_main.wait(dve, "normed", 12)
            for i in range(2):
                last = v.tensor_copy(dnm[:, i, :, :].rearrange("p t (j h) -> p t j h", h=2),
                                     stat[:, :, 4 * i:4 * i + 4].rearrange("p j (t h) -> p t j h", t=T))
            chain(last)
            nm = [dnm[:, 0, :, 15 + 3 * g:18 + 3 * g] for g in range(3)]
            d9 = lambda i: dl[:, i, :].rearrange("p (t g h) -> p t g h", t=T, g=3)
            chain(v.tensor_tensor(d9(0)[:, :, 0, :], nm[0], nm[1], ALU.min))
            chain(v.tensor_tensor(d9(0)[:, :, 0, :], d9(0)[:, :, 0, :], nm[2], ALU.min))
            for g in range(3):
                last = v.tensor_tensor(d9(1)[:, :, g, :], d9(0)[:, :, 0, :], nm[g], ALU.subtract)
            chain(last)
            dve.sem_inc(S("dd"), 1)
            dve.wait_ge(S("dexp"), 1)
            ll = dnm[:, 1, :, 15:24]
            chain(v.tensor_tensor(dl[:, 3, :].rearrange("p (t h) -> p t h", t=T), dl[:, 2, :].rearrange(
                "p (t h) -> p t h", t=T), ll, ALU.mult))
            chain(v.tensor_tensor(d9(4)[:, :, 0, :], d9(3)[:, :, 0, :], d9(3)[:, :, 1, :], ALU.add))
            chain(v.tensor_tensor(d9(4)[:, :, 0, :], d9(4)[:, :, 0, :], d9(3)[:, :, 2, :], ALU.add))
            chain(v.reciprocal(d9(4)[:, :, 1, :], d9(4)[:, :, 0, :]))
            for g in range(3):
                last = v.tensor_tensor(d9(5)[:, :, g, :], d9(3)[:, :, g, :], d9(4)[:, :, 1, :], ALU.mult)
            chain(last)
            od = X[:, :, 960:1536].rearrange("p t (h d) -> p t h d", h=9)
            v.tensor_tensor(od, od, dl[:, 5, :].rearrange("p (t h) -> p t h", t=T).unsqueeze(3).broadcast_to(
                [P, T, 9, HD]), ALU.mult)
            dve.wait_ge(S("gates"), 1)
            at_nsa.wait(dve, "normed", 8)
            gt = lambda i: gates[:, :, :, i].unsqueeze(3).broadcast_to([P, T, NSA, HD])
            on = X[:, :, 448:960].rearrange("p t (h d) -> p t h d", h=8)
            dve.wait_ge(S("valid"), 1)
            chain(v.tensor_tensor(gates[:, 0, :, 0], gates[:, 0, :, 0], valid[:, :].broadcast_to([P, NSA]), ALU.mult))
            v.tensor_tensor(on, on, gt(1), ALU.mult)
            v.tensor_tensor(res_nsa[:, :, 0:8, :], res_nsa[:, :, 0:8, :], gt(2), ALU.mult)
            chain(v.tensor_tensor(res_nsa[:, :, 8:16, :], res_nsa[:, :, 8:16, :], gt(0), ALU.mult))
            chain(v.tensor_tensor(on, on, res_nsa[:, :, 0:8, :], ALU.add))
            chain(v.tensor_tensor(on, on, res_nsa[:, :, 8:16, :], ALU.add))
            at_diff.wait(dve, "normed", 4)
            for t in range(T):
                last = v.scalar_tensor_tensor(o3(X[:, t, 1536:2048], 4), res_diff[:, t, :, 1, :], lam[:, 5:6],
                                              res_diff[:, t, :, 0, :], ALU.mult, ALU.add)
            chain(last)
            xd = X[:, :, 1536:2048]
            chain(v.tensor_tensor(diff_tmp[:, :, :], xd, xd, ALU.mult))
            chain(v.tensor_reduce(o3(dss[:, 0, :], 2), diff_tmp[:, :, :].rearrange("p t (h d) -> p t h d", h=4), AX.X, ALU.add))
            v.tensor_scalar(dss[:, 1, :], dss[:, 0, :], 1.0 / 128, RMS_EPS, ALU.mult, ALU.add).then_inc(S("dif_ms"), 1)
            dve.wait_ge(S("dif_rinv"), 1)
            xd4 = xd.rearrange("p t (h d) -> p t h d", h=4)
            chain(v.tensor_tensor(xd4, xd4, o3(dss[:, 2, :], 2).unsqueeze(3).broadcast_to([P, T, 4, 128]), ALU.mult))
            for t in range(T):
                last = v.tensor_tensor(o3(X[:, t, 1536:2048], 4), o3(X[:, t, 1536:2048], 4),
                                       subg[:, :].unsqueeze(1).broadcast_to([P, 4, 128]), ALU.mult)
            last.then_inc(S("o1_ready"), 1)
            split_plain_lo(dve, "o1", actT)

            def gated_add(name, at_k=12, take=None, one_acc=False):
                st = ST[name]

                def f(p, j):
                    dve.wait_ge(ada_taken, 1 + (place(st, p, j).an + 1 if take else ST["gu0"].end[3]))
                    panel_done(dve, st, p, j)
                    q = p * 2 + j if len(st.panels) == 2 else j
                    for t in range(T):
                        last = v.tensor_tensor(gy[:, t, :], ps[:, bank_of(st, j) + t, :], gb0[:, ds(q * NC, NC)], ALU.mult)
                    last.then_inc(S("gy"), 1)
                    dve.wait_ge(S("gy"), 4 * ("wout", "down0", "down1", "down2").index(name) + panel_no(st, p, j) + 1)
                    for t in range(T):
                        xs = X[:, t, ds(q * NC, NC)]
                        last = v.tensor_tensor(xs, xs, gy[:, t, :], ALU.add)
                    last.then_inc(acc_read, 1)
                stage_split_lo(dve, name, {at_k: f}, take=take)
                f(st.bodies - 1, len(st.panels) - 1)
                dve.wait_ge(acc_read, 2 + st.end[2])

            dve.wait_ge(S("x_again"), 32)
            gated_add("wout", take=take_rows(ST["wout"], 2))
            moments("n2", RMS_EPS, True)
            gains(1)
            split_mod_lo(dve, "u2", actT, 1)
            dve.wait_ge(S("g2b_in"), 16)
            for i in range(3):
                st = ST[f"gu{i}"]

                def up_mul(p, j):
                    dve.wait_ge(S("sil"), 8 * i + panel_no(st, p, j) + 1)
                    for t in range(T):
                        last = v.tensor_tensor(hid[:, j, t, :], sil[:, j, t, :], ps[:, bank_of(st, j) + t, 256:512], ALU.mult)
                    last.then_inc(acc_read, 1)

                def hid_lo(p, j):
                    q = panel_no(st, p, j)
                    dve.wait_ge(S("hid_hi"), 8 * i + q + 1)
                    v.tensor_tensor(hidT[:, 1, ds(2 * q, 2), :], o3(ps[:, 4 + j, :], 2),
                                    hidT[:, 0, ds(2 * q, 2), :].bitcast(f32), ALU.subtract).then_inc(S("hid_taken"), 1)
                stage_split_lo(dve, f"gu{i}", {8: up_mul, 15: hid_lo},
                               take=take_rows(ST["gu0"], 1) if i == 0 else None, one_acc=True)
                up_mul(st.bodies - 1, 1)
                hid_lo(st.bodies - 1, 1)
                gated_add(f"down{i}", 12 if i < 2 else 8)
            moments("n3", RMS_EPS, True)
            dve.wait_ge(S("fin_in"), 16)
            dve.wait_ge(S("rinv"), NORM["n3"])
            for t in range(T):
                v.scalar_tensor_tensor(X[:, t, :], X[:, t, :], rinv_x[:, t:t + 1], gb0[:, :],
                                       ALU.mult, ALU.mult).then_inc(S("h0_ready"), 1)
            split_plain_lo(dve, "h0", actT)
            stage_split_lo(dve, "in0")
            dve.wait_ge(S("poolw_in"), 80)
            dve.wait_ge(S("gsilu0"), 1)
            for grp in range(4):
                for t in range(T):
                    n = grp * T + t
                    dve.wait_ge(S("pool_out"), n + 1)
                    v.tensor_tensor(U[:, t, grp * 384:(grp + 1) * 384], ps[:, 2 + n % 2, 0:384],
                                    gb0[:, grp * 384:(grp + 1) * 384], ALU.mult).then_inc(S("pool_mixed"), 1)

            def gate_mixed(tag):
                v.tensor_tensor(U[:, :, 0:BR], U[:, :, 0:BR], U[:, :, BR:2 * BR], ALU.mult)
                v.tensor_tensor(U[:, :, 2 * BR:2 * BR + 512], U[:, :, 2 * BR:2 * BR + 512], U[:, :, 2 * BR + 512:],
                                ALU.mult).then_inc(S(tag), 1)

            def layer_out(name, tag, ln_in, done, res_n):
                st = ST[name]

                def f(p, j):
                    panel_done(dve, st, p, j)
                    for t in range(T):
                        xs = X[:, t, ds((p * 2 + j) * NC, NC)]
                        last = v.scalar_tensor_tensor(xs, xs, ALPHA, ps[:, bank_of(st, j) + t, :], ALU.mult, ALU.add)
                    last.then_inc(acc_read, 1)
                stage_split_lo(dve, name, {12: f})
                f(st.bodies - 1, 1)
                dve.wait_ge(acc_read, 2 + st.end[2])
                moments(tag, LN_EPS, False)
                dve.wait_ge(S(ln_in), 32)
                dve.wait_ge(S("rinv"), NORM[tag])
                for t in range(T):
                    chain(v.tensor_scalar(X[:, t, :], X[:, t, :], mv[:, t, 0:1], rinv_x[:, t:t + 1],
                                          ALU.subtract, ALU.mult))
                    chain(v.tensor_tensor(X[:, t, :], X[:, t, :], gb0[:, :], ALU.mult))
                    v.tensor_tensor(X[:, t, :], X[:, t, :], gb1[:, :], ALU.add).then_inc(S(done), 1)

            at_mem[0].dve(dve)
            dve.wait_ge(S("pool_mixed"), 8)
            at_mem[0].finished(dve)
            gate_mixed("m0_ready")
            split_plain_lo(dve, "m0", actT)
            layer_out("out0", "l0", "ln0_in", "h1_ready", 0)
            split_plain_lo(dve, "h1", actT)
            stage_split_lo(dve, "kv")
            stage_split_lo(dve, "in1")
            at_moba.dve(dve)
            at_mem[1].dve(dve)
            dve.wait_ge(S("gsilu1"), 1)
            at_moba.finished(dve)
            at_mem[1].finished(dve)
            gate_mixed("m1_ready")
            split_plain_lo(dve, "m1", actT)
            layer_out("out1", "l1", "ln1_in", "y_done", 1)


_INS = ['x', 'c', 'ada_w', 'ada_b', 'norm_mix_g', 'norm_ffn_g', 'w_in', 'fox_f_bias', 'nsa_cmp_w1', 'nsa_cmp_w2',
        'nsa_cmp_pos', 'diff_lambda', 'diff_subln_g', 'w_out', 'ffn_w_gate', 'ffn_w_up', 'ffn_w_down',
        'final_norm_g', 'mem_2', 'w_in_2', 'w_out_2', 'w_mem_kv_2', 'ln_g_2', 'ln_b_2', 'pool_w_2', 'pool_scale_2',
        'w_kv_shared_2']


def kernel(**inputs):
    import numpy as _np
    import concourse.bacc as _bacc
    from concourse import mybir as _mybir
    from concourse.bass_utils import run_bass_kernel_spmd as _run

    nc = _bacc.Bacc("TRN2", target_bir_lowering=False, num_devices=1)
    arrays, args = {}, []
    for name in _INS:
        a = _np.ascontiguousarray(inputs[name])
        arrays[f"in_{name}"] = a
        args.append(nc.dram_tensor(f"in_{name}", a.shape, _mybir.dt.from_np(a.dtype), kind="ExternalInput").ap())
    y = nc.dram_tensor("out_0", (1, SEQ, D), _mybir.dt.float32, kind="ExternalOutput").ap()
    program(nc, *args, y)
    r = _run(nc, [arrays], core_ids=[0])
    return r.results[0]["out_0"]
```

```python
import numpy as np
import concourse.bass as bass
from concourse import mybir
from contextlib import ExitStack

P = 128
T = 2
SEQ = P * T
D = 2048
KD = D // P
NC = 512
HD = 64
FF = 5632
FOX, NSA, GROUPS, DIL, DIFF = 7, 8, 2, 9, 4
SPLITS = [("fox_q", FOX * HD), ("fox_k", FOX * HD), ("fox_v", FOX * HD), ("fox_f", FOX), ("nsa_q", NSA * HD),
          ("cmp_k", 128), ("cmp_v", 128), ("slc_k", 128), ("slc_v", 128), ("win_k", 128), ("win_v", 128),
          ("gate", NSA * 3), ("dil_q", DIL * HD), ("dil_k", DIL * HD), ("dil_v", DIL * HD),
          ("diff_q", 512), ("diff_k", 512), ("diff_v", 512)]
COL, _at = {}, 0
for _n, _w in SPLITS:
    COL[_n] = _at
    _at += _w
N_IN = _at
LAST_W = 288
MASKED = 1.0e30
CMP_LEN, CMP_STRIDE = 32, 16
N_CMP = SEQ // CMP_STRIDE - CMP_LEN // CMP_STRIDE + 1
LAM_INIT = 0.2
RMS_EPS, LN_EPS = 1e-6, 1e-5
ALPHA = 4 ** 0.25
BR, MEMW, HD2 = 1536, 512, 128
POOL_WINDOWS = (2, 4, 8, 16)
RING, HILO = 8, 4


def slope(h, n):
    return float(np.float32(2.0 ** (-8.0 * (h + 1) / n)))


class Stage:

    def __init__(self, name, bodies, panels):
        self.name, self.bodies, self.panels = name, bodies, panels


STAGES = [
    Stage("memkv", 2, [("wa", 16)] * 2), Stage("ada1", 2, [("a", 16)] * 2),
    Stage("win", 2, [("wa", 16)] * 3 + [("w", 16)]), Stage("win_end", 1, [("wa", 16), ("w", 16)] * 2),
    Stage("wout", 2, [("wa", 16)] * 2),
    Stage("gu0", 4, [("w", 16), ("wa", 16)]), Stage("down0", 2, [("w", 16)] * 2),
    Stage("gu1", 4, [("w", 16)] * 2), Stage("down1", 2, [("w", 16)] * 2),
    Stage("gu2", 3, [("w", 16)] * 2), Stage("down2", 1, [("w", 12)] * 4),
    Stage("in0", 4, [("w", 16)] * 2), Stage("out0", 2, [("w", 16)] * 2),
    Stage("kv", 3, [("w", 16)] * 2), Stage("in1", 4, [("w", 16)] * 2), Stage("out1", 2, [("w", 16)] * 2),
]


class Place:

    def __init__(self, kb, gb, pn, an):
        self.kb, self.gb, self.pn, self.an = kb, gb, pn, an


_kb = _gb = _pn = _an = 0
for _s in STAGES:
    _s.start = (_kb, _gb, _pn, _an)
    _s.local = []
    k = g = n = a = 0
    for _kind, _nk in _s.panels:
        _s.local.append((k, g, n, a))
        k += _nk * len(_kind)
        g += _nk * ("w" in _kind)
        n += "w" in _kind
        a += "a" in _kind
    _s.per = (k, g, n, a)
    _kb, _gb, _pn, _an = (x + y * _s.bodies for x, y in zip(_s.start, _s.per))
    _s.end = (_kb, _gb, _pn, _an)
ST = {s.name: s for s in STAGES}


def place(stage, p, j):
    return Place(*(s + l + p * q for s, l, q in zip(stage.start, stage.local[j], stage.per)))


def run_bodies(eng, stage, body):
    body(0, True)
    if stage.bodies > 1:
        with eng.Fori(1, stage.bodies) as p:
            body(p, False)


def program(nc, x, c, ada_w, ada_b, norm_mix_g, norm_ffn_g, w_in, fox_f_bias, cmp_w1, cmp_w2, cmp_pos,
            diff_lambda, diff_subln_g, w_out, w_gate, w_up, w_down, final_g, mem, w_in2, w_out2,
            w_mem_kv, ln_g, ln_b, pool_w, pool_scale, w_kv, out):
    f32, f32r, i32 = mybir.dt.float32, mybir.dt.float32r, mybir.dt.int32
    ACT, ALU, AX = mybir.ActivationFunctionType, mybir.AluOpType, mybir.AxisListType
    ds = bass.ds
    ctx = ExitStack()
    with ctx:
        arena_bytes = 212800
        arena = ctx.enter_context(nc.sbuf_tensor("arena", [P, arena_bytes // 4], f32))
        base = nc.sbuf_base
        base = (base - arena_bytes) // 32 * 32 + 32 if nc.sbuf_base > arena_bytes else (base + 31) // 32 * 32
        top = [0]

        def at(name, shape, dt, off):
            size = 4 * int(np.prod(shape[1:]))
            assert off % 32 == 0 and off + size <= arena_bytes, (name, off, size)
            return nc.alloc_sbuf_tensor_at(name, shape, dt, offset=base + off)

        def new(name, shape, dt=f32):
            off = top[0]
            top[0] += (4 * int(np.prod(shape[1:])) + 31) // 32 * 32
            return at(name, shape, dt, off)

        def region(size):
            off = top[0]
            top[0] += size
            return off

        raw = new("raw", [P, RING, 2, NC])
        r_hilo = region(2 * HILO * NC * 4)
        w_hi = at("w_hi", [P, HILO, NC], f32r, r_hilo)
        w_lo = at("w_lo", [P, HILO, NC], f32r, r_hilo + HILO * NC * 4)
        probs = at("probs", [P, 2, 2, 512], f32, r_hilo)
        probsT = at("probsT", [P, 2, 2, 512], f32, r_hilo + 8192)
        r_act = region(32768)
        actT = at("actT", [P, 2, KD, SEQ], f32r, r_act)
        res_nsa = at("res_nsa", [P, T, 16, HD], f32, r_act)
        res_diff = at("res_diff", [P, T, DIFF, 2, 128], f32, r_act + 8192)
        diff_tmp = at("diff_tmp", [P, T, 512], f32, r_act + 16384)
        pooledT = at("pooledT", [P, 12, SEQ], f32, r_act)
        poolw_s = at("poolw_s", [P, 4, 3, 384], f32, r_act + 12288)
        r_x = top[0]
        X = new("X", [P, T, D])
        memkv = new("memkv", [P, 2, T, 1024])
        r_one = region(66368)
        proj = at("proj", [P, T, N_IN], f32, r_one)
        o1 = (N_IN * T * 4 + 31) // 32 * 32
        cumk = at("cumk", [P, FOX, SEQ], f32, r_one + o1)
        dist = at("dist", [P, 5, 384], f32, r_one + o1 + 7168)
        cmp_kv = at("cmp_kv", [P, 2, T, 2, HD], f32, r_one + o1 + 14848)
        upper = at("upper", [P, T, SEQ], f32, r_one + o1 + 16896)
        assert o1 + 16896 + 2048 <= 66368
        hidT = at("hidT", [P, 2, KD, SEQ], f32r, r_one)
        xn2 = at("xn2", [P, T, D], f32, r_one + 32768)
        hid = at("hid", [P, 2, T, 256], f32, r_one + 49152)
        sil = at("sil", [P, 2, T, 256], f32, r_one + 53248)
        U = at("U", [P, T, 4096], f32, r_one)
        KV = at("KV", [P, T, 3072], f32, r_one + 32768)
        band = at("band", [P, 4, T, SEQ], f32, r_one + 57344)
        r_stg = region(20480)
        gb0 = at("gb0", [P, D], f32, r_stg)
        gb1 = at("gb1", [P, D], f32, r_stg + 8192)
        ada_acc = at("ada_acc", [P, 2, NC], f32, r_stg + 16384)
        w1_s = at("w1_s", [P, 2, CMP_LEN, HD], f32, r_stg)
        qk_s = at("qk_s", [P, 2, 2, T, 128], f32, r_stg)
        v_s = at("v_s", [P, 2, T, 128], f32, r_stg + 4096)
        tab_s = at("tab_s", [P, 2, 2, 384], f32, r_stg + 6144)
        qkT_s = at("qkT_s", [P, 2, 2, SEQ], f32, r_stg + 12288)
        qk2_s = at("qk2_s", [P, 2, 2, T, 256], f32, r_stg)
        v2_s = at("v2_s", [P, 2, T, 256], f32, r_stg + 8192)
        qkT2_s = at("qkT2_s", [P, 2, 2, 2, SEQ], f32, r_stg + 12288)
        ident = new("ident", [P, P])
        ones = new("ones", [P, P])
        rows = new("rows", [P, 2, P])
        pos_r = new("pos_r", [CMP_LEN, 2, 2, HD])
        cols = new("cols", [P, P])
        cols2 = new("cols2", [P, 3 * KD])
        c_col = new("c_col", [P, KD])
        c_raw = new("c_raw", [P, KD])
        posT = new("posT", [P, 2, CMP_LEN])
        modT = new("modT", [P, 4 * KD])
        gain = new("gain", [P, 2, KD])
        cmask = new("cmask", [P, 384])
        stats = new("stats", [P, T, 4, 6])
        mv = new("mv", [P, T, 2])
        ms = new("ms", [P, T])
        rinv_x = new("rinv_x", [P, T])
        nmean = new("nmean", [P, T])
        mhalf = new("mhalf", [P, 8])
        sm = new("sm", [P, 2, 8])
        mx = new("mx", [P, 2, 4])
        mx_zero = new("mx_zero", [P, 2, 2])
        rs = new("rs", [P, 2, 4])
        stat = new("stat", [P, 12, 8])
        fox_b = new("fox_b", [P, FOX])
        fz = new("fz", [P, 8, T, FOX])
        logf = new("logf", [P, T, FOX])
        cumq = new("cumq", [P, T, FOX])
        gates = new("gates", [P, T, NSA, 3])
        lamv = new("lamv", [P, 4, HD])
        lam = new("lam", [P, 8])
        subg = new("subg", [P, 128])
        dl = new("dl", [P, 6, T * 9])
        dnm = new("dnm", [P, 2, T, 24])
        dss = new("dss", [P, 3, 8])
        cmp_in = at("cmp_in", [P, 2, 2, SEQ], f32, r_x)
        cmp_h = new("cmp_h", [HD, 2, 2, 16])
        w2_s = new("w2_s", [HD, 2, HD])
        evac = at("evac", [P, 2, 512], f32, r_one + 49152)
        valid = new("valid", [P, 1])
        rec = new("rec", [P, 16])
        gy = at("gy", [P, T, NC], f32, r_stg + 8192)
        ps = ctx.enter_context(nc.psum_tensor("ps", [P, 8, 512], f32))

        def o3(ap, a):
            return ap.rearrange("p (a b) -> p a b", a=a)

        sems = {}

        def S(name):
            if name not in sems:
                sems[name] = ctx.enter_context(nc.semaphore(name))
            return sems[name]

        w_loaded = [S(f"w_loaded{i}") for i in range(RING)]
        blocks_read = S("blocks_read")
        hi_ready = S("hi_ready")
        parts_used = S("parts_used")
        acc_read = S("acc_read")
        ada_summed = S("ada_summed")
        ada_taken = S("ada_taken")

        def chunks(stage, j):
            kind, nk = stage.panels[j]
            off = 0
            for ch in range(nk // 2):
                for k in kind:
                    yield k, ch, off
                    off += 2

        def stage_loads(sp, name, w_src, a_src=None, width=NC):
            st = ST[name]

            def body(p, first):
                for j in range(len(st.panels)):
                    pl = place(st, p, j)
                    for kind, ch, off in chunks(st, j):
                        slot = ((st.start[0] + st.local[j][0] + off) // 2) % RING
                        sp.wait_ge(blocks_read, pl.kb + off + 2)
                        if kind == "w":
                            for dst, src in w_src(p, j, ch):
                                sp.dma_start(raw[:, slot, :, dst[0]:dst[1]], src).then_inc(w_loaded[slot], 16)
                        else:
                            sp.dma_start(raw[:, slot, :, :], a_src(p, j, ch)).then_inc(w_loaded[slot], 16)
            run_bodies(sp, st, body)

        loads_before = []
        n = [0] * RING
        for st in STAGES:
            st.slot_start = list(n)
            st.slot_local = []
            cnt = [0] * RING
            for j in range(len(st.panels)):
                row = []
                for kind, ch, off in chunks(st, j):
                    s = ((st.start[0] + st.local[j][0] + off) // 2) % RING
                    cnt[s] += 32 if st.name.startswith("gu") and kind == "w" else 16
                    row.append((s, cnt[s]))
                st.slot_local.append(row)
            st.slot_per = cnt
            n = [a + b * st.bodies for a, b in zip(n, cnt)]

        def wait_chunk(eng, st, p, j, idx):
            s, local = st.slot_local[j][idx]
            eng.wait_ge(w_loaded[s], st.slot_start[s] + local + p * st.slot_per[s])

        def beside(work):
            ks = {k for _, k in work}
            return {k: (lambda p, j, k=k: work[j + 1, k]() if (j + 1, k) in work else None) for k in ks}

        def stage_split_hi(act, name, hooks=None, width=None, lead=None):
            st = ST[name]

            def body(p, first):
                for j in range(len(st.panels)):
                    if "w" not in st.panels[j][0]:
                        continue
                    pl = place(st, p, j)
                    w = width[j] if width else NC
                    for idx, (kind, ch, off) in enumerate(chunks(st, j)):
                        if kind != "w":
                            continue
                        for b in range(2):
                            k = 2 * ch + b
                            if hooks and k in hooks and not (first and j == 0):
                                hooks[k](*((p, j - 1) if j else (p - 1, len(st.panels) - 1)))
                            if lead and k in lead and first and j == 0:
                                lead[k]()
                            if b == 0:
                                wait_chunk(act, st, p, j, idx)
                            slot = ((st.start[0] + st.local[j][0] + off) // 2) % RING
                            act.wait_ge(parts_used, pl.gb + k + 1)
                            g = (st.local[j][1] + k) % HILO
                            act.activation(w_hi[:, g, 0:w], raw[:, slot, b, 0:w], ACT.Copy).then_inc(hi_ready, 1)
            run_bodies(act, st, body)

        def stage_split_lo(dve, name, hooks=None, width=None, take=None, one_acc=False, lead=None):
            st = ST[name]
            kinds = [k for k, _ in st.panels]

            def before(p, j):
                return (p, j - 1) if j else (p - 1, len(st.panels) - 1)

            def body(p, first):
                na = 0
                for j in range(len(st.panels)):
                    pl = place(st, p, j)
                    w = width[j] if width else NC
                    alone = first and j == 0
                    for idx, (kind, ch, off) in enumerate(chunks(st, j)):
                        slot = ((st.start[0] + st.local[j][0] + off) // 2) % RING
                        for b in range(2):
                            k = 2 * ch + b
                            if not alone and kind == kinds[j][0]:
                                if k == 12 and take and "a" in kinds[before(0, j)[1]]:
                                    take(*before(p, j))
                                if hooks and k in hooks:
                                    hooks[k](*before(p, j))
                            if alone and lead and k in lead and kind == kinds[j][0]:
                                lead[k]()
                            if kind == "w":
                                dve.wait_ge(hi_ready, pl.gb + k + 1)
                                g = (st.local[j][1] + k) % HILO
                                nc.vector.tensor_tensor(w_lo[:, g, 0:w], raw[:, slot, b, 0:w],
                                                        w_hi[:, g, 0:w].bitcast(f32),
                                                        ALU.subtract).then_inc(blocks_read, 1)
                            else:
                                acc = ada_acc[:, 0 if one_acc else na % 2, :]
                                if k == 0:
                                    wait_chunk(dve, st, p, j, idx)
                                    nc.vector.tensor_scalar(acc, raw[:, slot, b, :], c_col[:, 0:1], None,
                                                            ALU.mult).then_inc(blocks_read, 1)
                                else:
                                    if b == 0:
                                        wait_chunk(dve, st, p, j, idx)
                                    dve.wait_ge(blocks_read, 2 * RING + pl.kb + off + b - (1 if b else
                                                1 + 2 * (len(kinds[j]) - 1)) + 1)
                                    nc.vector.scalar_tensor_tensor(acc, raw[:, slot, b, :], c_col[:, k:k + 1], acc,
                                                                   ALU.mult, ALU.add).then_inc(blocks_read, 1)
                    na += "a" in kinds[j]
            run_bodies(dve, st, body)
            if take and "a" in kinds[-1]:
                take(st.bodies - 1, len(st.panels) - 1)

        def ada_sum(pe, st, p, j, na, as_columns, one_acc=False):
            pl = place(st, p, j)
            acc = ada_acc[:, 0 if one_acc else na % 2, :]
            kind, nk = st.panels[j]
            pe.wait_ge(blocks_read, 2 * RING + pl.kb + nk * len(kind))
            pe.wait_ge(ada_taken, pl.an + 1)
            if as_columns:
                for i in range(4):
                    last = nc.tensor.matmul(ps[:, 6, i:i + 1], acc[:, i * P:(i + 1) * P], ones[:, 0:1],
                                            start=True, stop=True)
            else:
                last = nc.tensor.matmul(ps[:, 6, :], ones[:, :], acc, start=True, stop=True)
            last.then_inc(ada_summed, 1)

        def stage_matmuls(pe, name, lhs, hooks=None, width=None, as_columns=False, one_acc=False, lead=None):
            st = ST[name]
            kinds = [k for k, _ in st.panels]

            def body(p, first):
                na = 0
                for j, (kind, nk) in enumerate(st.panels):
                    pl = place(st, p, j)
                    w = width[j] if width else NC
                    pj = (p, j - 1) if j else (p - 1, len(st.panels) - 1)
                    pa = [sum("a" in q for q in kinds[:pj[1]])][0]
                    if kind == "a":
                        ada_sum(pe, st, p, j, na, as_columns)
                        na += 1
                        continue
                    pe.wait_ge(acc_read, pl.pn + 1)
                    bank = 2 * ((st.start[2] + st.local[j][2]) % 2)
                    for idx, (kd, ch, off) in enumerate(chunks(st, j)):
                        if kd != "w":
                            continue
                        for b in range(2):
                            k = 2 * ch + b
                            if not (first and j == 0):
                                if k == 8 and "a" in kinds[pj[1]]:
                                    ada_sum(pe, st, pj[0], pj[1], pa, as_columns, one_acc)
                                if hooks and k in hooks:
                                    hooks[k](*pj)
                            elif lead and k in lead:
                                lead[k]()
                            pe.wait_ge(blocks_read, 2 * RING + pl.kb + off + b + 1)
                            g = (st.local[j][1] + k) % HILO
                            for t in range(T):
                                hi, lo = (lhs[:, part, k, t * P:(t + 1) * P] for part in range(2))
                                o = ps[:, bank + t, 0:w]
                                nc.tensor.matmul(o, hi, w_hi[:, g, 0:w], start=(k == 0), stop=False)
                                nc.tensor.matmul(o, hi, w_lo[:, g, 0:w], start=False, stop=False)
                                last = nc.tensor.matmul(o, lo, w_hi[:, g, 0:w], start=False, stop=(k == nk - 1))
                            last.then_inc(parts_used, 1)
            run_bodies(pe, st, body)
            if kinds[-1] == "wa":
                ada_sum(pe, st, st.bodies - 1, len(kinds) - 1, sum("a" in q for q in kinds[:-1]), as_columns, one_acc)

        def panel_done(eng, st, p, j):
            pl = place(st, p, j)
            eng.wait_ge(parts_used, HILO + pl.gb + st.panels[j][1])

        def bank_of(st, j):
            return 2 * ((st.start[2] + st.local[j][2]) % 2)

        def panel_no(st, p, j):
            return p * len(st.panels) + j

        def ada_no(st, p, j):
            return p * st.per[3] + st.local[j][3]

        TURNS = {tag: 8 * i for i, tag in enumerate(("mem", "u1", "o1", "u2", "h0", "m0", "h1", "m1"))}
        MODS = {"u1": 0, "u2": 8, "h0": 16, "h1": 24}
        turned = S("turned")
        turn_mod = S("turn_mod")
        turn_hi = S("turn_hi")
        turn_taken = S("turn_taken")

        def turning(pe, tag, src, ready):
            def turn(g):
                ready(g)
                for i in range(4):
                    k, t = 2 * g + i // 2, i % 2
                    last = nc.tensor.transpose(ps[:, 4 + g % 4, i * P:(i + 1) * P], src(k, t), ident[:, :])
                last.then_inc(turned, 1)

            def before(g):
                if 1 <= g <= 4:
                    turn(g + 3)
                pe.wait_ge(turn_taken, TURNS[tag] + g + 1)
            for g in range(4):
                turn(g)
            return {2 * g: (lambda g=g: before(g)) for g in range(8)}

        def in_lead(first, later):
            lead = {2 * g: (lambda g=g: later(g)) for g in range(3, 8)}
            lead[4] = first
            return lead

        def split_plain_hi(act, tag, dst):
            def high(g):
                act.wait_ge(turned, TURNS[tag] + g + 1)
                act.activation(dst[:, 0, 2 * g:2 * g + 2, :], o3(ps[:, 4 + g % 4, :], 2),
                               ACT.Copy).then_inc(turn_hi, 1)
            return in_lead(lambda: [high(g) for g in range(3)], high)

        def split_plain_lo(dve, tag, dst, between=None):
            def low(g):
                if between and g in between:
                    between[g]()
                dve.wait_ge(turn_hi, TURNS[tag] + g + 1)
                nc.vector.tensor_tensor(dst[:, 1, 2 * g:2 * g + 2, :], o3(ps[:, 4 + g % 4, :], 2),
                                        dst[:, 0, 2 * g:2 * g + 2, :].bitcast(f32),
                                        ALU.subtract).then_inc(turn_taken, 1)
            return in_lead(lambda: [low(g) for g in range(3)], low)

        def split_mod_hi(act, tag, dst, quarter=None):
            def high(g):
                if quarter and g == 3:
                    quarter(3)
                act.wait_ge(turn_mod, MODS[tag] + g + 1)
                act.activation(dst[:, 0, 2 * g:2 * g + 2, :], o3(evac[:, g % 2, :], 2),
                               ACT.Copy).then_inc(turn_hi, 1)

            def first():
                if quarter:
                    quarter(0)
                    quarter(1)
                high(0)
                high(1)
                if quarter:
                    quarter(2)
                high(2)
            return in_lead(first, high)

        def split_mod_lo(dve, tag, dst, gain_of, shift_of):
            def mod(g):
                if g >= 2:
                    dve.wait_ge(turn_taken, TURNS[tag] + g - 1)
                dve.wait_ge(turned, TURNS[tag] + g + 1)
                for i in range(2):
                    k = 2 * g + i
                    args = (evac[:, g % 2, i * SEQ:(i + 1) * SEQ], ps[:, 4 + g % 4, i * SEQ:(i + 1) * SEQ], gain_of(k))
                    if shift_of:
                        last = nc.vector.tensor_scalar(*args, shift_of(k), ALU.mult, ALU.add)
                    else:
                        last = nc.vector.tensor_scalar(*args, None, ALU.mult)
                last.then_inc(turn_mod, 1)

            def low(g):
                dve.wait_ge(turn_hi, TURNS[tag] + g + 1)
                nc.vector.tensor_tensor(dst[:, 1, 2 * g:2 * g + 2, :], o3(evac[:, g % 2, :], 2),
                                        dst[:, 0, 2 * g:2 * g + 2, :].bitcast(f32),
                                        ALU.subtract).then_inc(turn_taken, 1)

            def first():
                mod(0)
                mod(1)
                low(0)
                mod(2)
                low(1)

            def later(g):
                mod(g)
                low(g - 1)
            lead = in_lead(first, later)
            lead[15] = lambda: low(7)
            return lead

        class Attn:

            def __init__(self, tag, pairs, dh, dv, full, table, scale, dest, keep=False):
                self.tag, self.pairs, self.dh, self.dv, self.full = tag, pairs, dh, dv, full
                self.table, self.scale, self.dest, self.keep = table, scale, dest, keep
                self.start = Attn.started
                Attn.started += pairs
                self.kw = 512 if full else 384

            PER = {"exp": 2, "scores": 2, "p_tr": 2}
            started = 0

            def s(self, name):
                return S("at_" + name)

            def wait(self, eng, name, value):
                eng.wait_ge(self.s(name), self.start * self.PER.get(name, 1) + value)

            def staged(self, eng, what, i_par, half):
                n = 64 if what == "qk" else 32
                eng.wait_ge(S(f"at_{what}{i_par}"), n * (self.start // 2) + n * half + n)

            def spans(self):
                return [(0, 0, 256 if self.full else 128), (1, self.kw - 256, 256)]

            def steps(self, eng, step, first):
                first()
                n = self.pairs
                if n > 4:
                    with eng.Fori(0, n // 2 - 2) as p:
                        step(2 * p, 0, p, 3)
                        step(2 * p + 1, 1, p, 3)
                for i in range(max(n - 4, 0), n):
                    step(i, i % 2, i // 2, n - 1 - i)

            def q_src(self, par, kind, head, t):
                if self.dh == HD:
                    return qk_s[:, par, kind, t, :]
                return qk2_s[:, par, kind, t, head * 128:(head + 1) * 128]

            def qT(self, par, head, kind):
                if self.dh == HD:
                    return qkT_s[head * HD:(head + 1) * HD, par, kind, :]
                return qkT2_s[:, par, head, kind, :]

            def v(self, par, head, kt):
                if self.dh == HD:
                    return v_s[:, par, kt, :] if self.dv == 128 else v_s[:, par, kt, head * HD:(head + 1) * HD]
                return v2_s[:, par, kt, head * 128:(head + 1) * 128]

            def pe(self, pe):
                nq = 1 if self.dh == HD else 2

                def turn(i, par, p):
                    self.staged(pe, "qk", par, p)
                    for b in range(nq):
                        for kind in range(2):
                            for t in range(T):
                                last = nc.tensor.transpose(ps[:, b, (kind * T + t) * P:(kind * T + t + 1) * P],
                                                           self.q_src(par, kind, b, t), ident[:, :])
                    last.then_inc(self.s("qk_tr"), 1)

                def scores(i, par, wait_read):
                    self.wait(pe, "qkT", i + 1)
                    if wait_read:
                        if self.table:
                            self.wait(pe, "max", i)
                        else:
                            self.wait(pe, "exp", 2 * i)
                    for h in range(2):
                        q, k = self.qT(par, h, 0), self.qT(par, h, 1)
                        for t, c0, nk in self.spans():
                            last = nc.tensor.matmul(ps[:, 2 + h, c0:c0 + nk], q[:, t * P:(t + 1) * P], k[:, 0:nk],
                                                    start=True, stop=True)
                        last.then_inc(self.s("scores"), 1)

                def step(i, par, p, more):
                    if more:
                        scores(i + 1, 1 - par, True)
                    if more > 1:
                        turn(i + 2, par, p + 1)
                    for h in range(2):
                        self.wait(pe, "exp", 2 * i + h + 1)
                        if h == 1:
                            self.wait(pe, "pT1", i + 1)
                        for t, c0, nk in self.spans():
                            for kt in range(nk // P):
                                d = self.pT_col(kt, t)
                                last = nc.tensor.transpose(ps[:, 4 + h, d:d + P],
                                                           probs[:, par, h, c0 + kt * P:c0 + (kt + 1) * P], ident[:, :])
                        last.then_inc(self.s("p_tr"), 1)
                    self.staged(pe, "v", par, p)
                    for h in range(2):
                        self.wait(pe, "pT0", i + 1) if h == 0 else self.wait(pe, "pT1", i + 2)
                        for t, c0, nk in self.spans():
                            o = ps[:, 6 + par, (t * 2 + h) * self.dv:(t * 2 + h + 1) * self.dv]
                            for kt in range(nk // P):
                                d = self.pT_col(kt, t)
                                last = nc.tensor.matmul(o, probsT[:, par, h, d:d + P], self.v(par, h, kt),
                                                        start=(kt == 0), stop=(kt == nk // P - 1))
                    last.then_inc(self.s("pv"), 1)

                def first():
                    turn(0, 0, 0)
                    scores(0, 0, False)
                    turn(1, 1, 0)
                self.steps(pe, step, first)

            def pT_col(self, kt, t):
                return (kt * T + t) * P if self.full or kt == 0 else 256

            def act(self, act, merge=None):
                def early(i, par):
                    self.wait(act, "qk_tr", i + 1)
                    if self.dh == HD:
                        act.activation(qkT_s[:, par, :, :], o3(ps[:, 0, :], 2), ACT.Copy).then_inc(self.s("qkT"), 1)
                    else:
                        act.activation(qkT2_s[:, par, :, :, :].rearrange("p a b c -> p (a b c)"),
                                       ps[:, 0:2, :].rearrange("p a b -> p (a b)"), ACT.Copy).then_inc(self.s("qkT"), 1)

                def late(i, par):
                    self.wait(act, "max", i + 1)
                    for h in range(2):
                        for t, c0, nk in self.spans():
                            src = (probs[:, par, h, c0:c0 + nk] if self.table else ps[:, 2 + h, c0:c0 + nk])
                            q = t * 2 + h
                            last = act.activation(probs[:, par, h, c0:c0 + nk], src, ACT.Exp, bias=sm[:, par, q:q + 1],
                                                  scale=self.scale, accum_out=sm[:, par, 4 + q:5 + q])
                        last.then_inc(self.s("exp"), 1)

                def step(i, par, p, more):
                    if more > 1:
                        early(i + 2, par)
                    self.wait(act, "p_tr", 2 * i + 1)
                    act.activation(probsT[:, par, 0, 0:self.kw], ps[:, 4, 0:self.kw],
                                   ACT.Copy).then_inc(self.s("pT0"), 1)
                    if more:
                        late(i + 1, 1 - par)
                    if merge:
                        merge(i)

                def first():
                    early(0, 0)
                    early(1, 1)
                    late(0, 0)
                self.steps(act, step, first)

            def dve(self, dve, merge=None):
                def late(i, par):
                    if self.table == "staged":
                        self.wait(dve, "tab", i + 1)
                    for h in range(2):
                        self.wait(dve, "scores", 2 * i + h + 1)
                        if self.table:
                            nc.vector.memset(mx_zero[:, par, h:h + 1], 0.0)
                            for t, c0, nk in self.spans():
                                q = t * 2 + h
                                tab = tab_s[:, par, h, c0:c0 + nk] if self.table == "staged" else cmask[:, c0:c0 + nk]
                                last = nc.vector.tensor_tensor_reduce(
                                    out=probs[:, par, h, c0:c0 + nk], in0=ps[:, 2 + h, c0:c0 + nk], in1=tab,
                                    scale=1.0, scalar=-3.0e38, op0=ALU.add, op1=ALU.max,
                                    accum_out=mx[:, par, q:q + 1])
                        else:
                            last = nc.vector.tensor_reduce(mx[:, par, h:h + 3:2], o3(ps[:, 2 + h, :], 2), AX.X, ALU.max)
                    last.then_inc(self.s("raw_max"), 1)
                    self.wait(dve, "raw_max", i + 1)
                    nc.vector.tensor_scalar(sm[:, par, 0:4], mx[:, par, :], -self.scale, None,
                                            ALU.mult).then_inc(self.s("max"), 1)

                def step(i, par, p, more):
                    if more:
                        late(i + 1, 1 - par)
                    self.wait(dve, "p_tr", 2 * i + 2)
                    nc.vector.tensor_copy(probsT[:, par, 1, 0:self.kw], ps[:, 5, 0:self.kw]).then_inc(self.s("pT1"), 1)
                    if self.keep:
                        nc.vector.tensor_copy(stat[:, ds(i, 1), :], sm[:, par:par + 1, :])
                    nc.vector.reciprocal(rs[:, par, :], sm[:, par, 4:8]).then_inc(self.s("rs"), 1)
                    self.wait(dve, "rs", i + 1)
                    self.wait(dve, "pv", i + 1)
                    o = ps[:, 6 + par, 0:4 * self.dv].rearrange("p (t h d) -> p t h d", t=T, h=2)
                    r = rs[:, par, :].rearrange("p (t h) -> p t h", t=T).unsqueeze(3).broadcast_to([P, T, 2, self.dv])
                    nc.vector.tensor_tensor(self.dest(i), o, r, ALU.mult).then_inc(self.s("normed"), 1)
                    if merge:
                        merge(i)

                self.steps(dve, step, lambda: late(0, 0))

            def gather(self, sp, source, late=None):
                wide = self.dh == HD2

                def move(i, kinds, sem):
                    for kind in kinds:
                        src = source(i, kind)
                        for t in range(T):
                            qkv = (qk2_s, v2_s) if wide else (qk_s, v_s)
                            dst = qkv[1][:, i % 2, t, :] if kind == 2 else qkv[0][:, i % 2, kind, t, :]
                            if len(src.shape) == 4:
                                dst = dst.rearrange("p (h d) -> p h d", h=2)
                            sp.dma_start(dst, src[:, t]).then_inc(sem, 16)

                for i in range(self.pairs + 2):
                    if i == 4 and late:
                        sp.wait_ge(S(late[0]), late[1])
                    if i >= 2:
                        if i >= 4:
                            self.wait(sp, "pv", i - 3)
                        move(i - 2, (2,), S(f"at_v{i % 2}"))
                    if i < self.pairs:
                        if i >= 2:
                            self.wait(sp, "qk_tr", i - 1)
                        move(i, (0, 1), S(f"at_qk{i % 2}"))

            def tables(self, pool, build):
                for i in range(self.pairs):
                    if i >= 2:
                        self.wait(pool, "max", i - 1)
                    build(i, i % 2).then_inc(self.s("tab"), 1)

            def finished(self, eng):
                self.wait(eng, "normed", self.pairs)

        SC = HD ** -0.5
        heads = []
        for h in range(FOX):
            heads.append((COL["fox_q"] + h * HD, COL["fox_k"] + h * HD, COL["fox_v"] + h * HD, ("fox", h)))
        for h in range(NSA):
            g = h // (NSA // GROUPS) * HD
            heads.append((COL["nsa_q"] + h * HD, COL["slc_k"] + g, COL["slc_v"] + g, (0, slope(h, NSA))))
        for h in range(DIL):
            heads.append((COL["dil_q"] + h * HD, COL["dil_k"] + h * HD, COL["dil_v"] + h * HD,
                          (1 + h // 3, slope(h, DIL))))
        for h in range(NSA):
            g = h // (NSA // GROUPS) * HD
            heads.append((COL["nsa_q"] + h * HD, COL["win_k"] + g, COL["win_v"] + g, (0, slope(h, NSA))))
        for h in range(NSA):
            heads.append((COL["nsa_q"] + h * HD, ("cmp", h // 4), ("cmp", h // 4), (4, slope(h, NSA))))

        at_main = Attn("main", 12, HD, HD, False, "staged", SC,
                       lambda i: X[:, :, ds(i * 128, 128)].rearrange("p t (h d) -> p t h d", h=2), keep=True)
        at_nsa = Attn("nsa", 8, HD, HD, False, "staged", SC, lambda i: res_nsa[:, :, ds(i * 2, 2), :])
        at_diff = Attn("diff", 4, HD, 128, False, "staged", SC,
                       lambda i: res_diff[:, :, ds(i, 1), :, :].rearrange("p t a m d -> p t (a m) d"))
        SC2 = HD2 ** -0.5

        def mem_attn(tag):
            return Attn(tag, 2, HD2, HD2, True, None, SC2,
                        lambda i: U[:, :, ds(2 * BR + i * 256, 256)].rearrange("p t (h d) -> p t h d", h=2))
        at_mem = [mem_attn("mem0")]
        at_moba = Attn("moba", 6, HD2, HD2, False, "mask", SC2,
                       lambda i: U[:, :, ds(i * 256, 256)].rearrange("p t (h d) -> p t h d", h=2))
        at_mem.append(mem_attn("mem1"))

        def bcast(row, n):
            return row.rearrange("(a n) -> a n", a=1).broadcast_to([P, n])

        NORM = {"n1": 1, "n2": 2, "n3": 3, "l0": 4, "l1": 5}
        XN = {"u1": 0, "u2": 4, "h0": 8, "h1": 12}

        def quarter_ready(tag):
            return lambda g: nc.tensor.wait_ge(S("xn"), XN[tag] + g // 2 + 1)

        def x_block(k, t):
            return X[:, t, k * P:(k + 1) * P]

        block = ctx.enter_context(nc.Block())

        @block.sync
        def _(sp):
            def blocks2(w, row0, ch, c0, n):
                r = row0 + ch * 256
                return w[ds(r, 256), :].rearrange("(b p) n -> p b n", p=P)[:, :, ds(c0, n)]

            def pair64(first):
                def source(i, what):
                    a, b = (h[what] for h in heads[first + 2 * i:first + 2 * i + 2])
                    if isinstance(a, tuple):
                        return cmp_kv[:, what - 1, :, a[1], :].unsqueeze(2).broadcast_to([P, T, 2, HD])
                    if a == b:
                        return proj[:, :, a:a + HD].unsqueeze(2).broadcast_to([P, T, 2, HD])
                    if b == a + HD:
                        return proj[:, :, a:a + 2 * HD]
                    return proj[:, :, a:2 * b - a].rearrange("p t (h s) -> p t h s", h=2)[:, :, :, 0:HD]
                return source

            def pair_diff(i, what):
                c0 = COL[("diff_q", "diff_k", "diff_v")[what]] + i * 128
                return proj[:, :, c0:c0 + 128]

            def pair_mem(layer):
                def source(i, what):
                    if what == 0:
                        return U[:, :, 2 * BR + i * 256:2 * BR + (i + 1) * 256]
                    c0 = (what - 1) * MEMW + i * 256
                    return memkv[:, layer, :, c0:c0 + 256]
                return source

            def pair_moba(i, what):
                src = U if what == 0 else KV
                c0 = i * 256 + (BR if what == 2 else 0)
                return src[:, :, c0:c0 + 256]

            def panels(w, row0=0, per=2):
                return lambda p, j, ch: [((0, NC), blocks2(w, row0, ch, p * per * NC + j * NC, NC))]

            ADA = {"memkv": 0, "ada1": D, "win": 3 * D, "win_end": 3 * D + 6 * NC, "wout": 2 * D, "gu0": 5 * D}

            def ada(name):
                return lambda p, j, ch: blocks2(ada_w[0], 0, ch, ADA[name] + ada_no(ST[name], p, j) * NC, NC)

            def gate_up(first):
                def src(p, j, ch):
                    c0 = first * P + (p * 2 + j) * 256
                    return [((0, 256), blocks2(w_gate[0], 0, ch, c0, 256)), ((256, 512), blocks2(w_up[0], 0, ch, c0, 256))]
                return src

            sp.dma_start(X[:, :, :], mem[0].rearrange("(t p) n -> p t n", p=P)).then_inc(S("mem_in"), 16)
            stage_loads(sp, "memkv", lambda p, j, ch: [((0, NC), w_mem_kv[ds(p, 1), :, :].rearrange("a k n -> (a k) n")[
                ch * 256:(ch + 1) * 256, j * NC:(j + 1) * NC].rearrange("(b p) n -> p b n", p=P))], ada("memkv"))
            stage_loads(sp, "ada1", None, ada("ada1"))
            stage_loads(sp, "win", panels(w_in[0], per=4), ada("win"))

            def win_end(p, j, ch):
                c0, n = (8 * NC + j * NC, NC) if j < 3 else (N_IN - LAST_W, LAST_W)
                return [((0, n), blocks2(w_in[0], 0, ch, c0, n))]
            stage_loads(sp, "win_end", win_end, ada("win_end"))
            sp.wait_ge(acc_read, 2 + ST["win"].end[2])
            sp.wait_ge(S("cmp_h_ps"), 1)
            at_main.gather(sp, pair64(0), late=("proj_done", 1))
            at_main.wait(sp, "pv", 12)
            at_nsa.gather(sp, pair64(24))
            at_nsa.wait(sp, "pv", 8)
            at_diff.gather(sp, pair_diff)
            stage_loads(sp, "wout", panels(w_out[0]), ada("wout"))
            stage_loads(sp, "gu0", gate_up(0), ada("gu0"))
            stage_loads(sp, "down0", panels(w_down[0], 0))
            stage_loads(sp, "gu1", gate_up(16))
            stage_loads(sp, "down1", panels(w_down[0], 2048))
            stage_loads(sp, "gu2", gate_up(32))
            stage_loads(sp, "down2", panels(w_down[0], 4096))
            stage_loads(sp, "in0", panels(w_in2[0]))
            sp.wait_ge(S("pool_mixed"), 8)
            at_mem[0].gather(sp, pair_mem(0))
            stage_loads(sp, "out0", panels(w_out2[0]))
            stage_loads(sp, "kv", panels(w_kv))
            stage_loads(sp, "in1", panels(w_in2[1]))
            sp.wait_ge(S("u1l_done"), 1)
            sp.wait_ge(S("natural"), 2 * T)
            at_moba.gather(sp, pair_moba)
            at_moba.wait(sp, "pv", 6)
            at_mem[1].gather(sp, pair_mem(1))
            stage_loads(sp, "out1", panels(w_out2[1]))
            for half in range(2):
                cs = slice(half * D // 2, (half + 1) * D // 2)
                for t in range(T):
                    sp.wait_ge(S("y_done"), 2 * half + t + 1)
                    sp.dma_start(out[0, t * P:(t + 1) * P, cs], X[:, t, cs]).then_inc(S("stored"), 16)
            sp.wait_ge(S("stored"), 16 * 2 * T)

        @block.gpsimd
        def _(pool):
            g = nc.gpsimd
            cn = [0]

            def chain(ins):
                cn[0] += 1
                ins.then_inc(S("pool_chain"), 1)
                pool.wait_ge(S("pool_chain"), cn[0])

            pool.dma_start(rows[0:96, 0, :], ada_b[0].rearrange("(r n) -> r n", n=P)).then_inc(S("rows_in"), 16)
            pool.dma_start(rows[96:112, 0, :], norm_mix_g[0].rearrange("(r n) -> r n", n=P)).then_inc(S("rows_in"), 16)
            pool.dma_start(rows[112:128, 0, :], norm_ffn_g[0].rearrange("(r n) -> r n", n=P)).then_inc(S("rows_in"), 16)
            pool.dma_start(rows[0:KD, 1, :], c[0].rearrange("(r n) -> r n", n=P)).then_inc(S("rows_in"), 16)
            for i, row in enumerate((final_g, ln_g[0], ln_b[0])):
                pool.dma_start(rows[(i + 1) * KD:(i + 2) * KD, 1, :], row.rearrange("(r n) -> r n", n=P)
                               ).then_inc(S("rows_in"), 16)
            chain(g.memset(ident[:, :], 0.0))
            g.affine_select(out=ident[:, :], in_=ident[:, :], compare_op=ALU.not_equal, fill=1.0, base=0,
                            pattern=[[-1, P]], channel_multiplier=1).then_inc(S("ident"), 1)
            g.memset(ones[:, :], 1.0).then_inc(S("ones"), 1)
            g.memset(mhalf[:, :], -0.5)
            for half in range(2):
                for kv in range(2):
                    pool.dma_start(pos_r[:, kv, half, :], cmp_pos[0, kv]).then_inc(S("cmp_in"), 16)
                    pool.dma_start(w1_s[half * HD:(half + 1) * HD, kv, :, :],
                                   cmp_w1[0, kv].rearrange("(j d) f -> d j f", d=HD)).then_inc(S("cmp_in"), 16)
            pool.dma_start(w2_s[:, :, :], cmp_w2[0].rearrange("a d f -> d a f")).then_inc(S("cmp_in"), 16)
            pool.dma_start(fox_b[:, :], bcast(fox_f_bias[0], FOX)).then_inc(S("cmp_in"), 16)
            pool.dma_start(lamv[:, :, :], diff_lambda[0].rearrange("(a r) d -> a r d", a=1).broadcast_to([P, 4, HD])
                           ).then_inc(S("cmp_in"), 16)
            pool.dma_start(subg[:, :], bcast(diff_subln_g[0], 128)).then_inc(S("cmp_in"), 16)
            spans = [(0, 128, 0), (128, 256, 128)]
            for c0, n, q0 in spans:
                g.iota(dist[:, 0, c0:c0 + n], [[-1, n]], base=q0, channel_multiplier=1,
                       allow_small_or_imprecise_dtypes=True)
                g.iota(dist[:, 4, c0:c0 + n], [[-CMP_STRIDE, n]], base=q0 - (CMP_LEN - 1), channel_multiplier=1,
                       allow_small_or_imprecise_dtypes=True)
                for kk in (2, 3):
                    last = g.iota(dist[:, kk, c0:c0 + n].bitcast(i32), [[-1, n]], base=q0 + 256, channel_multiplier=1)
            chain(last)
            chain(g.memset(cmask[:, :], 0.0))
            for c0, n, q0 in spans:
                g.affine_select(out=dist[:, 0, c0:c0 + n], in_=dist[:, 0, c0:c0 + n], compare_op=ALU.is_ge, fill=MASKED,
                                base=q0, pattern=[[-1, n]], channel_multiplier=1)
                g.affine_select(out=dist[:, 4, c0:c0 + n], in_=dist[:, 4, c0:c0 + n], compare_op=ALU.is_ge, fill=MASKED,
                                base=q0 - (CMP_LEN - 1), pattern=[[-CMP_STRIDE, n]], channel_multiplier=1)
                last = g.affine_select(out=cmask[:, c0:c0 + n], in_=cmask[:, c0:c0 + n], compare_op=ALU.is_ge,
                                       fill=-MASKED, base=q0, pattern=[[-1, n]], channel_multiplier=1)
            chain(last)
            for c0, n, q0 in spans:
                last = g.affine_select(out=dist[:, 1, c0:c0 + n], in_=dist[:, 0, c0:c0 + n], compare_op=ALU.is_ge,
                                       fill=MASKED, base=128 - q0, pattern=[[1, n]], channel_multiplier=-1)
            last.then_inc(S("dist"), 1)
            chain(g.memset(upper[:, :, :], -1.0 / SC))
            for t in range(T):
                last = g.affine_select(out=upper[:, t, :], in_=upper[:, t, :], compare_op=ALU.is_ge, fill=0.0,
                                       base=-t * P, pattern=[[1, SEQ]], channel_multiplier=-1)
            last.then_inc(S("upper"), 1)
            chain(g.memset(valid[:, :], 1.0))
            g.affine_select(out=valid[:, :], in_=valid[:, :], compare_op=ALU.is_ge, fill=0.0, base=-(CMP_LEN - 1),
                            pattern=[[0, 1]], channel_multiplier=1).then_inc(S("valid"), 1)
            for i in range(16):
                last = g.memset(rec[:, i:i + 1], 1.0 / (i + 1))
            chain(last)

            pool.wait_ge(turned, TURNS["mem"] + 8)
            pool.dma_start(X[:, :, :], x[0].rearrange("(t p) n -> p t n", p=P)).then_inc(S("x_in"), 16)

            def inv_sqrt(tag, n, dst, src):
                pool.wait_ge(S("ms"), NORM[tag])
                if tag == "l0":
                    chain(g.tensor_tensor(dst, src, mhalf[:, 0:n], ALU.pow))
                    chain(g.tensor_tensor(nmean[:, :], mv[:, :, 0], rinv_x[:, :], ALU.mult))
                    g.tensor_scalar(nmean[:, :], nmean[:, :], -1.0, 1.0, ALU.mult, ALU.mult).then_inc(S("rinv"), 1)
                else:
                    g.tensor_tensor(dst, src, mhalf[:, 0:n], ALU.pow).then_inc(S("rinv"), 1)

            def natural(tag, gain_row, shift_row):
                pool.wait_ge(turned, TURNS[tag] + 8)
                for t in range(T):
                    ins = g.tensor_tensor(X[:, t, :], X[:, t, :], gain_row[:, :], ALU.mult)
                    if shift_row is not None:
                        chain(ins)
                        ins = g.tensor_tensor(X[:, t, :], X[:, t, :], shift_row[:, :], ALU.add)
                    ins.then_inc(S("natural"), 1)
            inv_sqrt("n1", T, rinv_x[:, :], ms[:, :])

            g.memset(cmp_kv[:, :, :, :, :].rearrange("p a t g d -> p (a t g d)"), 0.0).then_inc(S("cmp_zero"), 1)

            pool.wait_ge(S("tabs"), 1)

            def fox_table(par, h, val):
                for t, c0, n in at_main.spans():
                    last = g.tensor_tensor(tab_s[:, par, h, c0:c0 + n], cmask[:, c0:c0 + n], cumk[:, val, 0:n], ALU.add)
                chain(last)
                for t, c0, n in at_main.spans():
                    last = g.tensor_scalar(tab_s[:, par, h, c0:c0 + n], tab_s[:, par, h, c0:c0 + n],
                                           cumq[:, t, val:val + 1], 1.0, ALU.add, ALU.mult)
                return last

            def tables64(first):
                def build(i, par):
                    for h in range(2):
                        kind, val = heads[first + 2 * i + h][3]
                        last = fox_table(par, h, val) if kind == "fox" else g.tensor_scalar(
                            tab_s[:, par, h, :], dist[:, kind, :], -val / SC, 1.0, ALU.mult, ALU.mult)
                    return last
                return build

            def tables_diff(i, par):
                return g.tensor_scalar(tab_s[:, par, :, :], dist[:, 0, :].unsqueeze(1).broadcast_to([P, 2, 384]),
                                       -slope(i, DIFF) / SC, 1.0, ALU.mult, ALU.mult)
            at_main.tables(pool, tables64(0))
            at_main.wait(pool, "max", 12)
            at_nsa.tables(pool, tables64(24))
            at_nsa.wait(pool, "max", 8)
            at_diff.tables(pool, tables_diff)

            pool.wait_ge(S("dif_ms"), 1)
            g.tensor_tensor(dss[:, 2, :], dss[:, 1, :], mhalf[:, 0:8], ALU.pow).then_inc(S("dif_rinv"), 1)

            pool.wait_ge(turned, TURNS["o1"] + 8)
            pool.dma_start(X[:, :, :], x[0].rearrange("(t p) n -> p t n", p=P)).then_inc(S("x_again"), 16)
            pool.dma_start(gb0[:, :], bcast(ada_b[0, 2 * D:3 * D], D)).then_inc(S("x_again"), 16)
            inv_sqrt("n2", T, rinv_x[:, :], ms[:, :])
            pool.dma_start(gb0[:, :], bcast(ada_b[0, 5 * D:6 * D], D)).then_inc(S("g2b_in"), 16)
            for w, win in enumerate(POOL_WINDOWS):
                for s in range(T):
                    g.tensor_copy(band[:, w, s, 0:win], rec[:, 0:win])
                    last = g.memset(band[:, w, s, win:SEQ], 1.0 / win)
            chain(last)
            for w, win in enumerate(POOL_WINDOWS):
                for s in range(T):
                    last = g.affine_select(out=band[:, w, s, :], in_=band[:, w, s, :], compare_op=ALU.is_ge, fill=0.0,
                                           base=-s * P, pattern=[[1, SEQ]], channel_multiplier=-1)
            chain(last)
            for w, win in enumerate(POOL_WINDOWS):
                for s in range(T):
                    last = g.affine_select(out=band[:, w, s, :], in_=band[:, w, s, :], compare_op=ALU.is_ge, fill=0.0,
                                           base=win - 1 + s * P, pattern=[[-1, SEQ]], channel_multiplier=1)
            chain(last)
            for w in range(4):
                for s in range(T):
                    last = g.tensor_tensor(band[:, w, s, s * P:(s + 1) * P], band[:, w, s, s * P:(s + 1) * P],
                                           ident[:, :], ALU.subtract)
            last.then_inc(S("band"), 1)

            inv_sqrt("n3", T, rinv_x[:, :], ms[:, :])
            pool.dma_start(gb0[:, :], bcast(final_g, D)).then_inc(S("fin_in"), 16)
            pool.wait_ge(S("fin_in"), 16)
            natural("h0", gb0, None)

            pool.wait_ge(S("natural"), T)
            pool.wait_ge(S("u0_done"), 1)
            for grp in range(4):
                pool.dma_start(poolw_s[:, grp, :, :], pool_w[0, grp].rearrange("(k p) n -> p k n", p=P)
                               ).then_inc(S("poolw_in"), 16)
            pool.dma_start(gb0[:, 0:BR], bcast(pool_scale[0], BR)).then_inc(S("poolw_in"), 16)
            pool.wait_ge(turned, TURNS["m0"] + 8)
            pool.dma_start(gb0[:, :], bcast(ln_g[0], D)).then_inc(S("ln0_in"), 16)
            pool.dma_start(gb1[:, :], bcast(ln_b[0], D)).then_inc(S("ln0_in"), 16)
            inv_sqrt("l0", T, rinv_x[:, :], ms[:, :])
            pool.wait_ge(S("ln0_in"), 32)
            natural("h1", gb0, gb1)
            pool.wait_ge(turned, TURNS["m1"] + 8)
            pool.dma_start(gb0[:, :], bcast(ln_g[1], D)).then_inc(S("ln1_in"), 16)
            pool.dma_start(gb1[:, :], bcast(ln_b[1], D)).then_inc(S("ln1_in"), 16)
            inv_sqrt("l1", T, rinv_x[:, :], ms[:, :])

        @block.tensor
        def _(pe):
            pe.sem_inc(parts_used, HILO)
            pe.wait_ge(S("ident"), 1)
            pe.wait_ge(S("rows_in"), 112)
            nc.tensor.transpose(ps[:, 0, 0:P], rows[:, 0, :], ident[:, :])
            nc.tensor.transpose(ps[:, 0, P:P + 4 * KD], rows[0:4 * KD, 1, :], ident[0:4 * KD, 0:4 * KD]).then_inc(S("cols_tr"), 1)
            pe.wait_ge(S("ones"), 1)
            pe.wait_ge(S("cols_done"), 1)
            lead = turning(pe, "mem", x_block, lambda g: pe.wait_ge(S("mem_in"), 16))
            stage_matmuls(pe, "memkv", actT, as_columns=True, lead=lead)
            stage_matmuls(pe, "ada1", None, as_columns=True)
            pe.wait_ge(S("cmp_in"), 16 * 12)
            pe.wait_ge(ada_taken, 1 + ST["ada1"].end[3])
            lead = turning(pe, "u1", x_block, quarter_ready("u1"))
            stage_matmuls(pe, "win", actT, as_columns=True, lead=lead)

            def fox_sums():
                pe.wait_ge(S("upper"), 1)
                pe.wait_ge(S("logf"), 1)
                for h in range(FOX):
                    for s in range(T):
                        nc.tensor.matmul(ps[:, 4 + h // 2, (h % 2) * SEQ:(h % 2 + 1) * SEQ],
                                         logf[:, s, h:h + 1].broadcast_to([P, P]), upper[:, s, :],
                                         start=(s == 0), stop=(s == 1))
                for t in range(T):
                    for s in range(T):
                        last = nc.tensor.matmul(ps[:, 7, SEQ + t * FOX:SEQ + (t + 1) * FOX],
                                                upper[:, s, t * P:(t + 1) * P],
                                                logf[:, s, :], start=(s == 0), stop=(s == 1))
                last.then_inc(S("cum_ps"), 1)

            def cmp_turn():
                pe.wait_ge(acc_read, 2 + ST["win"].end[2])
                for kv in range(2):
                    for t in range(T):
                        cc = COL["cmp_k"] + kv * 128
                        nc.tensor.transpose(ps[:, 4, (kv * T + t) * P:(kv * T + t + 1) * P],
                                            proj[:, t, cc:cc + 128], ident[:, :])
                for kv in range(2):
                    last = nc.tensor.transpose(ps[:, 5, kv * CMP_LEN:(kv + 1) * CMP_LEN],
                                               pos_r[:, kv, :, :].rearrange("j a d -> j (a d)"),
                                               ident[0:CMP_LEN, 0:CMP_LEN])
                last.then_inc(S("cmp_tr"), 1)

            def cmp_hidden(grp):
                pe.wait_ge(S("cmp_pos"), 1)
                half = slice(grp * HD, (grp + 1) * HD)
                for kv in range(2):
                    for j in range(CMP_LEN):
                        r, jj = divmod(j, CMP_STRIDE)
                        src = cmp_in[half, kv, r, :].rearrange("p (c j) -> p c j", j=CMP_STRIDE)[:, r:r + N_CMP, jj]
                        last = nc.tensor.matmul(ps[0:HD, (5, 7)[grp], 64 + kv * 16:64 + kv * 16 + N_CMP],
                                                w1_s[half, kv, j, :], src, start=(j == 0), stop=(j == CMP_LEN - 1))
                if grp:
                    last.then_inc(S("cmp_h_ps"), 1)

            def cmp_out():
                pe.wait_ge(S("cmp_h"), 1)
                for kv in range(2):
                    for grp in range(GROUPS):
                        last = nc.tensor.matmul(ps[0:N_CMP, 4, (kv * 2 + grp) * HD:(kv * 2 + grp + 1) * HD],
                                                cmp_h[:, kv, grp, 0:N_CMP], w2_s[:, kv, :], start=True, stop=True)
                last.then_inc(S("cmp_ps"), 1)
            stage_matmuls(pe, "win_end", actT, width=[NC, NC, NC, LAST_W], as_columns=True,
                          lead={4: cmp_turn, 11: lambda: cmp_hidden(0), 14: lambda: cmp_hidden(1)},
                          hooks=beside({(1, 9): cmp_out, (2, 3): fox_sums}))
            pe.wait_ge(S("proj_done"), 1)
            pe.wait_ge(S("tabs"), 1)
            at_main.pe(pe)
            at_nsa.pe(pe)
            at_diff.pe(pe)
            lead = turning(pe, "o1", x_block, lambda g: pe.wait_ge(S("o1_ready"), 1 if g < 6 else 2))
            stage_matmuls(pe, "wout", actT, lead=lead)
            lead = turning(pe, "u2", lambda k, t: xn2[:, t, k * P:(k + 1) * P], quarter_ready("u2"))
            for i in range(3):
                st = ST[f"gu{i}"]

                def turn(p, j):
                    q = panel_no(st, p, j)
                    pe.wait_ge(acc_read, 2 + place(st, p, j).pn + 1)
                    for kk in range(2):
                        for t in range(T):
                            last = nc.tensor.transpose(ps[:, 4 + j, (kk * T + t) * P:(kk * T + t + 1) * P],
                                                       hid[:, j, t, kk * P:(kk + 1) * P], ident[:, :])
                    last.then_inc(S("hid_tr"), 1)
                stage_matmuls(pe, f"gu{i}", actT, hooks={11: turn}, one_acc=True, lead=lead if i == 0 else None)
                turn(st.bodies - 1, 1)
                pe.wait_ge(S("hid_taken"), 8 * i + 2 * st.bodies)
                stage_matmuls(pe, f"down{i}", hidT)
            lead = turning(pe, "h0", x_block, quarter_ready("h0"))
            stage_matmuls(pe, "in0", actT, lead=lead)
            pe.wait_ge(S("u0_done"), 1)
            pe.wait_ge(S("band"), 1)
            for cb in range(12):
                bank = cb // 2 % 2
                if cb % 2 == 0 and cb >= 4:
                    pe.wait_ge(S("pooledT"), cb // 2 - 1)
                for s in range(T):
                    last = nc.tensor.matmul(ps[:, bank, (cb % 2) * SEQ:(cb % 2 + 1) * SEQ],
                                            U[:, s, cb * P:(cb + 1) * P], band[:, cb // 3, s, :],
                                            start=(s == 0), stop=(s == 1))
                if cb % 2:
                    last.then_inc(S("pool_ps"), 1)
            pe.wait_ge(S("pooledT"), 6)
            pe.wait_ge(S("poolw_in"), 80)
            for grp in range(4):
                for t in range(T):
                    n = grp * T + t
                    if n >= 2:
                        pe.wait_ge(S("pool_mixed"), n - 1)
                    for kk in range(3):
                        last = nc.tensor.matmul(ps[:, 2 + n % 2, 0:384], pooledT[:, grp * 3 + kk, t * P:(t + 1) * P],
                                                poolw_s[:, grp, kk, :], start=(kk == 0), stop=(kk == 2))
                    last.then_inc(S("pool_out"), 1)
            pe.wait_ge(S("pool_mixed"), 8)
            at_mem[0].pe(pe)
            mixed = lambda k, t: U[:, t, k * P:(k + 1) * P] if k < 12 else U[:, t, 2 * BR + (k - 12) * P:2 * BR + (k - 11) * P]
            lead = turning(pe, "m0", mixed, lambda g: pe.wait_ge(S("m0_ready"), 1 if g < 6 else 2))
            stage_matmuls(pe, "out0", actT, lead=lead)
            lead = turning(pe, "h1", x_block, quarter_ready("h1"))
            stage_matmuls(pe, "kv", actT, lead=lead)
            stage_matmuls(pe, "in1", actT)
            pe.wait_ge(S("u1l_done"), 1)
            at_moba.pe(pe)
            at_mem[1].pe(pe)
            lead = turning(pe, "m1", mixed, lambda g: pe.wait_ge(S("m1_ready"), 1 if g < 6 else 2))
            stage_matmuls(pe, "out1", actT, lead=lead)

        @block.scalar
        def _(act):
            a = nc.scalar

            def stage_copy(name, dst, flag=None, width=None, lead=None, hooks={}):
                st = ST[name]

                def take(p, j):
                    panel_done(act, st, p, j)
                    for t in range(T):
                        d = dst(p, j, t)
                        w = width[j] if width else NC
                        last = a.activation(d, ps[:, bank_of(st, j) + t, 0:w], ACT.Copy)
                    last.then_inc(acc_read, 1)
                stage_split_hi(act, name, {6: take, **hooks}, width, lead)
                take(st.bodies - 1, len(st.panels) - 1)
                if flag:
                    act.wait_ge(acc_read, 2 + st.end[2])
                    act.sem_inc(S(flag), 1)

            act.sem_inc(acc_read, 2)
            act.wait_ge(S("cols_tr"), 1)
            a.activation(c_col[:, :], ps[:, 0, P:P + KD], ACT.Silu).then_inc(S("c_col"), 1)
            stage_copy("memkv", lambda p, j, t: memkv[:, ds(p, 1), t, j * NC:(j + 1) * NC].rearrange("p a n -> p (a n)"),
                       lead=split_plain_hi(act, "mem", actT))

            def normalise(tag, dst, mean=False):
                def quarter(q):
                    if q == 0:
                        act.wait_ge(S("rinv"), NORM[tag])
                    for t in range(T):
                        cs = slice(q * NC, (q + 1) * NC)
                        if mean:
                            last = a.activation(dst[:, t, cs], X[:, t, cs], ACT.Identity, bias=nmean[:, t:t + 1],
                                                scale=rinv_x[:, t:t + 1])
                        else:
                            last = a.activation(dst[:, t, cs], X[:, t, cs], ACT.Copy, scale=rinv_x[:, t:t + 1])
                    last.then_inc(S("xn"), 1)
                return quarter
            for q in range(4):
                normalise("n1", X)(q)
            stage_copy("win", lambda p, j, t: proj[:, t, ds(p * 4 * NC + j * NC, NC)], lead=split_mod_hi(act, "u1", actT))

            def fox_exp():
                act.wait_ge(S("fz"), 1)
                a.activation(fz[:, 2, :, :], fz[:, 1, :, :], ACT.Exp).then_inc(S("fe"), 1)
                act.wait_ge(S("lam_s"), 1)
                a.activation(lam[:, 2:4], lam[:, 0:2], ACT.Exp).then_inc(S("lam_e"), 1)

            def cmp_gelu():
                act.wait_ge(S("cmp_h_ps"), 1)
                for grp in range(GROUPS):
                    last = a.activation(cmp_h[:, :, grp, 0:N_CMP], o3(ps[0:HD, (5, 7)[grp], 64:96], 2)[:, :, 0:N_CMP],
                                        ACT.Gelu_apprx_tanh)
                last.then_inc(S("cmp_h"), 1)

            def nsa_gates():
                a.activation(gates[:, :, :, :].rearrange("p t h c -> p t (h c)"), proj[:, :, COL["gate"]:COL["gate"] + 24],
                             ACT.Sigmoid).then_inc(S("gates"), 1)
            act.wait_ge(acc_read, 2 + ST["win"].end[2])
            stage_copy("win_end", lambda p, j, t: proj[:, t, (8 + j) * NC:(9 + j) * NC] if j < 3 else
                       proj[:, t, N_IN - LAST_W:N_IN], "proj_done", width=[NC, NC, NC, LAST_W],
                       lead={10: fox_exp}, hooks=beside({(1, 4): cmp_gelu, (2, 8): nsa_gates}))
            at_main.act(act)
            at_nsa.act(act)

            def dilated_exp(i):
                if i == 1:
                    act.wait_ge(S("dd"), 1)
                    a.activation(dl[:, 2, :], dl[:, 1, :], ACT.Exp).then_inc(S("dexp"), 1)
            at_diff.act(act, dilated_exp)
            at_diff.wait(act, "pv", 4)
            stage_split_hi(act, "wout", lead=split_plain_hi(act, "o1", actT))
            for i in range(3):
                st = ST[f"gu{i}"]

                def gate_act(p, j):
                    panel_done(act, st, p, j)
                    for t in range(T):
                        last = a.activation(sil[:, j, t, :], ps[:, bank_of(st, j) + t, 0:256], ACT.Silu)
                    last.then_inc(S("sil"), 1)

                def hid_hi(p, j):
                    q = panel_no(st, p, j)
                    act.wait_ge(S("hid_tr"), 8 * i + q + 1)
                    a.activation(hidT[:, 0, ds(2 * q, 2), :], o3(ps[:, 4 + j, :], 2), ACT.Copy).then_inc(S("hid_hi"), 1)
                stage_split_hi(act, f"gu{i}", {6: gate_act, 15: hid_hi},
                               lead=split_mod_hi(act, "u2", actT, normalise("n2", xn2)) if i == 0 else None)
                gate_act(st.bodies - 1, 1)
                hid_hi(st.bodies - 1, 1)
                stage_split_hi(act, f"down{i}")

            def u_dst(p, j, t):
                return U[:, t, ds(p * 2 * NC + j * NC, NC)]
            stage_copy("in0", u_dst, "u0_done", lead=split_mod_hi(act, "h0", actT, normalise("n3", X)))

            def silu_gates(tag):
                a.activation(U[:, :, BR:2 * BR], U[:, :, BR:2 * BR], ACT.Silu)
                a.activation(U[:, :, 2 * BR + 512:], U[:, :, 2 * BR + 512:], ACT.Silu).then_inc(S(tag), 1)
            silu_gates("gsilu0")
            for n in range(6):
                act.wait_ge(S("pool_ps"), n + 1)
                a.activation(pooledT[:, 2 * n:2 * n + 2, :], o3(ps[:, n % 2, :], 2), ACT.Copy).then_inc(S("pooledT"), 1)
            act.wait_ge(S("pool_mixed"), 8)
            at_mem[0].act(act)
            at_mem[0].wait(act, "pv", 2)
            stage_split_hi(act, "out0", lead=split_plain_hi(act, "m0", actT))
            stage_copy("kv", lambda p, j, t: KV[:, t, ds(p * 2 * NC + j * NC, NC)],
                       lead=split_mod_hi(act, "h1", actT, normalise("l0", X, mean=True)))
            stage_copy("in1", u_dst, "u1l_done")
            silu_gates("gsilu1")
            at_moba.act(act)
            at_mem[1].act(act)
            at_mem[1].wait(act, "pv", 2)
            stage_split_hi(act, "out1", lead=split_plain_hi(act, "m1", actT))

        @block.vector
        def _(dve):
            v = nc.vector
            cn = [0]

            def chain(ins):
                cn[0] += 1
                ins.then_inc(S("dve_chain"), 1)
                dve.wait_ge(S("dve_chain"), cn[0])

            def take_columns(first_bias, first_mod):
                def take(st):
                    def f(p, j):
                        pl = place(st, p, j)
                        q = ada_no(st, p, j)
                        dve.wait_ge(ada_summed, pl.an + 1)
                        v.tensor_tensor(modT[:, ds(first_mod + q * 4, 4)], ps[:, 6, 0:4],
                                        cols[:, ds(first_bias + q * 4, 4)], ALU.add).then_inc(ada_taken, 1)
                    return f
                return take

            def take_rows(st):
                def f(p, j):
                    pl = place(st, p, j)
                    q = ada_no(st, p, j)
                    dve.wait_ge(ada_summed, pl.an + 1)
                    dve.wait_ge(*((S("x_again"), 32) if st is ST["wout"] else (S("g2b_in"), 16)))
                    v.tensor_tensor(gb0[:, ds(q * NC, NC)], ps[:, 6, :], gb0[:, ds(q * NC, NC)],
                                    ALU.add).then_inc(ada_taken, 1)
                return f

            def moments(tag, eps, rms):
                if tag == "n1":
                    for t in range(T):
                        for i in range(4):
                            last = v.bn_stats(stats[:, t, i, :], X[:, t, i * 512:(i + 1) * 512])
                    chain(last)
                else:
                    dve.wait_ge(S("panel_stats"), 4 * (NORM[tag] - 1))
                for t in range(T):
                    last = v.bn_aggr(mv[:, t, :], stats[:, t, :, :].rearrange("p a b -> p (a b)"))
                chain(last)
                if rms:
                    chain(v.tensor_tensor(ms[:, :], mv[:, :, 0], mv[:, :, 0], ALU.mult))
                    chain(v.tensor_tensor(ms[:, :], ms[:, :], mv[:, :, 1], ALU.add))
                    v.tensor_scalar(ms[:, :], ms[:, :], eps, None, ALU.add).then_inc(S("ms"), 1)
                else:
                    v.tensor_scalar(ms[:, :], mv[:, :, 1], eps, None, ALU.add).then_inc(S("ms"), 1)

            def panel_stats(st, p, j, q):
                dve.wait_ge(acc_read, 2 + place(st, p, j).pn + 1)
                for t in range(T):
                    last = v.bn_stats(stats[:, t, ds(q, 1), :].rearrange("p a b -> p (a b)"), X[:, t, ds(q * NC, NC)])
                last.then_inc(S("panel_stats"), 1)

            def gains(half):
                m = modT[:, 32 * half + KD:32 * half + 2 * KD]
                chain(v.tensor_scalar(m, m, 1.0, None, ALU.add))
                chain(v.tensor_tensor(gain[:, half, :], m, cols[:, 96 + KD * half:96 + KD * (half + 1)], ALU.mult))

            dve.sem_inc(blocks_read, 2 * RING)
            dve.sem_inc(ada_taken, 1)
            dve.sem_inc(S("at_pT1"), 1)
            dve.wait_ge(S("cols_tr"), 1)
            dve.wait_ge(S("c_col"), 1)
            v.tensor_copy(cols2[:, :], ps[:, 0, P + KD:P + 4 * KD])
            v.tensor_copy(cols[:, :], ps[:, 0, 0:P]).then_inc(S("cols_done"), 1)
            dve.wait_ge(S("cols_done"), 1)
            stage_split_lo(dve, "memkv", take=take_columns(0, 0)(ST["memkv"]), lead=split_plain_lo(dve, "mem", actT))
            dve.wait_ge(S("x_in"), 16)
            moments("n1", RMS_EPS, True)
            stage_split_lo(dve, "ada1", take=take_columns(16, 16)(ST["ada1"]))
            dve.wait_ge(ada_taken, 1 + ST["ada1"].end[3])
            gains(0)

            def columns(of, first):
                return lambda k: of[:, first + k:first + k + 1]
            stage_split_lo(dve, "win", take=take_columns(48, 32)(ST["win"]),
                           lead=split_mod_lo(dve, "u1", actT, columns(gain[:, 0, :], 0), columns(modT, 0)))

            def far(kk, mask):
                dve.wait_ge(S("dist"), 1)
                di = dist[:, kk, :].bitcast(i32)
                chain(v.tensor_scalar(di, di, mask, None, ALU.bitwise_and))
                chain(v.tensor_scalar(dist[:, kk, :], di, 1.0, MASKED, ALU.min, ALU.mult))
                chain(v.tensor_tensor(dist[:, kk, :], dist[:, kk, :], dist[:, 0, :], ALU.add))

            def fox_start():
                dve.wait_ge(acc_read, 2 + ST["win"].end[2])
                dve.wait_ge(S("cmp_in"), 16 * 12)
                fb = fox_b[:, :].unsqueeze(1).broadcast_to([P, T, FOX])
                chain(v.tensor_tensor(fz[:, 0, :, :], proj[:, :, COL["fox_f"]:COL["fox_f"] + FOX], fb, ALU.add))
                chain(v.tensor_scalar(fz[:, 1, :, :], fz[:, 0, :, :], -1.0, None, ALU.mult))
                v.tensor_tensor(fz[:, 1, :, :], fz[:, 1, :, :], fz[:, 0, :, :], ALU.min).then_inc(S("fz"), 1)

            def lambda_dots():
                for i in range(2):
                    last = v.tensor_tensor_reduce(out=lamv[:, 2 * i, :], in0=lamv[:, 2 * i, :], in1=lamv[:, 2 * i + 1, :],
                                                  scale=1.0, scalar=0.0, op0=ALU.mult, op1=ALU.add,
                                                  accum_out=lam[:, i:i + 1])
                last.then_inc(S("lam_s"), 1)

            def flat(x):
                return x.rearrange("p t h -> p (t h)")
            e, tt, t2, acc = (fz[:, i, :, :] for i in (2, 3, 4, 5))

            def fox_ratio():
                dve.wait_ge(S("fe"), 1)
                chain(v.tensor_scalar(tt, e, 2.0, None, ALU.add))
                chain(v.reciprocal(tt, tt))
                chain(v.tensor_tensor(tt, tt, e, ALU.mult))
                chain(v.tensor_tensor(t2, tt, tt, ALU.mult))
                chain(v.tensor_scalar(acc, t2, 1.0 / 17.0, None, ALU.mult))

            def fox_terms(terms):
                for m in terms:
                    chain(v.scalar_tensor_tensor(flat(acc), flat(acc), 1.0 / m, flat(t2), ALU.add, ALU.mult))

            def fox_log():
                chain(v.scalar_tensor_tensor(flat(acc), flat(acc), 1.0, flat(tt), ALU.add, ALU.mult))
                chain(v.tensor_scalar(fz[:, 6, :, :], fz[:, 0, :, :], 0.0, None, ALU.min))
                v.scalar_tensor_tensor(flat(logf), flat(acc), -2.0, flat(fz[:, 6, :, :]),
                                       ALU.mult, ALU.add).then_inc(S("logf"), 1)

            def fox_take():
                dve.wait_ge(S("cum_ps"), 1)
                for h in range(FOX):
                    v.tensor_copy(cumk[:, h, :], ps[:, 4 + h // 2, (h % 2) * SEQ:(h % 2 + 1) * SEQ])
                v.tensor_scalar(flat(cumq), ps[:, 7, SEQ:SEQ + T * FOX], -1.0, None, ALU.mult).then_inc(S("tabs"), 1)

            def lambda_end():
                dve.wait_ge(S("lam_e"), 1)
                chain(v.tensor_tensor(lam[:, 4:5], lam[:, 3:4], lam[:, 2:3], ALU.subtract))
                chain(v.tensor_scalar(lam[:, 5:6], lam[:, 4:5], -LAM_INIT, None, ALU.add))
                chain(v.tensor_scalar(subg[:, :], subg[:, :], 1.0 - LAM_INIT, None, ALU.mult))

            def cmp_positions():
                dve.wait_ge(S("cmp_tr"), 1)
                chain(v.tensor_copy(posT[:, :, :].rearrange("p a j -> p (a j)"), ps[:, 5, 0:2 * CMP_LEN]))
                for kv in range(2):
                    for r in range(2):
                        pv = posT[:, kv, r * 16:(r + 1) * 16].unsqueeze(1).broadcast_to([P, 16, 16])
                        last = v.tensor_tensor(o3(cmp_in[:, kv, r, :], 16), o3(ps[:, 4, kv * SEQ:(kv + 1) * SEQ], 16),
                                               pv, ALU.add)
                last.then_inc(S("cmp_pos"), 1)

            def cmp_take():
                dve.wait_ge(S("cmp_ps"), 1)
                dve.wait_ge(S("cmp_zero"), 1)
                for kv in range(2):
                    last = v.tensor_copy(cmp_kv[0:N_CMP, kv, 0, :, :].rearrange("p g d -> p (g d)"),
                                         ps[0:N_CMP, 4, kv * 128:(kv + 1) * 128])
                last.then_inc(S("cmp_done"), 1)
            stage_split_lo(dve, "win_end", width=[NC, NC, NC, LAST_W], take=take_columns(72, 56)(ST["win_end"]),
                           lead={4: fox_start, 5: lambda_dots, 8: cmp_positions, 13: fox_ratio},
                           hooks=beside({(1, 1): lambda: fox_terms((15, 13, 11, 9)), (1, 3): lambda: fox_terms((7, 5, 3)),
                                         (1, 5): fox_log, (1, 8): lambda: far(2, 3), (1, 14): cmp_take,
                                         (1, 11): lambda: far(3, 15), (2, 8): fox_take, (2, 15): lambda_end}))
            at_main.dve(dve)
            at_nsa.dve(dve)

            nm = [dnm[:, 0, :, 15 + 3 * g:18 + 3 * g] for g in range(3)]

            def d9(i):
                return dl[:, i, :].rearrange("p (t g h) -> p t g h", t=T, g=3)

            def dilated_lse():
                for i in range(2):
                    last = v.tensor_copy(dnm[:, i, :, :].rearrange("p t (j h) -> p t j h", h=2),
                                         stat[:, :, 4 * i:4 * i + 4].rearrange("p j (t h) -> p t j h", t=T))
                chain(last)
                chain(v.tensor_tensor(d9(0)[:, :, 0, :], nm[0], nm[1], ALU.min))
                chain(v.tensor_tensor(d9(0)[:, :, 0, :], d9(0)[:, :, 0, :], nm[2], ALU.min))
                for g in range(3):
                    last = v.tensor_tensor(d9(1)[:, :, g, :], d9(0)[:, :, 0, :], nm[g], ALU.subtract)
                last.then_inc(S("dd"), 1)

            def dilated_weights():
                dve.wait_ge(S("dexp"), 1)
                ll = dnm[:, 1, :, 15:24]
                chain(v.tensor_tensor(dl[:, 3, :].rearrange("p (t h) -> p t h", t=T), dl[:, 2, :].rearrange(
                    "p (t h) -> p t h", t=T), ll, ALU.mult))
                chain(v.tensor_tensor(d9(4)[:, :, 0, :], d9(3)[:, :, 0, :], d9(3)[:, :, 1, :], ALU.add))
                chain(v.tensor_tensor(d9(4)[:, :, 0, :], d9(4)[:, :, 0, :], d9(3)[:, :, 2, :], ALU.add))
                chain(v.reciprocal(d9(4)[:, :, 1, :], d9(4)[:, :, 0, :]))
                for g in range(3):
                    last = v.tensor_tensor(d9(5)[:, :, g, :], d9(3)[:, :, g, :], d9(4)[:, :, 1, :], ALU.mult)
                chain(last)
                od = X[:, :, 960:1536].rearrange("p t (h d) -> p t h d", h=9)
                v.tensor_tensor(od, od, dl[:, 5, :].rearrange("p (t h) -> p t h", t=T).unsqueeze(3).broadcast_to(
                    [P, T, 9, HD]), ALU.mult)

            def gate_of(i):
                return gates[:, :, :, i].unsqueeze(3).broadcast_to([P, T, NSA, HD])
            on = X[:, :, 448:960].rearrange("p t (h d) -> p t h d", h=8)

            def nsa_gated():
                dve.wait_ge(S("gates"), 1)
                dve.wait_ge(S("valid"), 1)
                chain(v.tensor_tensor(gates[:, 0, :, 0], gates[:, 0, :, 0], valid[:, :].broadcast_to([P, NSA]), ALU.mult))
                v.tensor_tensor(on, on, gate_of(1), ALU.mult)
                chain(v.tensor_tensor(res_nsa[:, :, 0:8, :], res_nsa[:, :, 0:8, :], gate_of(2), ALU.mult))

            def nsa_sum():
                v.tensor_tensor(res_nsa[:, :, 8:16, :], res_nsa[:, :, 8:16, :], gate_of(0), ALU.mult)
                chain(v.tensor_tensor(on, on, res_nsa[:, :, 0:8, :], ALU.add))
                chain(v.tensor_tensor(on, on, res_nsa[:, :, 8:16, :], ALU.add))

            def merge(i):
                if i == 0:
                    at_nsa.wait(dve, "normed", 8)
                    dilated_lse()
                    nsa_gated()
                elif i == 1:
                    dilated_weights()
                elif i == 2:
                    nsa_sum()
            at_diff.dve(dve, merge)
            at_diff.wait(dve, "normed", 4)
            for t in range(T):
                last = v.scalar_tensor_tensor(o3(X[:, t, 1536:2048], 4), res_diff[:, t, :, 1, :], lam[:, 5:6],
                                              res_diff[:, t, :, 0, :], ALU.mult, ALU.add)
            chain(last)
            dve.sem_inc(S("o1_ready"), 1)
            xd = X[:, :, 1536:2048]
            chain(v.tensor_tensor(diff_tmp[:, :, :], xd, xd, ALU.mult))
            chain(v.tensor_reduce(o3(dss[:, 0, :], 2), diff_tmp[:, :, :].rearrange("p t (h d) -> p t h d", h=4), AX.X, ALU.add))
            v.tensor_scalar(dss[:, 1, :], dss[:, 0, :], 1.0 / 128, RMS_EPS, ALU.mult, ALU.add).then_inc(S("dif_ms"), 1)
            dve.wait_ge(S("dif_rinv"), 1)
            xd4 = xd.rearrange("p t (h d) -> p t h d", h=4)
            chain(v.tensor_tensor(xd4, xd4, o3(dss[:, 2, :], 2).unsqueeze(3).broadcast_to([P, T, 4, 128]), ALU.mult))
            for t in range(T):
                last = v.tensor_tensor(o3(X[:, t, 1536:2048], 4), o3(X[:, t, 1536:2048], 4),
                                       subg[:, :].unsqueeze(1).broadcast_to([P, 4, 128]), ALU.mult)
            last.then_inc(S("o1_ready"), 1)

            def gated_add(name, at_k=12, take=None, lead=None):
                st = ST[name]

                def f(p, j):
                    dve.wait_ge(ada_taken, 1 + (place(st, p, j).an + 1 if take else ST["gu0"].end[3]))
                    panel_done(dve, st, p, j)
                    q = p * 2 + j if len(st.panels) == 2 else j
                    for t in range(T):
                        last = v.tensor_tensor(gy[:, t, :], ps[:, bank_of(st, j) + t, :], gb0[:, ds(q * NC, NC)], ALU.mult)
                    last.then_inc(S("gy"), 1)
                    if name == "wout":
                        dve.wait_ge(S("x_again"), 32)
                    dve.wait_ge(S("gy"), 4 * ("wout", "down0", "down1", "down2").index(name) + panel_no(st, p, j) + 1)
                    for t in range(T):
                        xs = X[:, t, ds(q * NC, NC)]
                        last = v.tensor_tensor(xs, xs, gy[:, t, :], ALU.add)
                    last.then_inc(acc_read, 1)
                    if name in ("wout", "down2"):
                        panel_stats(st, p, j, q)
                stage_split_lo(dve, name, {at_k: f}, take=take, lead=lead)
                f(st.bodies - 1, len(st.panels) - 1)

            gated_add("wout", take=take_rows(ST["wout"]), lead=split_plain_lo(dve, "o1", actT))
            moments("n2", RMS_EPS, True)
            gains(1)
            u2_lead = split_mod_lo(dve, "u2", actT, columns(gain[:, 1, :], 0), columns(modT, 32))
            for i in range(3):
                st = ST[f"gu{i}"]

                def up_mul(p, j):
                    dve.wait_ge(S("sil"), 8 * i + panel_no(st, p, j) + 1)
                    for t in range(T):
                        last = v.tensor_tensor(hid[:, j, t, :], sil[:, j, t, :], ps[:, bank_of(st, j) + t, 256:512], ALU.mult)
                    last.then_inc(acc_read, 1)

                def hid_lo(p, j):
                    q = panel_no(st, p, j)
                    dve.wait_ge(S("hid_hi"), 8 * i + q + 1)
                    v.tensor_tensor(hidT[:, 1, ds(2 * q, 2), :], o3(ps[:, 4 + j, :], 2),
                                    hidT[:, 0, ds(2 * q, 2), :].bitcast(f32), ALU.subtract).then_inc(S("hid_taken"), 1)
                stage_split_lo(dve, f"gu{i}", {8: up_mul, 15: hid_lo},
                               take=take_rows(ST["gu0"]) if i == 0 else None, one_acc=True,
                               lead=u2_lead if i == 0 else None)
                up_mul(st.bodies - 1, 1)
                hid_lo(st.bodies - 1, 1)
                gated_add(f"down{i}", 12 if i < 2 else 8)
            moments("n3", RMS_EPS, True)
            stage_split_lo(dve, "in0", lead=split_mod_lo(dve, "h0", actT, columns(cols2, 0), None))
            dve.wait_ge(S("poolw_in"), 80)
            dve.wait_ge(S("gsilu0"), 1)
            for grp in range(4):
                for t in range(T):
                    n = grp * T + t
                    dve.wait_ge(S("pool_out"), n + 1)
                    v.tensor_tensor(U[:, t, grp * 384:(grp + 1) * 384], ps[:, 2 + n % 2, 0:384],
                                    gb0[:, grp * 384:(grp + 1) * 384], ALU.mult).then_inc(S("pool_mixed"), 1)

            def gate_mixed(tag):
                v.tensor_tensor(U[:, :, 0:BR], U[:, :, 0:BR], U[:, :, BR:2 * BR], ALU.mult).then_inc(S(tag), 1)
                v.tensor_tensor(U[:, :, 2 * BR:2 * BR + 512], U[:, :, 2 * BR:2 * BR + 512], U[:, :, 2 * BR + 512:],
                                ALU.mult).then_inc(S(tag), 1)

            def layer_out(name, tag, lead):
                st = ST[name]

                def f(p, j):
                    dve.wait_ge(S("natural"), T * (1 if tag == "l0" else 2))
                    panel_done(dve, st, p, j)
                    for t in range(T):
                        xs = X[:, t, ds((p * 2 + j) * NC, NC)]
                        last = v.scalar_tensor_tensor(xs, xs, ALPHA, ps[:, bank_of(st, j) + t, :], ALU.mult, ALU.add)
                    last.then_inc(acc_read, 1)
                    panel_stats(st, p, j, p * 2 + j)
                stage_split_lo(dve, name, {12: f}, lead=lead)
                f(st.bodies - 1, 1)
                moments(tag, LN_EPS, False)

            at_mem[0].dve(dve)
            dve.wait_ge(S("pool_mixed"), 8)
            at_mem[0].finished(dve)
            gate_mixed("m0_ready")
            layer_out("out0", "l0", split_plain_lo(dve, "m0", actT))
            stage_split_lo(dve, "kv", lead=split_mod_lo(dve, "h1", actT, columns(cols2, 16), columns(cols2, 32)))
            stage_split_lo(dve, "in1")
            at_moba.dve(dve)
            at_mem[1].dve(dve)
            dve.wait_ge(S("gsilu1"), 1)
            at_moba.finished(dve)
            at_mem[1].finished(dve)
            gate_mixed("m1_ready")
            layer_out("out1", "l1", split_plain_lo(dve, "m1", actT))
            dve.wait_ge(S("ln1_in"), 32)
            dve.wait_ge(S("rinv"), NORM["l1"])
            for half in range(2):
                cs = slice(half * D // 2, (half + 1) * D // 2)
                for t in range(T):
                    last = v.scalar_tensor_tensor(X[:, t, cs], X[:, t, cs], mv[:, t, 0:1], gb0[:, cs],
                                                  ALU.subtract, ALU.mult)
                chain(last)
                for t in range(T):
                    v.scalar_tensor_tensor(X[:, t, cs], X[:, t, cs], rinv_x[:, t:t + 1], gb1[:, cs],
                                           ALU.mult, ALU.add).then_inc(S("y_done"), 1)


_INS = ['x', 'c', 'ada_w', 'ada_b', 'norm_mix_g', 'norm_ffn_g', 'w_in', 'fox_f_bias', 'nsa_cmp_w1', 'nsa_cmp_w2',
        'nsa_cmp_pos', 'diff_lambda', 'diff_subln_g', 'w_out', 'ffn_w_gate', 'ffn_w_up', 'ffn_w_down',
        'final_norm_g', 'mem_2', 'w_in_2', 'w_out_2', 'w_mem_kv_2', 'ln_g_2', 'ln_b_2', 'pool_w_2', 'pool_scale_2',
        'w_kv_shared_2']


def kernel(**inputs):
    import numpy as _np
    import concourse.bacc as _bacc
    from concourse import mybir as _mybir
    from concourse.bass_utils import run_bass_kernel_spmd as _run

    nc = _bacc.Bacc("TRN2", target_bir_lowering=False, num_devices=1)
    arrays, args = {}, []
    for name in _INS:
        a = _np.ascontiguousarray(inputs[name])
        arrays[f"in_{name}"] = a
        args.append(nc.dram_tensor(f"in_{name}", a.shape, _mybir.dt.from_np(a.dtype), kind="ExternalInput").ap())
    y = nc.dram_tensor("out_0", (1, SEQ, D), _mybir.dt.float32, kind="ExternalOutput").ap()
    program(nc, *args, y)
    r = _run(nc, [arrays], core_ids=[0])
    return r.results[0]["out_0"]
```

```python
import numpy as np
import concourse.bass as bass
from concourse import mybir
from contextlib import ExitStack

P = 128
T = 2
SEQ = P * T
D = 2048
KD = D // P
NC = 512
HD = 64
FF = 5632
FOX, NSA, GROUPS, DIL, DIFF = 7, 8, 2, 9, 4
SPLITS = [("fox_q", FOX * HD), ("fox_k", FOX * HD), ("fox_v", FOX * HD), ("fox_f", FOX), ("nsa_q", NSA * HD),
          ("cmp_k", 128), ("cmp_v", 128), ("slc_k", 128), ("slc_v", 128), ("win_k", 128), ("win_v", 128),
          ("gate", NSA * 3), ("dil_q", DIL * HD), ("dil_k", DIL * HD), ("dil_v", DIL * HD),
          ("diff_q", 512), ("diff_k", 512), ("diff_v", 512)]
COL, _at = {}, 0
for _n, _w in SPLITS:
    COL[_n] = _at
    _at += _w
N_IN = _at
LAST_W = 288
MASKED = 1.0e30
CMP_LEN, CMP_STRIDE = 32, 16
N_CMP = SEQ // CMP_STRIDE - CMP_LEN // CMP_STRIDE + 1
LAM_INIT = 0.2
RMS_EPS, LN_EPS = 1e-6, 1e-5
ALPHA = 4 ** 0.25
BR, MEMW, HD2 = 1536, 512, 128
POOL_WINDOWS = (2, 4, 8, 16)
RING, HILO = 8, 4


def slope(h, n):
    return float(np.float32(2.0 ** (-8.0 * (h + 1) / n)))


class Stage:

    def __init__(self, name, bodies, panels):
        self.name, self.bodies, self.panels = name, bodies, panels


STAGES = [
    Stage("memkv", 2, [("wa", 16)] * 2), Stage("ada1", 2, [("a", 16)] * 2),
    Stage("win", 2, [("w", 16)] + [("wa", 16)] * 3), Stage("win_end", 1, [("wa", 16), ("w", 16)] * 2),
    Stage("wout", 2, [("wa", 16)] * 2),
    Stage("gu0", 4, [("w", 16), ("wa", 16)]), Stage("down0", 2, [("w", 16)] * 2),
    Stage("gu1", 4, [("w", 16)] * 2), Stage("down1", 2, [("w", 16)] * 2),
    Stage("gu2", 3, [("w", 16)] * 2), Stage("down2", 1, [("w", 12)] * 4),
    Stage("in0", 3, [("w", 16)] * 2), Stage("in0m", 1, [("w", 16)] * 2), Stage("out0", 2, [("w", 16)] * 2),
    Stage("kv", 3, [("w", 16)] * 2), Stage("in1", 3, [("w", 16)] * 2), Stage("in1m", 1, [("w", 16)] * 2), Stage("out1", 2, [("w", 16)] * 2),
]


class Place:

    def __init__(self, kb, gb, pn, an):
        self.kb, self.gb, self.pn, self.an = kb, gb, pn, an


_kb = _gb = _pn = _an = 0
for _s in STAGES:
    _s.start = (_kb, _gb, _pn, _an)
    _s.local = []
    k = g = n = a = 0
    for _kind, _nk in _s.panels:
        _s.local.append((k, g, n, a))
        k += _nk * len(_kind)
        g += _nk * ("w" in _kind)
        n += "w" in _kind
        a += "a" in _kind
    _s.per = (k, g, n, a)
    _kb, _gb, _pn, _an = (x + y * _s.bodies for x, y in zip(_s.start, _s.per))
    _s.end = (_kb, _gb, _pn, _an)
ST = {s.name: s for s in STAGES}


def place(stage, p, j):
    return Place(*(s + l + p * q for s, l, q in zip(stage.start, stage.local[j], stage.per)))


def run_bodies(eng, stage, body):
    body(0, True)
    if stage.bodies > 1:
        with eng.Fori(1, stage.bodies) as p:
            body(p, False)


def program(nc, x, c, ada_w, ada_b, norm_mix_g, norm_ffn_g, w_in, fox_f_bias, cmp_w1, cmp_w2, cmp_pos,
            diff_lambda, diff_subln_g, w_out, w_gate, w_up, w_down, final_g, mem, w_in2, w_out2,
            w_mem_kv, ln_g, ln_b, pool_w, pool_scale, w_kv, out):
    f32, f32r, i32 = mybir.dt.float32, mybir.dt.float32r, mybir.dt.int32
    ACT, ALU, AX = mybir.ActivationFunctionType, mybir.AluOpType, mybir.AxisListType
    ds = bass.ds
    ctx = ExitStack()
    with ctx:
        arena_bytes = 212800
        arena = ctx.enter_context(nc.sbuf_tensor("arena", [P, arena_bytes // 4], f32))
        base = nc.sbuf_base
        base = (base - arena_bytes) // 32 * 32 + 32 if nc.sbuf_base > arena_bytes else (base + 31) // 32 * 32
        top = [0]

        def at(name, shape, dt, off):
            size = 4 * int(np.prod(shape[1:]))
            assert off % 32 == 0 and off + size <= arena_bytes, (name, off, size)
            return nc.alloc_sbuf_tensor_at(name, shape, dt, offset=base + off)

        def new(name, shape, dt=f32):
            off = top[0]
            top[0] += (4 * int(np.prod(shape[1:])) + 31) // 32 * 32
            return at(name, shape, dt, off)

        def region(size):
            off = top[0]
            top[0] += size
            return off

        raw = new("raw", [P, RING, 2, NC])
        r_hilo = region(2 * HILO * NC * 4)
        w_hi = at("w_hi", [P, HILO, NC], f32r, r_hilo)
        w_lo = at("w_lo", [P, HILO, NC], f32r, r_hilo + HILO * NC * 4)
        probs = at("probs", [P, 2, 2, 512], f32, r_hilo)
        probsT = at("probsT", [P, 2, 2, 512], f32, r_hilo + 8192)
        r_act = region(32768)
        actT = at("actT", [P, 2, KD, SEQ], f32r, r_act)
        res_nsa = at("res_nsa", [P, T, 16, HD], f32, r_act)
        res_diff = at("res_diff", [P, T, DIFF, 2, 128], f32, r_act + 8192)
        pooledT = at("pooledT", [P, 12, SEQ], f32, r_act)
        poolw_s = at("poolw_s", [P, 4, 3, 384], f32, r_act + 12288)
        r_x = top[0]
        X = new("X", [P, T, D])
        memkv = new("memkv", [P, 2, T, 1024])
        r_one = region(66368)
        proj = at("proj", [P, T, N_IN], f32, r_one)
        o1 = (N_IN * T * 4 + 31) // 32 * 32
        cumk = at("cumk", [P, FOX, SEQ], f32, r_one + o1)
        diff_tmp = at("diff_tmp", [P, T, 512], f32, r_one + o1)
        dist = at("dist", [P, 5, 384], f32, r_one + o1 + 7168)
        cmp_kv = at("cmp_kv", [P, 2, T, 2, HD], f32, r_one + o1 + 14848)
        upper = at("upper", [P, T, SEQ], f32, r_one + o1 + 16896)
        assert o1 + 16896 + 2048 <= 66368
        hidT = at("hidT", [P, 2, KD, SEQ], f32r, r_one)
        xn2 = at("xn2", [P, T, D], f32, r_one + 32768)
        hid = at("hid", [P, 2, T, 256], f32, r_one + 49152)
        sil = at("sil", [P, 2, T, 256], f32, r_one + 53248)
        U = at("U", [P, T, 4096], f32, r_one)
        KV = at("KV", [P, T, 3072], f32, r_one + 32768)
        pscale = at("pscale", [P, BR], f32, r_one + 32768)
        band = at("band", [P, 4, T, SEQ], f32, r_one + 57344)
        r_stg = region(20480)
        gb0 = at("gb0", [P, D], f32, r_stg)
        gb1 = at("gb1", [P, D], f32, r_stg + 8192)
        ada_acc = at("ada_acc", [P, 2, NC], f32, r_stg + 16384)
        w1_s = at("w1_s", [HD, 2, CMP_LEN, HD], f32, r_stg)
        qk_s = at("qk_s", [P, 2, 2, T, 128], f32, r_stg)
        v_s = at("v_s", [P, 2, T, 128], f32, r_stg + 4096)
        tab_s = at("tab_s", [P, 2, 2, 384], f32, r_stg + 6144)
        qkT_s = at("qkT_s", [P, 2, 2, SEQ], f32, r_stg + 12288)
        qk2_s = at("qk2_s", [P, 2, 2, T, 256], f32, r_stg)
        v2_s = at("v2_s", [P, 2, T, 256], f32, r_stg + 8192)
        qkT2_s = at("qkT2_s", [P, 2, 2, 2, SEQ], f32, r_stg + 12288)
        ident = new("ident", [P, P])
        ones = new("ones", [P, P])
        rows = new("rows", [P, 2, P])
        pos_r = new("pos_r", [CMP_LEN, 2, HD])
        cols = new("cols", [P, P])
        cols2 = new("cols2", [P, 3 * KD])
        c_col = new("c_col", [P, KD])
        c_raw = new("c_raw", [P, KD])
        posT = new("posT", [HD, 2, CMP_LEN])
        modT = new("modT", [P, 4 * KD])
        gain = new("gain", [P, 2, KD])
        cmask = new("cmask", [P, 384])
        stats = new("stats", [P, T, 4, 6])
        mv = new("mv", [P, T, 2])
        ms = new("ms", [P, T])
        rinv_x = new("rinv_x", [P, T])
        nmean = new("nmean", [P, T])
        mhalf = new("mhalf", [P, 8])
        sm = new("sm", [P, 2, 8])
        mx = new("mx", [P, 2, 4])
        mx_zero = new("mx_zero", [P, 2, 2])
        rs = new("rs", [P, 2, 4])
        stat = new("stat", [P, 12, 8])
        fox_b = new("fox_b", [P, FOX])
        fz = new("fz", [P, 8, T, FOX])
        logf = new("logf", [P, T, FOX])
        cumq = new("cumq", [P, T, FOX])
        gates = new("gates", [P, T, NSA, 3])
        lamv = new("lamv", [P, 4, HD])
        lam = new("lam", [P, 8])
        subg = new("subg", [P, 128])
        dl = new("dl", [P, 6, T * 9])
        dnm = new("dnm", [P, 2, T, 24])
        dss = new("dss", [P, 3, 8])
        cmp_in = at("cmp_in", [HD, 2, 2, GROUPS * SEQ], f32, r_x)
        cmp_h = new("cmp_h", [HD, 2, 2, 16])
        w2_s = new("w2_s", [HD, 2, HD])
        evac = at("evac", [P, 2, 512], f32, r_one + 49152)
        valid = new("valid", [P, 1])
        rec = new("rec", [P, 16])
        gy = at("gy", [P, T, NC], f32, r_stg + 8192)
        ps = ctx.enter_context(nc.psum_tensor("ps", [P, 8, 512], f32))

        def o3(ap, a):
            return ap.rearrange("p (a b) -> p a b", a=a)

        sems = {}

        def S(name):
            if name not in sems:
                sems[name] = ctx.enter_context(nc.semaphore(name))
            return sems[name]

        w_loaded = [S(f"w_loaded{i}") for i in range(RING)]
        blocks_read = S("blocks_read")
        hi_ready = S("hi_ready")
        parts_used = S("parts_used")
        acc_read = S("acc_read")
        ada_summed = S("ada_summed")
        ada_taken = S("ada_taken")

        def chunks(stage, j):
            kind, nk = stage.panels[j]
            off = 0
            for ch in range(nk // 2):
                for k in kind:
                    yield k, ch, off
                    off += 2

        def stage_loads(sp, name, w_src, a_src=None, width=NC):
            st = ST[name]

            def body(p, first):
                for j in range(len(st.panels)):
                    pl = place(st, p, j)
                    for kind, ch, off in chunks(st, j):
                        slot = ((st.start[0] + st.local[j][0] + off) // 2) % RING
                        sp.wait_ge(blocks_read, pl.kb + off + 2)
                        if kind == "w":
                            for dst, src in w_src(p, j, ch):
                                sp.dma_start(raw[:, slot, :, dst[0]:dst[1]], src).then_inc(w_loaded[slot], 16)
                        else:
                            sp.dma_start(raw[:, slot, :, :], a_src(p, j, ch)).then_inc(w_loaded[slot], 16)
            run_bodies(sp, st, body)

        loads_before = []
        n = [0] * RING
        for st in STAGES:
            st.slot_start = list(n)
            st.slot_local = []
            cnt = [0] * RING
            for j in range(len(st.panels)):
                row = []
                for kind, ch, off in chunks(st, j):
                    s = ((st.start[0] + st.local[j][0] + off) // 2) % RING
                    cnt[s] += 32 if st.name.startswith("gu") and kind == "w" else 16
                    row.append((s, cnt[s]))
                st.slot_local.append(row)
            st.slot_per = cnt
            n = [a + b * st.bodies for a, b in zip(n, cnt)]

        def wait_chunk(eng, st, p, j, idx):
            s, local = st.slot_local[j][idx]
            eng.wait_ge(w_loaded[s], st.slot_start[s] + local + p * st.slot_per[s])

        def beside(work):
            ks = {k for _, k in work}
            return {k: (lambda p, j, k=k: work[j + 1, k]() if (j + 1, k) in work else None) for k in ks}

        def stage_split_hi(act, name, hooks=None, width=None, lead=None):
            st = ST[name]

            def body(p, first):
                for j in range(len(st.panels)):
                    if "w" not in st.panels[j][0]:
                        continue
                    pl = place(st, p, j)
                    w = width[j] if width else NC
                    for idx, (kind, ch, off) in enumerate(chunks(st, j)):
                        if kind != "w":
                            continue
                        for b in range(2):
                            k = 2 * ch + b
                            if hooks and k in hooks and not (first and j == 0):
                                hooks[k](*((p, j - 1) if j else (p - 1, len(st.panels) - 1)))
                            if lead and k in lead and first and j == 0:
                                lead[k]()
                            if b == 0:
                                wait_chunk(act, st, p, j, idx)
                            slot = ((st.start[0] + st.local[j][0] + off) // 2) % RING
                            act.wait_ge(parts_used, pl.gb + k + 1)
                            g = (st.local[j][1] + k) % HILO
                            act.activation(w_hi[:, g, 0:w], raw[:, slot, b, 0:w], ACT.Copy).then_inc(hi_ready, 1)
            run_bodies(act, st, body)

        def stage_split_lo(dve, name, hooks=None, width=None, take=None, one_acc=False, lead=None):
            st = ST[name]
            kinds = [k for k, _ in st.panels]

            def before(p, j):
                return (p, j - 1) if j else (p - 1, len(st.panels) - 1)

            def body(p, first):
                na = 0
                for j in range(len(st.panels)):
                    pl = place(st, p, j)
                    w = width[j] if width else NC
                    alone = first and j == 0
                    for idx, (kind, ch, off) in enumerate(chunks(st, j)):
                        slot = ((st.start[0] + st.local[j][0] + off) // 2) % RING
                        for b in range(2):
                            k = 2 * ch + b
                            if not alone and kind == kinds[j][0]:
                                if k == 12 and take and "a" in kinds[before(0, j)[1]]:
                                    take(*before(p, j))
                                if hooks and k in hooks:
                                    hooks[k](*before(p, j))
                            if alone and lead and k in lead and kind == kinds[j][0]:
                                lead[k]()
                            if kind == "w":
                                dve.wait_ge(hi_ready, pl.gb + k + 1)
                                g = (st.local[j][1] + k) % HILO
                                nc.vector.tensor_tensor(w_lo[:, g, 0:w], raw[:, slot, b, 0:w],
                                                        w_hi[:, g, 0:w].bitcast(f32),
                                                        ALU.subtract).then_inc(blocks_read, 1)
                            else:
                                acc = ada_acc[:, 0 if one_acc else na % 2, :]
                                if k == 0:
                                    wait_chunk(dve, st, p, j, idx)
                                    nc.vector.tensor_scalar(acc, raw[:, slot, b, :], c_col[:, 0:1], None,
                                                            ALU.mult).then_inc(blocks_read, 1)
                                else:
                                    if b == 0:
                                        wait_chunk(dve, st, p, j, idx)
                                    dve.wait_ge(blocks_read, 2 * RING + pl.kb + off + b - (1 if b else
                                                1 + 2 * (len(kinds[j]) - 1)) + 1)
                                    nc.vector.scalar_tensor_tensor(acc, raw[:, slot, b, :], c_col[:, k:k + 1], acc,
                                                                   ALU.mult, ALU.add).then_inc(blocks_read, 1)
                    na += "a" in kinds[j]
            run_bodies(dve, st, body)
            if take and "a" in kinds[-1]:
                take(st.bodies - 1, len(st.panels) - 1)

        def ada_sum(pe, st, p, j, na, as_columns, one_acc=False):
            pl = place(st, p, j)
            acc = ada_acc[:, 0 if one_acc else na % 2, :]
            kind, nk = st.panels[j]
            pe.wait_ge(blocks_read, 2 * RING + pl.kb + nk * len(kind))
            pe.wait_ge(ada_taken, pl.an + 1)
            if as_columns:
                for i in range(4):
                    last = nc.tensor.matmul(ps[:, 6, i:i + 1], acc[:, i * P:(i + 1) * P], ones[:, 0:1],
                                            start=True, stop=True)
            else:
                last = nc.tensor.matmul(ps[:, 6, :], ones[:, :], acc, start=True, stop=True)
            last.then_inc(ada_summed, 1)

        def stage_matmuls(pe, name, lhs, hooks=None, width=None, as_columns=False, one_acc=False, lead=None):
            st = ST[name]
            kinds = [k for k, _ in st.panels]

            def body(p, first):
                na = 0
                for j, (kind, nk) in enumerate(st.panels):
                    pl = place(st, p, j)
                    w = width[j] if width else NC
                    pj = (p, j - 1) if j else (p - 1, len(st.panels) - 1)
                    pa = [sum("a" in q for q in kinds[:pj[1]])][0]
                    if kind == "a":
                        ada_sum(pe, st, p, j, na, as_columns)
                        na += 1
                        continue
                    pe.wait_ge(acc_read, pl.pn + 1)
                    bank = 2 * ((st.start[2] + st.local[j][2]) % 2)
                    for idx, (kd, ch, off) in enumerate(chunks(st, j)):
                        if kd != "w":
                            continue
                        for b in range(2):
                            k = 2 * ch + b
                            if not (first and j == 0):
                                if k == 8 and "a" in kinds[pj[1]]:
                                    ada_sum(pe, st, pj[0], pj[1], pa, as_columns, one_acc)
                                if hooks and k in hooks:
                                    hooks[k](*pj)
                            elif lead and k in lead:
                                lead[k]()
                            pe.wait_ge(blocks_read, 2 * RING + pl.kb + off + b + 1)
                            g = (st.local[j][1] + k) % HILO
                            for t in range(T):
                                hi, lo = (lhs[:, part, k, t * P:(t + 1) * P] for part in range(2))
                                o = ps[:, bank + t, 0:w]
                                nc.tensor.matmul(o, hi, w_hi[:, g, 0:w], start=(k == 0), stop=False)
                                nc.tensor.matmul(o, hi, w_lo[:, g, 0:w], start=False, stop=False)
                                last = nc.tensor.matmul(o, lo, w_hi[:, g, 0:w], start=False, stop=(k == nk - 1))
                            last.then_inc(parts_used, 1)
            run_bodies(pe, st, body)
            if kinds[-1] == "wa":
                ada_sum(pe, st, st.bodies - 1, len(kinds) - 1, sum("a" in q for q in kinds[:-1]), as_columns, one_acc)

        def panel_done(eng, st, p, j):
            pl = place(st, p, j)
            eng.wait_ge(parts_used, HILO + pl.gb + st.panels[j][1])

        def bank_of(st, j):
            return 2 * ((st.start[2] + st.local[j][2]) % 2)

        def panel_no(st, p, j):
            return p * len(st.panels) + j

        def ada_no(st, p, j):
            return p * st.per[3] + st.local[j][3]

        TURNS = {tag: 8 * i for i, tag in enumerate(("mem", "u1", "o1", "u2", "h0", "m0", "h1", "m1"))}
        MODS = {"u1": 0, "u2": 8, "h0": 16, "h1": 24}
        turned = S("turned")
        turn_mod = S("turn_mod")
        turn_hi = S("turn_hi")
        turn_taken = S("turn_taken")

        def turning(pe, tag, src, ready, when={4: 1, 5: 2, 6: 3, 7: 4}):
            def turn(g):
                ready(g)
                for i in range(4):
                    k, t = 2 * g + i // 2, i % 2
                    last = nc.tensor.transpose(ps[:, 4 + g % 4, i * P:(i + 1) * P], src(k, t), ident[:, :])
                last.then_inc(turned, 1)

            def before(g):
                for other in when:
                    if when[other] == g:
                        turn(other)
                pe.wait_ge(turn_taken, TURNS[tag] + g + 1)
            for g in range(4):
                turn(g)
            return {2 * g: (lambda g=g: before(g)) for g in range(8)}

        def in_lead(first, later):
            lead = {2 * g: (lambda g=g: later(g)) for g in range(3, 8)}
            lead[4] = first
            return lead

        def split_plain_hi(act, tag, dst):
            def high(g):
                act.wait_ge(turned, TURNS[tag] + g + 1)
                act.activation(dst[:, 0, 2 * g:2 * g + 2, :], o3(ps[:, 4 + g % 4, :], 2),
                               ACT.Copy).then_inc(turn_hi, 1)
            return in_lead(lambda: [high(g) for g in range(3)], high)

        def split_plain_lo(dve, tag, dst, between=None):
            def low(g):
                if between and g in between:
                    between[g]()
                dve.wait_ge(turn_hi, TURNS[tag] + g + 1)
                nc.vector.tensor_tensor(dst[:, 1, 2 * g:2 * g + 2, :], o3(ps[:, 4 + g % 4, :], 2),
                                        dst[:, 0, 2 * g:2 * g + 2, :].bitcast(f32),
                                        ALU.subtract).then_inc(turn_taken, 1)
            return in_lead(lambda: [low(g) for g in range(3)], low)

        def split_mod_hi(act, tag, dst, quarter=None):
            def high(g):
                if quarter and g == 3:
                    quarter(3)
                act.wait_ge(turn_mod, MODS[tag] + g + 1)
                act.activation(dst[:, 0, 2 * g:2 * g + 2, :], o3(evac[:, g % 2, :], 2),
                               ACT.Copy).then_inc(turn_hi, 1)

            def first():
                if quarter:
                    quarter(0)
                    quarter(1)
                high(0)
                high(1)
                if quarter:
                    quarter(2)
                high(2)
            return in_lead(first, high)

        def split_mod_lo(dve, tag, dst, gain_of, shift_of):
            def mod(g):
                if g >= 2:
                    dve.wait_ge(turn_taken, TURNS[tag] + g - 1)
                dve.wait_ge(turned, TURNS[tag] + g + 1)
                for i in range(2):
                    k = 2 * g + i
                    args = (evac[:, g % 2, i * SEQ:(i + 1) * SEQ], ps[:, 4 + g % 4, i * SEQ:(i + 1) * SEQ], gain_of(k))
                    if shift_of:
                        last = nc.vector.tensor_scalar(*args, shift_of(k), ALU.mult, ALU.add)
                    else:
                        last = nc.vector.tensor_scalar(*args, None, ALU.mult)
                last.then_inc(turn_mod, 1)

            def low(g):
                dve.wait_ge(turn_hi, TURNS[tag] + g + 1)
                nc.vector.tensor_tensor(dst[:, 1, 2 * g:2 * g + 2, :], o3(evac[:, g % 2, :], 2),
                                        dst[:, 0, 2 * g:2 * g + 2, :].bitcast(f32),
                                        ALU.subtract).then_inc(turn_taken, 1)

            def first():
                mod(0)
                mod(1)
                low(0)
                mod(2)
                low(1)

            def later(g):
                mod(g)
                low(g - 1)
            lead = in_lead(first, later)
            lead[15] = lambda: low(7)
            return lead

        class Attn:

            def __init__(self, tag, pairs, dh, dv, full, table, scale, dest, keep=False):
                self.tag, self.pairs, self.dh, self.dv, self.full = tag, pairs, dh, dv, full
                self.table, self.scale, self.dest, self.keep = table, scale, dest, keep
                self.start = Attn.started
                Attn.started += pairs
                self.before = self.after = None
                self.kw = 512 if full else 384

            PER = {"exp": 2, "scores": 2, "p_tr": 2}
            started = 0

            def s(self, name):
                return S("at_" + name)

            def wait(self, eng, name, value):
                eng.wait_ge(self.s(name), self.start * self.PER.get(name, 1) + value)

            def staged(self, eng, what, i_par, half):
                n = 64 if what == "qk" else 32
                eng.wait_ge(S(f"at_{what}{i_par}"), n * (self.start // 2) + n * half + n)

            def spans(self):
                return [(0, 0, 256 if self.full else 128), (1, self.kw - 256, 256)]

            def steps(self, eng, step, first):
                first()
                n = self.pairs
                if n > 4:
                    with eng.Fori(0, n // 2 - 2) as p:
                        step(2 * p, 0, p, 3)
                        step(2 * p + 1, 1, p, 3)
                for i in range(max(n - 4, 0), n):
                    step(i, i % 2, i // 2, n - 1 - i)

            def q_src(self, par, kind, head, t):
                if self.dh == HD:
                    return qk_s[:, par, kind, t, :]
                return qk2_s[:, par, kind, t, head * 128:(head + 1) * 128]

            def qT(self, par, head, kind):
                if self.dh == HD:
                    return qkT_s[head * HD:(head + 1) * HD, par, kind, :]
                return qkT2_s[:, par, head, kind, :]

            def v(self, par, head, kt):
                if self.dh == HD:
                    return v_s[:, par, kt, :] if self.dv == 128 else v_s[:, par, kt, head * HD:(head + 1) * HD]
                return v2_s[:, par, kt, head * 128:(head + 1) * 128]

            def turn(self, pe, i, par, p):
                self.staged(pe, "qk", par, p)
                for b in range(1 if self.dh == HD else 2):
                    for kind in range(2):
                        for t in range(T):
                            last = nc.tensor.transpose(ps[:, b, (kind * T + t) * P:(kind * T + t + 1) * P],
                                                       self.q_src(par, kind, b, t), ident[:, :])
                last.then_inc(self.s("qk_tr"), 1)

            def scores(self, pe, i, par, before):
                self.wait(pe, "qkT", i + 1)
                if before:
                    if before.table:
                        self.wait(pe, "max", i)
                    else:
                        self.wait(pe, "exp", 2 * i)
                for h in range(2):
                    q, k = self.qT(par, h, 0), self.qT(par, h, 1)
                    for t, c0, nk in self.spans():
                        last = nc.tensor.matmul(ps[:, 2 + h, c0:c0 + nk], q[:, t * P:(t + 1) * P], k[:, 0:nk],
                                                start=True, stop=True)
                    last.then_inc(self.s("scores"), 1)

            def pe(self, pe, beside_first=None):
                nxt = self.after

                def step(i, par, p, more):
                    if more:
                        self.scores(pe, i + 1, 1 - par, self)
                    elif nxt:
                        nxt.scores(pe, 0, 0, self)
                    if beside_first and type(i) is int and i == 0:
                        beside_first()
                    for h in range(2):
                        self.wait(pe, "exp", 2 * i + h + 1)
                        if h == 1:
                            self.wait(pe, "pT1", i + 1)
                        for t, c0, nk in self.spans():
                            for kt in range(nk // P):
                                d = self.pT_col(kt, t)
                                last = nc.tensor.transpose(ps[:, 4 + h, d:d + P],
                                                           probs[:, par, h, c0 + kt * P:c0 + (kt + 1) * P], ident[:, :])
                        last.then_inc(self.s("p_tr"), 1)
                    if more > 1:
                        self.turn(pe, i + 2, par, p + 1)
                    elif nxt:
                        nxt.turn(pe, 1 - more, par, 0)
                    self.staged(pe, "v", par, p)
                    for h in range(2):
                        self.wait(pe, "pT0", i + 1) if h == 0 else self.wait(pe, "pT1", i + 2)
                        for t, c0, nk in self.spans():
                            o = ps[:, 6 + par, (t * 2 + h) * self.dv:(t * 2 + h + 1) * self.dv]
                            for kt in range(nk // P):
                                d = self.pT_col(kt, t)
                                last = nc.tensor.matmul(o, probsT[:, par, h, d:d + P], self.v(par, h, kt),
                                                        start=(kt == 0), stop=(kt == nk // P - 1))
                    last.then_inc(self.s("pv"), 1)

                def first():
                    if not self.before:
                        self.turn(pe, 0, 0, 0)
                        self.scores(pe, 0, 0, None)
                        self.turn(pe, 1, 1, 0)
                self.steps(pe, step, first)

            def pT_col(self, kt, t):
                return (kt * T + t) * P if self.full or kt == 0 else 256

            def early(self, act, i, par):
                self.wait(act, "qk_tr", i + 1)
                if self.dh == HD:
                    act.activation(qkT_s[:, par, :, :], o3(ps[:, 0, :], 2), ACT.Copy).then_inc(self.s("qkT"), 1)
                else:
                    act.activation(qkT2_s[:, par, :, :, :].rearrange("p a b c -> p (a b c)"),
                                   ps[:, 0:2, :].rearrange("p a b -> p (a b)"), ACT.Copy).then_inc(self.s("qkT"), 1)

            def late(self, act, i, par):
                self.wait(act, "max", i + 1)
                for h in range(2):
                    for t, c0, nk in self.spans():
                        src = (probs[:, par, h, c0:c0 + nk] if self.table else ps[:, 2 + h, c0:c0 + nk])
                        q = t * 2 + h
                        last = act.activation(probs[:, par, h, c0:c0 + nk], src, ACT.Exp, bias=sm[:, par, q:q + 1],
                                              scale=self.scale, accum_out=sm[:, par, 4 + q:5 + q])
                    last.then_inc(self.s("exp"), 1)

            def act(self, act, merge=None, beside_first=None):
                nxt = self.after

                def step(i, par, p, more):
                    if beside_first and type(i) is int and i == 0:
                        beside_first()
                    self.wait(act, "p_tr", 2 * i + 1)
                    act.activation(probsT[:, par, 0, 0:self.kw], ps[:, 4, 0:self.kw],
                                   ACT.Copy).then_inc(self.s("pT0"), 1)
                    if more > 1:
                        self.early(act, i + 2, par)
                    elif nxt:
                        nxt.early(act, 1 - more, par)
                    if more:
                        self.late(act, i + 1, 1 - par)
                    elif nxt:
                        nxt.late(act, 0, 0)
                    if merge:
                        merge(i)

                def first():
                    if not self.before:
                        self.early(act, 0, 0)
                        self.early(act, 1, 1)
                        self.late(act, 0, 0)
                self.steps(act, step, first)

            def maxima(self, dve, i, par):
                if self.table == "staged":
                    self.wait(dve, "tab", i + 1)
                for h in range(2):
                    self.wait(dve, "scores", 2 * i + h + 1)
                    if self.table:
                        nc.vector.memset(mx_zero[:, par, h:h + 1], 0.0)
                        for t, c0, nk in self.spans():
                            q = t * 2 + h
                            tab = tab_s[:, par, h, c0:c0 + nk] if self.table == "staged" else cmask[:, c0:c0 + nk]
                            last = nc.vector.tensor_tensor_reduce(
                                out=probs[:, par, h, c0:c0 + nk], in0=ps[:, 2 + h, c0:c0 + nk], in1=tab,
                                scale=1.0, scalar=-3.0e38, op0=ALU.add, op1=ALU.max,
                                accum_out=mx[:, par, q:q + 1])
                    else:
                        last = nc.vector.tensor_reduce(mx[:, par, h:h + 3:2], o3(ps[:, 2 + h, :], 2), AX.X, ALU.max)
                last.then_inc(self.s("raw_max"), 1)
                self.wait(dve, "raw_max", i + 1)
                nc.vector.tensor_scalar(sm[:, par, 0:4], mx[:, par, :], -self.scale, None,
                                        ALU.mult).then_inc(self.s("max"), 1)

            def dve(self, dve, merge=None):
                nxt = self.after

                def step(i, par, p, more):
                    if more:
                        self.maxima(dve, i + 1, 1 - par)
                    elif nxt:
                        nxt.maxima(dve, 0, 0)
                    self.wait(dve, "p_tr", 2 * i + 2)
                    nc.vector.tensor_copy(probsT[:, par, 1, 0:self.kw], ps[:, 5, 0:self.kw]).then_inc(self.s("pT1"), 1)
                    if self.keep:
                        nc.vector.tensor_copy(stat[:, ds(i, 1), :], sm[:, par:par + 1, :])
                    nc.vector.reciprocal(rs[:, par, :], sm[:, par, 4:8]).then_inc(self.s("rs"), 1)
                    self.wait(dve, "rs", i + 1)
                    self.wait(dve, "pv", i + 1)
                    o = ps[:, 6 + par, 0:4 * self.dv].rearrange("p (t h d) -> p t h d", t=T, h=2)
                    r = rs[:, par, :].rearrange("p (t h) -> p t h", t=T).unsqueeze(3).broadcast_to([P, T, 2, self.dv])
                    nc.vector.tensor_tensor(self.dest(i), o, r, ALU.mult).then_inc(self.s("normed"), 1)
                    if merge:
                        merge(i)

                self.steps(dve, step, lambda: None if self.before else self.maxima(dve, 0, 0))

            def move(self, sp, i, kinds, sem, source):
                for kind in kinds:
                    src = source(i, kind)
                    for t in range(T):
                        qkv = (qk2_s, v2_s) if self.dh == HD2 else (qk_s, v_s)
                        dst = qkv[1][:, i % 2, t, :] if kind == 2 else qkv[0][:, i % 2, kind, t, :]
                        if len(src.shape) == 4:
                            dst = dst.rearrange("p (h d) -> p h d", h=2)
                        sp.dma_start(dst, src[:, t]).then_inc(sem, 16)

            def tables(self, pool, build):
                for i in range(self.pairs):
                    if self.start + i >= 2:
                        self.wait(pool, "max", i - 1)
                    build(i, i % 2).then_inc(self.s("tab"), 1)

            def finished(self, eng):
                self.wait(eng, "normed", self.pairs)

        SC = HD ** -0.5
        heads = []
        for h in range(FOX):
            heads.append((COL["fox_q"] + h * HD, COL["fox_k"] + h * HD, COL["fox_v"] + h * HD, ("fox", h)))
        for h in range(NSA):
            g = h // (NSA // GROUPS) * HD
            heads.append((COL["nsa_q"] + h * HD, COL["slc_k"] + g, COL["slc_v"] + g, (0, slope(h, NSA))))
        for h in range(DIL):
            heads.append((COL["dil_q"] + h * HD, COL["dil_k"] + h * HD, COL["dil_v"] + h * HD,
                          (1 + h // 3, slope(h, DIL))))
        for h in range(NSA):
            g = h // (NSA // GROUPS) * HD
            heads.append((COL["nsa_q"] + h * HD, COL["win_k"] + g, COL["win_v"] + g, (0, slope(h, NSA))))
        for h in range(NSA):
            heads.append((COL["nsa_q"] + h * HD, ("cmp", h // 4), ("cmp", h // 4), (4, slope(h, NSA))))

        at_main = Attn("main", 12, HD, HD, False, "staged", SC,
                       lambda i: X[:, :, ds(i * 128, 128)].rearrange("p t (h d) -> p t h d", h=2), keep=True)
        at_nsa = Attn("nsa", 8, HD, HD, False, "staged", SC, lambda i: res_nsa[:, :, ds(i * 2, 2), :])
        at_diff = Attn("diff", 4, HD, 128, False, "staged", SC,
                       lambda i: res_diff[:, :, ds(i, 1), :, :].rearrange("p t a m d -> p t (a m) d"))
        SC2 = HD2 ** -0.5

        def gather(sp, loops, late=None):
            pairs = [(loop, i, source) for loop, source in loops for i in range(loop.pairs)]
            for n in range(len(pairs) + 2):
                if n == 2 and late:
                    sp.wait_ge(S(late[0]), late[1])
                if n >= 2:
                    loop, i, source = pairs[n - 2]
                    if loop.start + i >= 2:
                        loop.wait(sp, "pv", i - 1)
                    loop.move(sp, i, (2,), S(f"at_v{i % 2}"), source)
                if n < len(pairs):
                    loop, i, source = pairs[n]
                    if loop.start + i >= 2:
                        loop.wait(sp, "qk_tr", i - 1)
                    loop.move(sp, i, (0, 1), S(f"at_qk{i % 2}"), source)

        def mem_attn(tag):
            return Attn(tag, 2, HD2, HD2, True, None, SC2,
                        lambda i: U[:, :, ds(2 * BR + i * 256, 256)].rearrange("p t (h d) -> p t h d", h=2))
        at_mem = [mem_attn("mem0")]
        at_moba = Attn("moba", 6, HD2, HD2, False, "mask", SC2,
                       lambda i: U[:, :, ds(i * 256, 256)].rearrange("p t (h d) -> p t h d", h=2))
        at_mem.append(mem_attn("mem1"))

        for one, other in ((at_main, at_nsa), (at_nsa, at_diff), (at_moba, at_mem[1])):
            one.after, other.before = other, one

        def bcast(row, n):
            return row.rearrange("(a n) -> a n", a=1).broadcast_to([P, n])

        NORM = {"n1": 1, "n2": 2, "n3": 3, "l0": 4, "l1": 5}
        XN = {"u1": 0, "u2": 4, "h0": 8, "h1": 12}

        def quarter_ready(tag):
            return lambda g: nc.tensor.wait_ge(S("xn"), XN[tag] + g // 2 + 1)

        def x_block(k, t):
            return X[:, t, k * P:(k + 1) * P]

        block = ctx.enter_context(nc.Block())

        @block.sync
        def _(sp):
            def blocks2(w, row0, ch, c0, n):
                r = row0 + ch * 256
                return w[ds(r, 256), :].rearrange("(b p) n -> p b n", p=P)[:, :, ds(c0, n)]

            def pair64(first):
                def source(i, what):
                    a, b = (h[what] for h in heads[first + 2 * i:first + 2 * i + 2])
                    if isinstance(a, tuple):
                        return cmp_kv[:, what - 1, :, a[1], :].unsqueeze(2).broadcast_to([P, T, 2, HD])
                    if a == b:
                        return proj[:, :, a:a + HD].unsqueeze(2).broadcast_to([P, T, 2, HD])
                    if b == a + HD:
                        return proj[:, :, a:a + 2 * HD]
                    return proj[:, :, a:2 * b - a].rearrange("p t (h s) -> p t h s", h=2)[:, :, :, 0:HD]
                return source

            def pair_diff(i, what):
                c0 = COL[("diff_q", "diff_k", "diff_v")[what]] + i * 128
                return proj[:, :, c0:c0 + 128]

            def pair_mem(layer):
                def source(i, what):
                    if what == 0:
                        return U[:, :, 2 * BR + i * 256:2 * BR + (i + 1) * 256]
                    c0 = (what - 1) * MEMW + i * 256
                    return memkv[:, layer, :, c0:c0 + 256]
                return source

            def pair_moba(i, what):
                src = U if what == 0 else KV
                c0 = i * 256 + (BR if what == 2 else 0)
                return src[:, :, c0:c0 + 256]

            def panels(w, row0=0, per=2):
                return lambda p, j, ch: [((0, NC), blocks2(w, row0, ch, p * per * NC + j * NC, NC))]

            ADA = {"memkv": 0, "ada1": D, "win": 3 * D, "win_end": 3 * D + 6 * NC, "wout": 2 * D, "gu0": 5 * D}

            def ada(name):
                return lambda p, j, ch: blocks2(ada_w[0], 0, ch, ADA[name] + ada_no(ST[name], p, j) * NC, NC)

            def gate_up(first):
                def src(p, j, ch):
                    c0 = first * P + (p * 2 + j) * 256
                    return [((0, 256), blocks2(w_gate[0], 0, ch, c0, 256)), ((256, 512), blocks2(w_up[0], 0, ch, c0, 256))]
                return src

            sp.dma_start(rows[0:96, 0, :], ada_b[0].rearrange("(r n) -> r n", n=P)).then_inc(S("rows_in"), 16)
            sp.dma_start(rows[96:112, 0, :], norm_mix_g[0].rearrange("(r n) -> r n", n=P)).then_inc(S("rows_in"), 16)
            sp.dma_start(rows[112:128, 0, :], norm_ffn_g[0].rearrange("(r n) -> r n", n=P)).then_inc(S("rows_in"), 16)
            for i, row in enumerate((c[0], final_g, ln_g[0], ln_b[0])):
                sp.dma_start(rows[i * KD:(i + 1) * KD, 1, :], row.rearrange("(r n) -> r n", n=P)
                             ).then_inc(S("rows_in"), 16)
            for q in range(4):
                sp.dma_start(X[:, :, q * NC:(q + 1) * NC], mem[0].rearrange("(t p) n -> p t n", p=P)[
                    :, :, q * NC:(q + 1) * NC]).then_inc(S(f"mem_in{q}"), 16)
            stage_loads(sp, "memkv", lambda p, j, ch: [((0, NC), w_mem_kv[ds(p, 1), :, :].rearrange("a k n -> (a k) n")[
                ch * 256:(ch + 1) * 256, j * NC:(j + 1) * NC].rearrange("(b p) n -> p b n", p=P))], ada("memkv"))
            stage_loads(sp, "ada1", None, ada("ada1"))
            stage_loads(sp, "win", panels(w_in[0], per=4), ada("win"))

            def win_end(p, j, ch):
                c0, n = (8 * NC + j * NC, NC) if j < 3 else (N_IN - LAST_W, LAST_W)
                return [((0, n), blocks2(w_in[0], 0, ch, c0, n))]
            stage_loads(sp, "win_end", win_end, ada("win_end"))
            sp.wait_ge(acc_read, 2 + ST["win"].end[2])
            sp.wait_ge(S("cmp_h_ps"), 1)
            gather(sp, [(at_main, pair64(0)), (at_nsa, pair64(24)), (at_diff, pair_diff)], late=("proj_done", 1))
            stage_loads(sp, "wout", panels(w_out[0]), ada("wout"))
            stage_loads(sp, "gu0", gate_up(0), ada("gu0"))
            stage_loads(sp, "down0", panels(w_down[0], 0))
            stage_loads(sp, "gu1", gate_up(16))
            stage_loads(sp, "down1", panels(w_down[0], 2048))
            stage_loads(sp, "gu2", gate_up(32))
            stage_loads(sp, "down2", panels(w_down[0], 4096))

            def branches(w):
                return lambda p, j, ch: [((0, NC), blocks2(w, 0, ch, p * NC + j * BR, NC))]
            stage_loads(sp, "in0", branches(w_in2[0]))
            stage_loads(sp, "in0m", lambda p, j, ch: [((0, NC), blocks2(w_in2[0], 0, ch, 2 * BR + j * NC, NC))])
            sp.wait_ge(S("natural"), T)
            sp.wait_ge(S("u0_done"), 1)
            gather(sp, [(at_mem[0], pair_mem(0))])
            stage_loads(sp, "out0", panels(w_out2[0]))
            stage_loads(sp, "kv", panels(w_kv))
            stage_loads(sp, "in1", branches(w_in2[1]))
            stage_loads(sp, "in1m", lambda p, j, ch: [((0, NC), blocks2(w_in2[1], 0, ch, 2 * BR + j * NC, NC))])
            sp.wait_ge(S("u1l_done"), 1)
            sp.wait_ge(S("natural"), 2 * T)
            gather(sp, [(at_moba, pair_moba), (at_mem[1], pair_mem(1))])
            stage_loads(sp, "out1", panels(w_out2[1]))
            for half in range(2):
                cs = slice(half * D // 2, (half + 1) * D // 2)
                for t in range(T):
                    sp.wait_ge(S("y_done"), 2 * half + t + 1)
                    sp.dma_start(out[0, t * P:(t + 1) * P, cs], X[:, t, cs]).then_inc(S("stored"), 16)
            sp.wait_ge(S("stored"), 16 * 2 * T)

        @block.gpsimd
        def _(pool):
            g = nc.gpsimd
            cn = [0]

            def chain(ins):
                cn[0] += 1
                ins.then_inc(S("pool_chain"), 1)
                pool.wait_ge(S("pool_chain"), cn[0])

            chain(g.memset(ident[:, :], 0.0))
            g.affine_select(out=ident[:, :], in_=ident[:, :], compare_op=ALU.not_equal, fill=1.0, base=0,
                            pattern=[[-1, P]], channel_multiplier=1).then_inc(S("ident"), 1)
            g.memset(ones[:, :], 1.0).then_inc(S("ones"), 1)
            g.memset(mhalf[:, :], -0.5)
            for kv in range(2):
                pool.dma_start(pos_r[:, kv, :], cmp_pos[0, kv]).then_inc(S("cmp_in"), 16)
                pool.dma_start(w1_s[:, kv, :, :], cmp_w1[0, kv].rearrange("(j d) f -> d j f", d=HD)
                               ).then_inc(S("cmp_in"), 16)
            pool.dma_start(w2_s[:, :, :], cmp_w2[0].rearrange("a d f -> d a f")).then_inc(S("cmp_in"), 16)
            pool.dma_start(fox_b[:, :], bcast(fox_f_bias[0], FOX)).then_inc(S("cmp_in"), 16)
            pool.dma_start(lamv[:, :, :], diff_lambda[0].rearrange("(a r) d -> a r d", a=1).broadcast_to([P, 4, HD])
                           ).then_inc(S("cmp_in"), 16)
            pool.dma_start(subg[:, :], bcast(diff_subln_g[0], 128)).then_inc(S("cmp_in"), 16)
            spans = [(0, 128, 0), (128, 256, 128)]
            for c0, n, q0 in spans:
                g.iota(dist[:, 0, c0:c0 + n], [[-1, n]], base=q0, channel_multiplier=1,
                       allow_small_or_imprecise_dtypes=True)
                g.iota(dist[:, 4, c0:c0 + n], [[-CMP_STRIDE, n]], base=q0 - (CMP_LEN - 1), channel_multiplier=1,
                       allow_small_or_imprecise_dtypes=True)
                for kk in (2, 3):
                    last = g.iota(dist[:, kk, c0:c0 + n].bitcast(i32), [[-1, n]], base=q0 + 256, channel_multiplier=1)
            chain(last)
            chain(g.memset(cmask[:, :], 0.0))
            for c0, n, q0 in spans:
                g.affine_select(out=dist[:, 0, c0:c0 + n], in_=dist[:, 0, c0:c0 + n], compare_op=ALU.is_ge, fill=MASKED,
                                base=q0, pattern=[[-1, n]], channel_multiplier=1)
                g.affine_select(out=dist[:, 4, c0:c0 + n], in_=dist[:, 4, c0:c0 + n], compare_op=ALU.is_ge, fill=MASKED,
                                base=q0 - (CMP_LEN - 1), pattern=[[-CMP_STRIDE, n]], channel_multiplier=1)
                last = g.affine_select(out=cmask[:, c0:c0 + n], in_=cmask[:, c0:c0 + n], compare_op=ALU.is_ge,
                                       fill=-MASKED, base=q0, pattern=[[-1, n]], channel_multiplier=1)
            chain(last)
            for c0, n, q0 in spans:
                last = g.affine_select(out=dist[:, 1, c0:c0 + n], in_=dist[:, 0, c0:c0 + n], compare_op=ALU.is_ge,
                                       fill=MASKED, base=128 - q0, pattern=[[1, n]], channel_multiplier=-1)
            last.then_inc(S("dist"), 1)
            chain(g.memset(upper[:, :, :], -1.0 / SC))
            for t in range(T):
                last = g.affine_select(out=upper[:, t, :], in_=upper[:, t, :], compare_op=ALU.is_ge, fill=0.0,
                                       base=-t * P, pattern=[[1, SEQ]], channel_multiplier=-1)
            last.then_inc(S("upper"), 1)
            chain(g.memset(valid[:, :], 1.0))
            g.affine_select(out=valid[:, :], in_=valid[:, :], compare_op=ALU.is_ge, fill=0.0, base=-(CMP_LEN - 1),
                            pattern=[[0, 1]], channel_multiplier=1).then_inc(S("valid"), 1)
            for i in range(16):
                last = g.memset(rec[:, i:i + 1], 1.0 / (i + 1))
            chain(last)

            pool.wait_ge(turned, TURNS["mem"] + 8)
            pool.dma_start(X[:, :, :], x[0].rearrange("(t p) n -> p t n", p=P)).then_inc(S("x_in"), 16)

            def inv_sqrt(tag, n, dst, src):
                pool.wait_ge(S("ms"), NORM[tag])
                if tag == "l0":
                    chain(g.tensor_tensor(dst, src, mhalf[:, 0:n], ALU.pow))
                    chain(g.tensor_tensor(nmean[:, :], mv[:, :, 0], rinv_x[:, :], ALU.mult))
                    g.tensor_scalar(nmean[:, :], nmean[:, :], -1.0, 1.0, ALU.mult, ALU.mult).then_inc(S("rinv"), 1)
                else:
                    g.tensor_tensor(dst, src, mhalf[:, 0:n], ALU.pow).then_inc(S("rinv"), 1)

            def natural(tag, gain_row, shift_row):
                pool.wait_ge(turned, TURNS[tag] + 8)
                for t in range(T):
                    ins = g.tensor_tensor(X[:, t, :], X[:, t, :], gain_row[:, :], ALU.mult)
                    if shift_row is not None:
                        chain(ins)
                        ins = g.tensor_tensor(X[:, t, :], X[:, t, :], shift_row[:, :], ALU.add)
                    ins.then_inc(S("natural"), 1)
            inv_sqrt("n1", T, rinv_x[:, :], ms[:, :])

            g.memset(cmp_kv[:, :, :, :, :].rearrange("p a t g d -> p (a t g d)"), 0.0).then_inc(S("cmp_zero"), 1)

            pool.wait_ge(S("tabs"), 1)

            def fox_table(par, h, val):
                for t, c0, n in at_main.spans():
                    last = g.tensor_tensor(tab_s[:, par, h, c0:c0 + n], cmask[:, c0:c0 + n], cumk[:, val, 0:n], ALU.add)
                chain(last)
                for t, c0, n in at_main.spans():
                    last = g.tensor_scalar(tab_s[:, par, h, c0:c0 + n], tab_s[:, par, h, c0:c0 + n],
                                           cumq[:, t, val:val + 1], 1.0, ALU.add, ALU.mult)
                return last

            def tables64(first):
                def build(i, par):
                    for h in range(2):
                        kind, val = heads[first + 2 * i + h][3]
                        last = fox_table(par, h, val) if kind == "fox" else g.tensor_scalar(
                            tab_s[:, par, h, :], dist[:, kind, :], -val / SC, 1.0, ALU.mult, ALU.mult)
                    return last
                return build

            def tables_diff(i, par):
                return g.tensor_scalar(tab_s[:, par, :, :], dist[:, 0, :].unsqueeze(1).broadcast_to([P, 2, 384]),
                                       -slope(i, DIFF) / SC, 1.0, ALU.mult, ALU.mult)
            at_main.tables(pool, tables64(0))
            at_nsa.tables(pool, tables64(24))
            at_diff.tables(pool, tables_diff)

            pool.wait_ge(S("dif_ms"), 1)
            g.tensor_tensor(dss[:, 2, :], dss[:, 1, :], mhalf[:, 0:8], ALU.pow).then_inc(S("dif_rinv"), 1)

            pool.wait_ge(turned, TURNS["o1"] + 8)
            pool.dma_start(X[:, :, :], x[0].rearrange("(t p) n -> p t n", p=P)).then_inc(S("x_again"), 16)
            pool.dma_start(gb0[:, :], bcast(ada_b[0, 2 * D:3 * D], D)).then_inc(S("x_again"), 16)
            inv_sqrt("n2", T, rinv_x[:, :], ms[:, :])
            pool.dma_start(gb0[:, :], bcast(ada_b[0, 5 * D:6 * D], D)).then_inc(S("g2b_in"), 16)
            for w, win in enumerate(POOL_WINDOWS):
                for s in range(T):
                    g.tensor_copy(band[:, w, s, 0:win], rec[:, 0:win])
                    last = g.memset(band[:, w, s, win:SEQ], 1.0 / win)
            chain(last)
            for w, win in enumerate(POOL_WINDOWS):
                for s in range(T):
                    last = g.affine_select(out=band[:, w, s, :], in_=band[:, w, s, :], compare_op=ALU.is_ge, fill=0.0,
                                           base=-s * P, pattern=[[1, SEQ]], channel_multiplier=-1)
            chain(last)
            for w, win in enumerate(POOL_WINDOWS):
                for s in range(T):
                    last = g.affine_select(out=band[:, w, s, :], in_=band[:, w, s, :], compare_op=ALU.is_ge, fill=0.0,
                                           base=win - 1 + s * P, pattern=[[-1, SEQ]], channel_multiplier=1)
            chain(last)
            for w in range(4):
                for s in range(T):
                    last = g.tensor_tensor(band[:, w, s, s * P:(s + 1) * P], band[:, w, s, s * P:(s + 1) * P],
                                           ident[:, :], ALU.subtract)
            last.then_inc(S("band"), 1)

            inv_sqrt("n3", T, rinv_x[:, :], ms[:, :])
            pool.dma_start(gb0[:, :], bcast(final_g, D)).then_inc(S("fin_in"), 16)
            pool.wait_ge(S("fin_in"), 16)
            natural("h0", gb0, None)

            pool.wait_ge(S("natural"), T)
            pool.wait_ge(S("u0_done"), 1)
            for grp in range(4):
                pool.dma_start(poolw_s[:, grp, :, :], pool_w[0, grp].rearrange("(k p) n -> p k n", p=P)
                               ).then_inc(S("poolw_in"), 16)
            pool.dma_start(pscale[:, :], bcast(pool_scale[0], BR)).then_inc(S("poolw_in"), 16)
            pool.wait_ge(turned, TURNS["m0"] + 8)
            pool.dma_start(gb0[:, :], bcast(ln_g[0], D)).then_inc(S("ln0_in"), 16)
            pool.dma_start(gb1[:, :], bcast(ln_b[0], D)).then_inc(S("ln0_in"), 16)
            inv_sqrt("l0", T, rinv_x[:, :], ms[:, :])
            pool.wait_ge(S("ln0_in"), 32)
            natural("h1", gb0, gb1)
            pool.wait_ge(turned, TURNS["m1"] + 8)
            pool.dma_start(gb0[:, :], bcast(ln_g[1], D)).then_inc(S("ln1_in"), 16)
            pool.dma_start(gb1[:, :], bcast(ln_b[1], D)).then_inc(S("ln1_in"), 16)
            inv_sqrt("l1", T, rinv_x[:, :], ms[:, :])

        @block.tensor
        def _(pe):
            pe.sem_inc(parts_used, HILO)
            pe.wait_ge(S("ident"), 1)
            pe.wait_ge(S("rows_in"), 112)
            nc.tensor.transpose(ps[:, 0, 0:P], rows[:, 0, :], ident[:, :])
            nc.tensor.transpose(ps[:, 0, P:P + 4 * KD], rows[0:4 * KD, 1, :], ident[0:4 * KD, 0:4 * KD]).then_inc(S("cols_tr"), 1)
            pe.wait_ge(S("ones"), 1)
            pe.wait_ge(S("cols_done"), 1)
            lead = turning(pe, "mem", x_block, lambda g: pe.wait_ge(S(f"mem_in{g // 2}"), 16))
            stage_matmuls(pe, "memkv", actT, as_columns=True, lead=lead)
            stage_matmuls(pe, "ada1", None, as_columns=True)
            pe.wait_ge(S("cmp_in"), 16 * 8)
            pe.wait_ge(ada_taken, 1 + ST["ada1"].end[3])
            lead = turning(pe, "u1", x_block, quarter_ready("u1"))
            stage_matmuls(pe, "win", actT, as_columns=True, lead=lead)

            def fox_sums():
                pe.wait_ge(S("upper"), 1)
                pe.wait_ge(S("logf"), 1)
                for h in range(FOX):
                    for s in range(T):
                        nc.tensor.matmul(ps[:, 4 + h // 2, (h % 2) * SEQ:(h % 2 + 1) * SEQ],
                                         logf[:, s, h:h + 1].broadcast_to([P, P]), upper[:, s, :],
                                         start=(s == 0), stop=(s == 1))
                for t in range(T):
                    for s in range(T):
                        last = nc.tensor.matmul(ps[:, 7, SEQ + t * FOX:SEQ + (t + 1) * FOX],
                                                upper[:, s, t * P:(t + 1) * P],
                                                logf[:, s, :], start=(s == 0), stop=(s == 1))
                last.then_inc(S("cum_ps"), 1)

            def cmp_turn():
                pe.wait_ge(acc_read, 2 + ST["win"].end[2])
                for kv in range(2):
                    for grp in range(GROUPS):
                        for t in range(T):
                            cc = COL["cmp_k"] + kv * 128 + grp * HD
                            nc.tensor.transpose(ps[0:HD, 4 + kv, (grp * T + t) * P:(grp * T + t + 1) * P],
                                                proj[:, t, cc:cc + HD], ident[:, :])
                for kv in range(2):
                    last = nc.tensor.transpose(ps[0:HD, 7, kv * CMP_LEN:(kv + 1) * CMP_LEN], pos_r[:, kv, :],
                                               ident[0:CMP_LEN, 0:CMP_LEN])
                last.then_inc(S("cmp_tr"), 1)

            def cmp_hidden(kv):
                pe.wait_ge(S("cmp_pos"), 1)
                for j in range(CMP_LEN):
                    r, jj = divmod(j, CMP_STRIDE)
                    src = cmp_in[:, kv, r, :].rearrange("p (g c j) -> p g c j", g=GROUPS, j=CMP_STRIDE)[
                        :, :, r:r + N_CMP, jj]
                    c0 = 64 + kv * 32
                    last = nc.tensor.matmul(ps[0:HD, 7, c0:c0 + GROUPS * N_CMP].rearrange("p (g c) -> p g c", g=GROUPS),
                                            w1_s[:, kv, j, :], src, start=(j == 0), stop=(j == CMP_LEN - 1))
                if kv:
                    last.then_inc(S("cmp_h_ps"), 1)

            def cmp_out():
                pe.wait_ge(S("cmp_h"), 1)
                for kv in range(2):
                    for grp in range(GROUPS):
                        last = nc.tensor.matmul(ps[0:N_CMP, 4, (kv * 2 + grp) * HD:(kv * 2 + grp + 1) * HD],
                                                cmp_h[:, kv, grp, 0:N_CMP], w2_s[:, kv, :], start=True, stop=True)
                last.then_inc(S("cmp_ps"), 1)
            stage_matmuls(pe, "win_end", actT, width=[NC, NC, NC, LAST_W], as_columns=True,
                          lead={7: cmp_turn, 12: lambda: cmp_hidden(0), 15: lambda: cmp_hidden(1)},
                          hooks=beside({(1, 9): cmp_out, (2, 3): fox_sums}))
            pe.wait_ge(S("proj_done"), 1)
            pe.wait_ge(S("tabs"), 1)
            at_main.pe(pe)
            at_nsa.pe(pe)
            at_diff.pe(pe)
            lead = turning(pe, "o1", x_block, lambda g: pe.wait_ge(S("o1_ready"), 1 if g < 6 else 2),
                           when={4: 1, 5: 2, 6: 5, 7: 5})
            stage_matmuls(pe, "wout", actT, lead=lead)
            lead = turning(pe, "u2", lambda k, t: xn2[:, t, k * P:(k + 1) * P], quarter_ready("u2"))
            for i in range(3):
                st = ST[f"gu{i}"]

                def turn(p, j):
                    q = panel_no(st, p, j)
                    pe.wait_ge(acc_read, 2 + place(st, p, j).pn + 1)
                    for kk in range(2):
                        for t in range(T):
                            last = nc.tensor.transpose(ps[:, 4 + j, (kk * T + t) * P:(kk * T + t + 1) * P],
                                                       hid[:, j, t, kk * P:(kk + 1) * P], ident[:, :])
                    last.then_inc(S("hid_tr"), 1)
                stage_matmuls(pe, f"gu{i}", actT, hooks={11: turn}, one_acc=True, lead=lead if i == 0 else None)
                last_k = 2 * (2 * st.bodies - 1)
                stage_matmuls(pe, f"down{i}", hidT, lead={
                    0: lambda: pe.wait_ge(S("hid_taken"), 8 * i + 2 * st.bodies - 1),
                    8: lambda: turn(st.bodies - 1, 1),
                    last_k: lambda: pe.wait_ge(S("hid_taken"), 8 * i + 2 * st.bodies)})
            lead = turning(pe, "h0", x_block, quarter_ready("h0"))
            stage_matmuls(pe, "in0", actT, lead=lead)
            stage_matmuls(pe, "in0m", actT)
            pe.wait_ge(S("u0_done"), 1)

            def pool_means():
                pe.wait_ge(S("band"), 1)
                at_mem[0].wait(pe, "qkT", 2)
                for cb in range(12):
                    bank = cb // 2 % 2
                    if cb % 2 == 0 and cb >= 4:
                        pe.wait_ge(S("pooledT"), cb // 2 - 1)
                    for s in range(T):
                        last = nc.tensor.matmul(ps[:, bank, (cb % 2) * SEQ:(cb % 2 + 1) * SEQ],
                                                U[:, s, cb * P:(cb + 1) * P], band[:, cb // 3, s, :],
                                                start=(s == 0), stop=(s == 1))
                    if cb % 2:
                        last.then_inc(S("pool_ps"), 1)
            at_mem[0].pe(pe, beside_first=pool_means)
            pe.wait_ge(S("pooledT"), 6)
            pe.wait_ge(S("poolw_in"), 80)
            for grp in range(4):
                for t in range(T):
                    n = grp * T + t
                    if n >= 2:
                        pe.wait_ge(S("pool_mixed"), n - 1)
                    for kk in range(3):
                        last = nc.tensor.matmul(ps[:, 2 + n % 2, 0:384], pooledT[:, grp * 3 + kk, t * P:(t + 1) * P],
                                                poolw_s[:, grp, kk, :], start=(kk == 0), stop=(kk == 2))
                    last.then_inc(S("pool_out"), 1)
            mixed = lambda k, t: U[:, t, k * P:(k + 1) * P] if k < 12 else U[:, t, 2 * BR + (k - 12) * P:2 * BR + (k - 11) * P]
            lead = turning(pe, "m0", mixed, lambda g: pe.wait_ge(S("m0_ready"), min(-(-(g + 1) * 256 // 384), 4)))
            stage_matmuls(pe, "out0", actT, lead=lead)
            lead = turning(pe, "h1", x_block, quarter_ready("h1"))
            stage_matmuls(pe, "kv", actT, lead=lead)
            stage_matmuls(pe, "in1", actT)
            stage_matmuls(pe, "in1m", actT)
            pe.wait_ge(S("u1l_done"), 1)
            at_moba.pe(pe)
            at_mem[1].pe(pe)
            lead = turning(pe, "m1", mixed, lambda g: pe.wait_ge(S("m1_ready"), 1 if g < 6 else 2))
            stage_matmuls(pe, "out1", actT, lead=lead)

        @block.scalar
        def _(act):
            a = nc.scalar

            def stage_copy(name, dst, flag=None, width=None, lead=None, hooks={}, func=(ACT.Copy, ACT.Copy), defer=False):
                """High parts, and the finished panels copied out of PSUM."""
                st = ST[name]

                def take(p, j):
                    panel_done(act, st, p, j)
                    for t in range(T):
                        d = dst(p, j, t)
                        w = width[j] if width else NC
                        last = a.activation(d, ps[:, bank_of(st, j) + t, 0:w], func[j % 2])
                    last.then_inc(acc_read, 1)
                stage_split_hi(act, name, {6: take, **hooks}, width, lead)

                def take_last():
                    take(st.bodies - 1, len(st.panels) - 1)
                    if flag:
                        act.wait_ge(acc_read, 2 + st.end[2])
                        act.sem_inc(S(flag), 1)
                if defer:
                    return take_last
                take_last()

            act.sem_inc(acc_read, 2)
            act.wait_ge(S("cols_tr"), 1)
            a.activation(c_col[:, :], ps[:, 0, P:P + KD], ACT.Silu).then_inc(S("c_col"), 1)
            stage_copy("memkv", lambda p, j, t: memkv[:, ds(p, 1), t, j * NC:(j + 1) * NC].rearrange("p a n -> p (a n)"),
                       lead=split_plain_hi(act, "mem", actT))

            def normalise(tag, dst, mean=False):
                def quarter(q):
                    if q == 0:
                        act.wait_ge(S("rinv"), NORM[tag])
                    for t in range(T):
                        cs = slice(q * NC, (q + 1) * NC)
                        if mean:
                            last = a.activation(dst[:, t, cs], X[:, t, cs], ACT.Identity, bias=nmean[:, t:t + 1],
                                                scale=rinv_x[:, t:t + 1])
                        else:
                            last = a.activation(dst[:, t, cs], X[:, t, cs], ACT.Copy, scale=rinv_x[:, t:t + 1])
                    last.then_inc(S("xn"), 1)
                return quarter
            for q in range(4):
                normalise("n1", X)(q)
            take_win = stage_copy("win", lambda p, j, t: proj[:, t, ds(p * 4 * NC + j * NC, NC)],
                                  lead=split_mod_hi(act, "u1", actT), defer=True)

            def fox_exp():
                act.wait_ge(acc_read, 2 + ST["win"].end[2])
                act.wait_ge(S("fz"), 1)
                a.activation(fz[:, 2, :, :], fz[:, 1, :, :], ACT.Exp).then_inc(S("fe"), 1)
                act.wait_ge(S("lam_s"), 1)
                a.activation(lam[:, 2:4], lam[:, 0:2], ACT.Exp).then_inc(S("lam_e"), 1)

            def cmp_gelu():
                act.wait_ge(S("cmp_h_ps"), 1)
                for kv in range(2):
                    last = a.activation(cmp_h[:, kv, :, 0:N_CMP], o3(ps[0:HD, 7, 64 + kv * 32:64 + kv * 32 + 2 * N_CMP], 2),
                                        ACT.Gelu_apprx_tanh)
                last.then_inc(S("cmp_h"), 1)

            def nsa_gates():
                a.activation(gates[:, :, :, :].rearrange("p t h c -> p t (h c)"), proj[:, :, COL["gate"]:COL["gate"] + 24],
                             ACT.Sigmoid).then_inc(S("gates"), 1)
            stage_copy("win_end", lambda p, j, t: proj[:, t, (8 + j) * NC:(9 + j) * NC] if j < 3 else
                       proj[:, t, N_IN - LAST_W:N_IN], "proj_done", width=[NC, NC, NC, LAST_W],
                       lead={6: take_win, 13: fox_exp}, hooks=beside({(1, 4): cmp_gelu, (2, 8): nsa_gates}))
            at_main.act(act)
            at_nsa.act(act)

            def dilated_exp(i):
                if i == 1:
                    act.wait_ge(S("dd"), 1)
                    a.activation(dl[:, 2, :], dl[:, 1, :], ACT.Exp).then_inc(S("dexp"), 1)
            at_diff.act(act, dilated_exp)
            at_diff.wait(act, "pv", 4)
            stage_split_hi(act, "wout", lead=split_plain_hi(act, "o1", actT))
            for i in range(3):
                st = ST[f"gu{i}"]

                def gate_act(p, j):
                    panel_done(act, st, p, j)
                    for t in range(T):
                        last = a.activation(sil[:, j, t, :], ps[:, bank_of(st, j) + t, 0:256], ACT.Silu)
                    last.then_inc(S("sil"), 1)

                def hid_hi(p, j):
                    q = panel_no(st, p, j)
                    act.wait_ge(S("hid_tr"), 8 * i + q + 1)
                    a.activation(hidT[:, 0, ds(2 * q, 2), :], o3(ps[:, 4 + j, :], 2), ACT.Copy).then_inc(S("hid_hi"), 1)
                stage_split_hi(act, f"gu{i}", {6: gate_act, 15: hid_hi},
                               lead=split_mod_hi(act, "u2", actT, normalise("n2", xn2)) if i == 0 else None)
                stage_split_hi(act, f"down{i}", lead={4: lambda: gate_act(st.bodies - 1, 1),
                                                      10: lambda: hid_hi(st.bodies - 1, 1)})

            def u_dst(p, j, t):
                return U[:, t, ds(p * NC + j * BR, NC)]

            def um_dst(p, j, t):
                return U[:, t, 2 * BR + j * NC:2 * BR + (j + 1) * NC]
            gated = (ACT.Copy, ACT.Silu)

            def pooled_out():
                for n in range(6):
                    act.wait_ge(S("pool_ps"), n + 1)
                    a.activation(pooledT[:, 2 * n:2 * n + 2, :], o3(ps[:, n % 2, :], 2), ACT.Copy).then_inc(S("pooledT"), 1)
            take = stage_copy("in0", u_dst, lead=split_mod_hi(act, "h0", actT, normalise("n3", X)), func=gated, defer=True)
            stage_copy("in0m", um_dst, "u0_done", func=gated, lead={6: take})

            at_mem[0].act(act, beside_first=pooled_out)
            at_mem[0].wait(act, "pv", 2)
            stage_split_hi(act, "out0", lead=split_plain_hi(act, "m0", actT))
            take = stage_copy("kv", lambda p, j, t: KV[:, t, ds(p * 2 * NC + j * NC, NC)],
                              lead=split_mod_hi(act, "h1", actT, normalise("l0", X, mean=True)), defer=True)
            take = stage_copy("in1", u_dst, func=gated, lead={6: take}, defer=True)
            stage_copy("in1m", um_dst, "u1l_done", func=gated, lead={6: take})
            at_moba.act(act)
            at_mem[1].act(act)
            at_mem[1].wait(act, "pv", 2)
            stage_split_hi(act, "out1", lead=split_plain_hi(act, "m1", actT))

        @block.vector
        def _(dve):
            v = nc.vector
            cn = [0]

            def chain(ins):
                cn[0] += 1
                ins.then_inc(S("dve_chain"), 1)
                dve.wait_ge(S("dve_chain"), cn[0])

            def take_columns(first_bias, first_mod):
                def take(st):
                    def f(p, j):
                        pl = place(st, p, j)
                        q = ada_no(st, p, j)
                        dve.wait_ge(ada_summed, pl.an + 1)
                        v.tensor_tensor(modT[:, ds(first_mod + q * 4, 4)], ps[:, 6, 0:4],
                                        cols[:, ds(first_bias + q * 4, 4)], ALU.add).then_inc(ada_taken, 1)
                    return f
                return take

            def take_rows(st):
                def f(p, j):
                    pl = place(st, p, j)
                    q = ada_no(st, p, j)
                    dve.wait_ge(ada_summed, pl.an + 1)
                    dve.wait_ge(*((S("x_again"), 32) if st is ST["wout"] else (S("g2b_in"), 16)))
                    v.tensor_tensor(gb0[:, ds(q * NC, NC)], ps[:, 6, :], gb0[:, ds(q * NC, NC)],
                                    ALU.add).then_inc(ada_taken, 1)
                return f

            def moments(tag, eps, rms):
                if tag == "n1":
                    for t in range(T):
                        for i in range(4):
                            last = v.bn_stats(stats[:, t, i, :], X[:, t, i * 512:(i + 1) * 512])
                    chain(last)
                else:
                    dve.wait_ge(S("panel_stats"), 4 * (NORM[tag] - 1))
                for t in range(T):
                    last = v.bn_aggr(mv[:, t, :], stats[:, t, :, :].rearrange("p a b -> p (a b)"))
                chain(last)
                if rms:
                    chain(v.tensor_tensor(ms[:, :], mv[:, :, 0], mv[:, :, 0], ALU.mult))
                    chain(v.tensor_tensor(ms[:, :], ms[:, :], mv[:, :, 1], ALU.add))
                    v.tensor_scalar(ms[:, :], ms[:, :], eps, None, ALU.add).then_inc(S("ms"), 1)
                else:
                    v.tensor_scalar(ms[:, :], mv[:, :, 1], eps, None, ALU.add).then_inc(S("ms"), 1)

            def panel_stats(st, p, j, q):
                dve.wait_ge(acc_read, 2 + place(st, p, j).pn + 1)
                for t in range(T):
                    last = v.bn_stats(stats[:, t, ds(q, 1), :].rearrange("p a b -> p (a b)"), X[:, t, ds(q * NC, NC)])
                last.then_inc(S("panel_stats"), 1)

            def gains(half):
                m = modT[:, 32 * half + KD:32 * half + 2 * KD]
                chain(v.tensor_scalar(m, m, 1.0, None, ALU.add))
                chain(v.tensor_tensor(gain[:, half, :], m, cols[:, 96 + KD * half:96 + KD * (half + 1)], ALU.mult))

            dve.sem_inc(blocks_read, 2 * RING)
            dve.sem_inc(ada_taken, 1)
            dve.sem_inc(S("at_pT1"), 1)
            dve.wait_ge(S("cols_tr"), 1)
            dve.wait_ge(S("c_col"), 1)
            v.tensor_copy(cols2[:, :], ps[:, 0, P + KD:P + 4 * KD])
            v.tensor_copy(cols[:, :], ps[:, 0, 0:P]).then_inc(S("cols_done"), 1)
            dve.wait_ge(S("cols_done"), 1)
            stage_split_lo(dve, "memkv", take=take_columns(0, 0)(ST["memkv"]), lead=split_plain_lo(dve, "mem", actT))
            dve.wait_ge(S("x_in"), 16)
            moments("n1", RMS_EPS, True)
            stage_split_lo(dve, "ada1", take=take_columns(16, 16)(ST["ada1"]))
            dve.wait_ge(ada_taken, 1 + ST["ada1"].end[3])
            gains(0)

            def columns(of, first):
                return lambda k: of[:, first + k:first + k + 1]
            stage_split_lo(dve, "win", take=take_columns(48, 32)(ST["win"]),
                           lead=split_mod_lo(dve, "u1", actT, columns(gain[:, 0, :], 0), columns(modT, 0)))

            def far(kk, mask):
                dve.wait_ge(S("dist"), 1)
                di = dist[:, kk, :].bitcast(i32)
                chain(v.tensor_scalar(di, di, mask, None, ALU.bitwise_and))
                chain(v.tensor_scalar(dist[:, kk, :], di, 1.0, MASKED, ALU.min, ALU.mult))
                chain(v.tensor_tensor(dist[:, kk, :], dist[:, kk, :], dist[:, 0, :], ALU.add))

            def fox_start():
                dve.wait_ge(acc_read, 2 + ST["win"].end[2])
                dve.wait_ge(S("cmp_in"), 16 * 8)
                fb = fox_b[:, :].unsqueeze(1).broadcast_to([P, T, FOX])
                chain(v.tensor_tensor(fz[:, 0, :, :], proj[:, :, COL["fox_f"]:COL["fox_f"] + FOX], fb, ALU.add))
                chain(v.tensor_scalar(fz[:, 1, :, :], fz[:, 0, :, :], -1.0, None, ALU.mult))
                v.tensor_tensor(fz[:, 1, :, :], fz[:, 1, :, :], fz[:, 0, :, :], ALU.min).then_inc(S("fz"), 1)

            def lambda_dots():
                for i in range(2):
                    last = v.tensor_tensor_reduce(out=lamv[:, 2 * i, :], in0=lamv[:, 2 * i, :], in1=lamv[:, 2 * i + 1, :],
                                                  scale=1.0, scalar=0.0, op0=ALU.mult, op1=ALU.add,
                                                  accum_out=lam[:, i:i + 1])
                last.then_inc(S("lam_s"), 1)

            def flat(x):
                return x.rearrange("p t h -> p (t h)")
            e, tt, t2, acc = (fz[:, i, :, :] for i in (2, 3, 4, 5))

            def fox_ratio():
                dve.wait_ge(S("fe"), 1)
                chain(v.tensor_scalar(tt, e, 2.0, None, ALU.add))
                chain(v.reciprocal(tt, tt))
                chain(v.tensor_tensor(tt, tt, e, ALU.mult))
                chain(v.tensor_tensor(t2, tt, tt, ALU.mult))
                chain(v.tensor_scalar(acc, t2, 1.0 / 17.0, None, ALU.mult))

            def fox_terms(terms):
                for m in terms:
                    chain(v.scalar_tensor_tensor(flat(acc), flat(acc), 1.0 / m, flat(t2), ALU.add, ALU.mult))

            def fox_log():
                chain(v.scalar_tensor_tensor(flat(acc), flat(acc), 1.0, flat(tt), ALU.add, ALU.mult))
                chain(v.tensor_scalar(fz[:, 6, :, :], fz[:, 0, :, :], 0.0, None, ALU.min))
                v.scalar_tensor_tensor(flat(logf), flat(acc), -2.0, flat(fz[:, 6, :, :]),
                                       ALU.mult, ALU.add).then_inc(S("logf"), 1)

            def fox_take():
                dve.wait_ge(S("cum_ps"), 1)
                for h in range(FOX):
                    v.tensor_copy(cumk[:, h, :], ps[:, 4 + h // 2, (h % 2) * SEQ:(h % 2 + 1) * SEQ])
                v.tensor_scalar(flat(cumq), ps[:, 7, SEQ:SEQ + T * FOX], -1.0, None, ALU.mult).then_inc(S("tabs"), 1)

            def lambda_end():
                dve.wait_ge(S("lam_e"), 1)
                chain(v.tensor_tensor(lam[:, 4:5], lam[:, 3:4], lam[:, 2:3], ALU.subtract))
                chain(v.tensor_scalar(lam[:, 5:6], lam[:, 4:5], -LAM_INIT, None, ALU.add))
                chain(v.tensor_scalar(subg[:, :], subg[:, :], 1.0 - LAM_INIT, None, ALU.mult))

            def cmp_positions():
                dve.wait_ge(S("cmp_tr"), 1)
                chain(v.tensor_copy(posT[:, :, :].rearrange("p a j -> p (a j)"), ps[0:HD, 7, 0:2 * CMP_LEN]))
                for kv in range(2):
                    for r in range(2):
                        pv = posT[:, kv, r * 16:(r + 1) * 16].unsqueeze(1).broadcast_to([HD, 32, 16])
                        last = v.tensor_tensor(o3(cmp_in[:, kv, r, :], 32), o3(ps[0:HD, 4 + kv, :], 32),
                                               pv, ALU.add)
                last.then_inc(S("cmp_pos"), 1)

            def cmp_take():
                dve.wait_ge(S("cmp_ps"), 1)
                dve.wait_ge(S("cmp_zero"), 1)
                for kv in range(2):
                    last = v.tensor_copy(cmp_kv[0:N_CMP, kv, 0, :, :].rearrange("p g d -> p (g d)"),
                                         ps[0:N_CMP, 4, kv * 128:(kv + 1) * 128])
                last.then_inc(S("cmp_done"), 1)
            stage_split_lo(dve, "win_end", width=[NC, NC, NC, LAST_W], take=take_columns(72, 56)(ST["win_end"]),
                           lead={8: fox_start, 9: lambda_dots, 10: cmp_positions, 15: fox_ratio},
                           hooks=beside({(1, 1): lambda: fox_terms((15, 13, 11, 9)), (1, 3): lambda: fox_terms((7, 5, 3)),
                                         (1, 5): fox_log, (1, 8): lambda: far(2, 3), (1, 14): cmp_take,
                                         (1, 11): lambda: far(3, 15), (2, 8): fox_take, (2, 15): lambda_end}))
            at_main.dve(dve)
            at_nsa.dve(dve)

            nm = [dnm[:, 0, :, 15 + 3 * g:18 + 3 * g] for g in range(3)]

            def d9(i):
                return dl[:, i, :].rearrange("p (t g h) -> p t g h", t=T, g=3)

            def dilated_lse():
                for i in range(2):
                    last = v.tensor_copy(dnm[:, i, :, :].rearrange("p t (j h) -> p t j h", h=2),
                                         stat[:, :, 4 * i:4 * i + 4].rearrange("p j (t h) -> p t j h", t=T))
                chain(last)
                chain(v.tensor_tensor(d9(0)[:, :, 0, :], nm[0], nm[1], ALU.min))
                chain(v.tensor_tensor(d9(0)[:, :, 0, :], d9(0)[:, :, 0, :], nm[2], ALU.min))
                for g in range(3):
                    last = v.tensor_tensor(d9(1)[:, :, g, :], d9(0)[:, :, 0, :], nm[g], ALU.subtract)
                last.then_inc(S("dd"), 1)

            def dilated_weights():
                dve.wait_ge(S("dexp"), 1)
                ll = dnm[:, 1, :, 15:24]
                chain(v.tensor_tensor(dl[:, 3, :].rearrange("p (t h) -> p t h", t=T), dl[:, 2, :].rearrange(
                    "p (t h) -> p t h", t=T), ll, ALU.mult))
                chain(v.tensor_tensor(d9(4)[:, :, 0, :], d9(3)[:, :, 0, :], d9(3)[:, :, 1, :], ALU.add))
                chain(v.tensor_tensor(d9(4)[:, :, 0, :], d9(4)[:, :, 0, :], d9(3)[:, :, 2, :], ALU.add))
                chain(v.reciprocal(d9(4)[:, :, 1, :], d9(4)[:, :, 0, :]))
                for g in range(3):
                    last = v.tensor_tensor(d9(5)[:, :, g, :], d9(3)[:, :, g, :], d9(4)[:, :, 1, :], ALU.mult)
                chain(last)
                od = X[:, :, 960:1536].rearrange("p t (h d) -> p t h d", h=9)
                v.tensor_tensor(od, od, dl[:, 5, :].rearrange("p (t h) -> p t h", t=T).unsqueeze(3).broadcast_to(
                    [P, T, 9, HD]), ALU.mult)

            def gate_of(i):
                return gates[:, :, :, i].unsqueeze(3).broadcast_to([P, T, NSA, HD])
            on = X[:, :, 448:960].rearrange("p t (h d) -> p t h d", h=8)

            def nsa_gated():
                dve.wait_ge(S("gates"), 1)
                dve.wait_ge(S("valid"), 1)
                chain(v.tensor_tensor(gates[:, 0, :, 0], gates[:, 0, :, 0], valid[:, :].broadcast_to([P, NSA]), ALU.mult))
                v.tensor_tensor(on, on, gate_of(1), ALU.mult)
                chain(v.tensor_tensor(res_nsa[:, :, 0:8, :], res_nsa[:, :, 0:8, :], gate_of(2), ALU.mult))

            def nsa_sum():
                v.tensor_tensor(res_nsa[:, :, 8:16, :], res_nsa[:, :, 8:16, :], gate_of(0), ALU.mult)
                chain(v.tensor_tensor(on, on, res_nsa[:, :, 0:8, :], ALU.add))
                chain(v.tensor_tensor(on, on, res_nsa[:, :, 8:16, :], ALU.add))

            def merge(i):
                if i == 0:
                    at_nsa.wait(dve, "normed", 8)
                    dilated_lse()
                    nsa_gated()
                elif i == 1:
                    dilated_weights()
                elif i == 2:
                    nsa_sum()
            at_diff.dve(dve, merge)
            at_diff.wait(dve, "normed", 4)
            for t in range(T):
                last = v.scalar_tensor_tensor(o3(X[:, t, 1536:2048], 4), res_diff[:, t, :, 1, :], lam[:, 5:6],
                                              res_diff[:, t, :, 0, :], ALU.mult, ALU.add)
            chain(last)
            dve.sem_inc(S("o1_ready"), 1)
            xd = X[:, :, 1536:2048]

            def subnorm_squares():
                chain(v.tensor_tensor(diff_tmp[:, :, :], xd, xd, ALU.mult))
                chain(v.tensor_reduce(o3(dss[:, 0, :], 2), diff_tmp[:, :, :].rearrange("p t (h d) -> p t h d", h=4),
                                      AX.X, ALU.add))
                v.tensor_scalar(dss[:, 1, :], dss[:, 0, :], 1.0 / 128, RMS_EPS, ALU.mult, ALU.add
                                ).then_inc(S("dif_ms"), 1)

            def subnorm_scale():
                dve.wait_ge(S("dif_rinv"), 1)
                xd4 = xd.rearrange("p t (h d) -> p t h d", h=4)
                chain(v.tensor_tensor(xd4, xd4, o3(dss[:, 2, :], 2).unsqueeze(3).broadcast_to([P, T, 4, 128]), ALU.mult))
                for t in range(T):
                    last = v.tensor_tensor(o3(X[:, t, 1536:2048], 4), o3(X[:, t, 1536:2048], 4),
                                           subg[:, :].unsqueeze(1).broadcast_to([P, 4, 128]), ALU.mult)
                last.then_inc(S("o1_ready"), 1)

            def gated_add(name, at_k=12, take=None, lead=None, defer=False):
                st = ST[name]

                def f(p, j):
                    dve.wait_ge(ada_taken, 1 + (place(st, p, j).an + 1 if take else ST["gu0"].end[3]))
                    panel_done(dve, st, p, j)
                    q = p * 2 + j if len(st.panels) == 2 else j
                    for t in range(T):
                        last = v.tensor_tensor(gy[:, t, :], ps[:, bank_of(st, j) + t, :], gb0[:, ds(q * NC, NC)], ALU.mult)
                    last.then_inc(S("gy"), 1)
                    if name == "wout":
                        dve.wait_ge(S("x_again"), 32)
                    dve.wait_ge(S("gy"), 4 * ("wout", "down0", "down1", "down2").index(name) + panel_no(st, p, j) + 1)
                    for t in range(T):
                        xs = X[:, t, ds(q * NC, NC)]
                        last = v.tensor_tensor(xs, xs, gy[:, t, :], ALU.add)
                    last.then_inc(acc_read, 1)
                    if name in ("wout", "down2"):
                        panel_stats(st, p, j, q)
                stage_split_lo(dve, name, {at_k: f}, take=take, lead=lead)
                if defer:
                    return lambda: f(st.bodies - 1, len(st.panels) - 1)
                f(st.bodies - 1, len(st.panels) - 1)

            o1_lead = {5: subnorm_squares, 9: subnorm_scale, **split_plain_lo(dve, "o1", actT)}
            gated_add("wout", take=take_rows(ST["wout"]), lead=o1_lead)
            moments("n2", RMS_EPS, True)
            gains(1)
            u2_lead = split_mod_lo(dve, "u2", actT, columns(gain[:, 1, :], 0), columns(modT, 32))
            for i in range(3):
                st = ST[f"gu{i}"]

                def up_mul(p, j):
                    dve.wait_ge(S("sil"), 8 * i + panel_no(st, p, j) + 1)
                    for t in range(T):
                        last = v.tensor_tensor(hid[:, j, t, :], sil[:, j, t, :], ps[:, bank_of(st, j) + t, 256:512], ALU.mult)
                    last.then_inc(acc_read, 1)

                def hid_lo(p, j):
                    q = panel_no(st, p, j)
                    dve.wait_ge(S("hid_hi"), 8 * i + q + 1)
                    v.tensor_tensor(hidT[:, 1, ds(2 * q, 2), :], o3(ps[:, 4 + j, :], 2),
                                    hidT[:, 0, ds(2 * q, 2), :].bitcast(f32), ALU.subtract).then_inc(S("hid_taken"), 1)
                stage_split_lo(dve, f"gu{i}", {8: up_mul, 15: hid_lo},
                               take=take_rows(ST["gu0"]) if i == 0 else None, one_acc=True,
                               lead=u2_lead if i == 0 else {12: add_last})
                add_last = gated_add(f"down{i}", 12 if i < 2 else 8,
                                     lead={6: lambda: up_mul(st.bodies - 1, 1),
                                           11: lambda: hid_lo(st.bodies - 1, 1)}, defer=i < 2)
            moments("n3", RMS_EPS, True)
            stage_split_lo(dve, "in0", lead=split_mod_lo(dve, "h0", actT, columns(cols2, 0), None))
            stage_split_lo(dve, "in0m")

            def layer_out(name, tag, lead):
                st = ST[name]

                def f(p, j):
                    dve.wait_ge(S("natural"), T * (1 if tag == "l0" else 2))
                    panel_done(dve, st, p, j)
                    for t in range(T):
                        xs = X[:, t, ds((p * 2 + j) * NC, NC)]
                        last = v.scalar_tensor_tensor(xs, xs, ALPHA, ps[:, bank_of(st, j) + t, :], ALU.mult, ALU.add)
                    last.then_inc(acc_read, 1)
                    panel_stats(st, p, j, p * 2 + j)
                stage_split_lo(dve, name, {12: f}, lead=lead)
                f(st.bodies - 1, 1)
                moments(tag, LN_EPS, False)

            at_mem[0].dve(dve)
            at_mem[0].finished(dve)
            dve.wait_ge(S("u0_done"), 1)
            um = U[:, :, 2 * BR:2 * BR + MEMW]
            v.tensor_tensor(um, um, U[:, :, 2 * BR + MEMW:], ALU.mult)
            dve.wait_ge(S("poolw_in"), 80)
            for grp in range(4):
                cs = slice(grp * 384, (grp + 1) * 384)
                for t in range(T):
                    n = grp * T + t
                    dve.wait_ge(S("pool_out"), n + 1)
                    v.tensor_tensor(U[:, t, cs], ps[:, 2 + n % 2, 0:384], pscale[:, cs], ALU.mult
                                    ).then_inc(S("pool_mixed"), 1)
                dve.wait_ge(S("pool_mixed"), 2 * grp + 2)
                v.tensor_tensor(U[:, :, cs], U[:, :, cs], U[:, :, BR + grp * 384:BR + (grp + 1) * 384], ALU.mult
                                ).then_inc(S("m0_ready"), 1)
            layer_out("out0", "l0", split_plain_lo(dve, "m0", actT))
            stage_split_lo(dve, "kv", lead=split_mod_lo(dve, "h1", actT, columns(cols2, 16), columns(cols2, 32)))
            stage_split_lo(dve, "in1")
            stage_split_lo(dve, "in1m")

            def gate_moba(i):
                if i == 0:
                    dve.wait_ge(S("u1l_done"), 1)
                    at_moba.finished(dve)
                ins = v.tensor_tensor(U[:, i, 0:BR], U[:, i, 0:BR], U[:, i, BR:2 * BR], ALU.mult)
                if i:
                    ins.then_inc(S("m1_ready"), 1)
            at_moba.dve(dve)
            at_mem[1].dve(dve, gate_moba)
            at_mem[1].finished(dve)
            v.tensor_tensor(um, um, U[:, :, 2 * BR + MEMW:], ALU.mult).then_inc(S("m1_ready"), 1)
            layer_out("out1", "l1", split_plain_lo(dve, "m1", actT))
            dve.wait_ge(S("ln1_in"), 32)
            dve.wait_ge(S("rinv"), NORM["l1"])
            for half in range(2):
                cs = slice(half * D // 2, (half + 1) * D // 2)
                for t in range(T):
                    last = v.scalar_tensor_tensor(X[:, t, cs], X[:, t, cs], mv[:, t, 0:1], gb0[:, cs],
                                                  ALU.subtract, ALU.mult)
                chain(last)
                for t in range(T):
                    v.scalar_tensor_tensor(X[:, t, cs], X[:, t, cs], rinv_x[:, t:t + 1], gb1[:, cs],
                                           ALU.mult, ALU.add).then_inc(S("y_done"), 1)


_INS = ['x', 'c', 'ada_w', 'ada_b', 'norm_mix_g', 'norm_ffn_g', 'w_in', 'fox_f_bias', 'nsa_cmp_w1', 'nsa_cmp_w2',
        'nsa_cmp_pos', 'diff_lambda', 'diff_subln_g', 'w_out', 'ffn_w_gate', 'ffn_w_up', 'ffn_w_down',
        'final_norm_g', 'mem_2', 'w_in_2', 'w_out_2', 'w_mem_kv_2', 'ln_g_2', 'ln_b_2', 'pool_w_2', 'pool_scale_2',
        'w_kv_shared_2']


def kernel(**inputs):
    import numpy as _np
    import concourse.bacc as _bacc
    from concourse import mybir as _mybir
    from concourse.bass_utils import run_bass_kernel_spmd as _run

    nc = _bacc.Bacc("TRN2", target_bir_lowering=False, num_devices=1)
    arrays, args = {}, []
    for name in _INS:
        a = _np.ascontiguousarray(inputs[name])
        arrays[f"in_{name}"] = a
        args.append(nc.dram_tensor(f"in_{name}", a.shape, _mybir.dt.from_np(a.dtype), kind="ExternalInput").ap())
    y = nc.dram_tensor("out_0", (1, SEQ, D), _mybir.dt.float32, kind="ExternalOutput").ap()
    program(nc, *args, y)
    r = _run(nc, [arrays], core_ids=[0])
    return r.results[0]["out_0"]
```
